# Optimizing a Trainium2 kernel written in Bass

```python
import math
import jax, jax.numpy as jnp
from jax import lax
import numpy as np

D_MODEL = 1024
BATCH = 1
SEQ = 1024
DEPTH = 1

GRID_W = 64
NORM_EPS = 1e-6
NEG_INF = -1e30

HY_D = D_MODEL // 4
HY_EMB = 33
HY_BANDS = (HY_EMB - 1) // 2
HY_FFN = 64
HY_MIN_DECAY = math.log(1e-2) / 1.5
HY_MAX_DECAY = math.log(1e-2) / 0.3

RW_N = 64
RW_D = D_MODEL // 2
RW_H = RW_D // RW_N
RW_W_LORA = 64
RW_A_LORA = 64
RW_G_LORA = 128
RW_GN_EPS = 64e-5

NA_HD = 64
NA_D = D_MODEL // 4
NA_H = NA_D // NA_HD
NA_KR = 8
NA_KC = 16

MIX_D = HY_D + RW_D + NA_D
IN_SIZES = (3 * HY_D, 3 * RW_D, RW_G_LORA, 2 * RW_W_LORA, 2 * RW_A_LORA, 3 * NA_D)
IN_D = sum(IN_SIZES)

MOE_GROUPS = 4
MOE_PER_GROUP = 8
MOE_EXPERTS = MOE_GROUPS * MOE_PER_GROUP
MOE_TOPK = 2
MOE_FF = 512
MOE_BLOCK = 256

kernel_name = 'hybrid_hyena_rwkv7_natten_hmoe_encoder'

def rmsnorm(x, g):
    x32 = x.astype(jnp.float32)
    y = x32 * lax.rsqrt(jnp.mean(x32 * x32, axis=-1, keepdims=True) + NORM_EPS)
    return y.astype(x.dtype) * g

def shift_prev(u):
    return jnp.pad(u, ((0, 0), (1, 0), (0, 0)))[:, :-1]

def shift_next(u):
    return jnp.pad(u, ((0, 0), (0, 1), (0, 0)))[:, 1:]

def hyena_positional_features(L):
    t = jnp.linspace(0.0, 1.0, L, dtype=jnp.float32)[:, None]
    w = (2.0 * math.pi / L) * jnp.arange(L, dtype=jnp.float32)[:, None]
    f = jnp.linspace(1e-4, HY_BANDS - 1, HY_BANDS, dtype=jnp.float32)[None, :]
    z = jnp.concatenate([t, jnp.cos(f * w), -jnp.sin(f * w)], axis=-1)
    return z, t

def hyena_filters(z, t, w1, b1, w2, b2, w3, b3, wout, freq):
    f32 = jnp.float32
    fr = freq.astype(f32)
    act = lambda u: jnp.sin(fr * u)
    h = act(z @ w1.astype(f32) + b1.astype(f32))
    h = act(h @ w2.astype(f32) + b2.astype(f32))
    h = act(h @ w3.astype(f32) + b3.astype(f32))
    h = (h @ wout.astype(f32)).reshape(-1, 2, HY_D)
    deltas = jnp.abs(jnp.linspace(HY_MIN_DECAY, HY_MAX_DECAY, HY_D, dtype=f32))
    h = h * jnp.exp(-t[:, :, None] * deltas)
    return h * lax.rsqrt(jnp.sum(h * h, axis=(0, 1), keepdims=True) + 1e-6)

def hyena_mixer(u, conv_w, conv_b, filt, skip):
    up = jnp.pad(u, ((0, 0), (1, 1), (0, 0)))
    uc = up[:, :-2] * conv_w[0] + up[:, 1:-1] * conv_w[1] + up[:, 2:] * conv_w[2] + conv_b
    x0, x1, v = jnp.split(uc, 3, axis=-1)
    z = (v * x1).astype(jnp.float32)
    L = z.shape[1]
    k2 = jnp.concatenate([filt[:1, 0] + filt[:1, 1], filt[1:, 0],
                          jnp.zeros((1, HY_D), jnp.float32), filt[1:, 1][::-1]], axis=0)
    y = jnp.fft.irfft(jnp.fft.rfft(z, n=2 * L, axis=1) * jnp.fft.rfft(k2, axis=0)[None],
                      n=2 * L, axis=1)[:, :L]
    y = y + z * skip.astype(jnp.float32)
    return (x0.astype(jnp.float32) * y).astype(u.dtype)

def wkv7_scan(r, w, k, v, a, b, reverse):
    Bn, L, H, N = r.shape
    xs = tuple(jnp.moveaxis(u, 1, 0) for u in (r, w, k, v, a, b))

    def step(S, inp):
        rt, wt, kt, vt, at, bt = inp
        sa = jnp.einsum('bhvk,bhk->bhv', S, at)
        S = S * wt[:, :, None, :] + sa[..., None] * bt[:, :, None, :] + vt[..., None] * kt[:, :, None, :]
        return S, jnp.einsum('bhvk,bhk->bhv', S, rt)

    _, y = lax.scan(step, jnp.zeros((Bn, H, N, N), jnp.float32), xs, reverse=reverse)
    return jnp.moveaxis(y, 0, 1)

def rwkv7_mixer(r, k, v, g_lo, w_lo, a_lo, mu, w0, w2, a0, a2, k_k, k_a, r_k, g2, ln_w, ln_b):
    f32 = jnp.float32
    Bn, L, C = r.shape

    def tshift(u, m):
        return u + m[0] * (shift_prev(u) - u) + m[1] * (shift_next(u) - u)

    r, k, v = (tshift(u, m).astype(f32) for u, m in zip((r, k, v), mu))
    w_lo = w_lo.astype(f32).reshape(Bn, L, 2, RW_W_LORA)
    a_lo = a_lo.astype(f32).reshape(Bn, L, 2, RW_A_LORA)
    w_log = -jax.nn.softplus(-(w0.astype(f32) + jnp.einsum('bldr,drc->bldc', jnp.tanh(w_lo), w2.astype(f32)))) - 0.5
    decay = jnp.exp(-jnp.exp(w_log))
    a = jax.nn.sigmoid(a0.astype(f32) + jnp.einsum('bldr,drc->bldc', a_lo, a2.astype(f32)))
    heads = lambda u: u.reshape(u.shape[:-1] + (RW_H, RW_N))
    kk = heads(k * k_k.astype(f32))
    kk = (kk * lax.rsqrt(jnp.maximum(jnp.sum(kk * kk, axis=-1, keepdims=True), 1e-24))).reshape(Bn, L, C)
    k_dir = k[:, :, None] * (1.0 + (a - 1.0) * k_a.astype(f32))
    rh, vh = heads(r), heads(v)
    y_f = wkv7_scan(rh, heads(decay[:, :, 0]), heads(k_dir[:, :, 0]), vh, heads(-kk), heads(kk * a[:, :, 0]), False)
    y_b = wkv7_scan(rh, heads(decay[:, :, 1]), heads(k_dir[:, :, 1]), vh, heads(-kk), heads(kk * a[:, :, 1]), True)
    y = y_f + y_b
    mean = jnp.mean(y, axis=-1, keepdims=True)
    var = jnp.mean(jnp.square(y - mean), axis=-1, keepdims=True)
    y = ((y - mean) * lax.rsqrt(var + RW_GN_EPS)).reshape(Bn, L, C) * ln_w.astype(f32) + ln_b.astype(f32)
    bonus = jnp.sum(rh * heads(k_dir[:, :, 0] + k_dir[:, :, 1]) * r_k.astype(f32), axis=-1, keepdims=True) * vh
    gate = jax.nn.sigmoid(g_lo.astype(f32)) @ g2.astype(f32)
    return ((y + bonus.reshape(Bn, L, C)) * gate).astype(g_lo.dtype)

def neighborhood_attention(q, k, v, rpb):
    Bn, L, H, Dh = q.shape
    R = L // GRID_W
    KR = min(NA_KR, R)
    f32 = jnp.float32
    grid = lambda u: u.reshape(Bn, R, GRID_W, H, Dh)
    rows = jnp.arange(R)
    row_idx = jnp.clip(rows - KR // 2, 0, R - KR)[:, None] + jnp.arange(KR)[None, :]
    k_rows = grid(k)[:, row_idx]
    v_rows = grid(v)[:, row_idx]
    cols = jnp.arange(GRID_W)
    col_start = jnp.clip(cols - NA_KC // 2, 0, GRID_W - NA_KC)
    in_band = (cols[None, :] >= col_start[:, None]) & (cols[None, :] < col_start[:, None] + NA_KC)
    dr = row_idx - rows[:, None] + (NA_KR - 1)
    dc = jnp.clip(cols[None, :] - cols[:, None], -(NA_KC - 1), NA_KC - 1) + (NA_KC - 1)
    bias = rpb.astype(f32)[:, dr[:, None, :, None], dc[None, :, None, :]]
    bias = jnp.where(in_band[None, None, :, None, :], bias, NEG_INF)
    s = jnp.einsum('brqhd,brikhd->bhrqik', grid(q).astype(f32), k_rows.astype(f32)) * (Dh ** -0.5)
    p = jax.nn.softmax(s + bias[None], axis=(-2, -1))
    o = jnp.einsum('bhrqik,brikhd->brqhd', p, v_rows.astype(f32))
    return o.reshape(Bn, L, H * Dh).astype(q.dtype)

def hier_moe(h, wg, bg, we, be, w1, w3, w2):
    N, Dm = h.shape
    f32 = jnp.float32
    h32 = h.astype(f32)
    g_logits = h32 @ wg.astype(f32) + bg.astype(f32)
    g_sel = jnp.argmax(g_logits, axis=-1)
    g_prob = jnp.take_along_axis(jax.nn.softmax(g_logits, axis=-1), g_sel[:, None], axis=-1)
    e_logits = (h32 @ we.astype(f32) + be.astype(f32)).reshape(N, MOE_GROUPS, MOE_PER_GROUP)
    e_logits = jnp.take_along_axis(e_logits, g_sel[:, None, None], axis=1)[:, 0]
    top_val, top_idx = lax.top_k(e_logits, MOE_TOPK)
    gate = g_prob * jax.nn.softmax(top_val, axis=-1)
    expert = g_sel[:, None] * MOE_PER_GROUP + top_idx
    M = N * MOE_TOPK
    flat_e = expert.reshape(M)
    order = jnp.argsort(flat_e)
    e_sorted = flat_e[order]
    counts = jnp.bincount(flat_e, length=MOE_EXPERTS)
    padded = (counts + MOE_BLOCK - 1) // MOE_BLOCK * MOE_BLOCK
    pad_end = jnp.cumsum(padded)
    first = (jnp.cumsum(counts) - counts)[e_sorted]
    slot = (pad_end - padded)[e_sorted] + jnp.arange(M) - first
    n_blocks = -(-M // MOE_BLOCK) + MOE_EXPERTS
    slot_src = jnp.full((n_blocks * MOE_BLOCK,), M, jnp.int32).at[slot].set(order.astype(jnp.int32))
    tok_src = jnp.append(jnp.arange(M, dtype=jnp.int32) // MOE_TOPK, N)[slot_src].reshape(n_blocks, MOE_BLOCK)
    w_src = jnp.append(gate.reshape(M), 0.0)[slot_src].reshape(n_blocks, MOE_BLOCK)
    block_e = jnp.minimum(jnp.searchsorted(pad_end, jnp.arange(n_blocks) * MOE_BLOCK, side='right'),
                          MOE_EXPERTS - 1)
    h_pad = jnp.concatenate([h, jnp.zeros((1, Dm), h.dtype)], axis=0)

    def expert_block(args):
        tok, wt, e = args
        xb = h_pad[tok]
        yb = (jax.nn.silu(xb @ w1[e]) * (xb @ w3[e])) @ w2[e]
        return yb * wt[:, None].astype(yb.dtype)

    y = lax.map(expert_block, (tok_src, w_src, block_e))
    return jnp.zeros((N + 1, Dm), h.dtype).at[tok_src.reshape(-1)].add(y.reshape(-1, Dm))[:N]

def setup_inputs(seed: int = 0) -> dict:
    key = jax.random.key(seed)
    ks = iter(jax.random.split(key, 48))

    def nrm(shape, scale):
        return scale * jax.random.normal(next(ks), shape, jnp.float32)

    Ld = DEPTH
    w0_ramp = jnp.linspace(-6.0, -1.0, RW_D, dtype=jnp.float32)
    return {
        'x': nrm((BATCH, SEQ, D_MODEL), 1.0),
        'norm1_g': 1.0 + nrm((Ld, D_MODEL), 0.05),
        'w_in': nrm((Ld, D_MODEL, IN_D), D_MODEL ** -0.5),
        'hy_conv_w': nrm((Ld, 3, 3 * HY_D), 3 ** -0.5),
        'hy_conv_b': nrm((Ld, 3 * HY_D), 0.1),
        'hy_w1': nrm((Ld, HY_EMB, HY_FFN), HY_EMB ** -0.5),
        'hy_b1': nrm((Ld, HY_FFN), 0.1),
        'hy_w2': nrm((Ld, HY_FFN, HY_FFN), HY_FFN ** -0.5),
        'hy_b2': nrm((Ld, HY_FFN), 0.1),
        'hy_w3': nrm((Ld, HY_FFN, HY_FFN), HY_FFN ** -0.5),
        'hy_b3': nrm((Ld, HY_FFN), 0.1),
        'hy_wout': nrm((Ld, HY_FFN, 2 * HY_D), HY_FFN ** -0.5),
        'hy_freq': 1.0 + nrm((Ld, HY_FFN), 0.1),
        'hy_skip': nrm((Ld, HY_D), 0.5),
        'rw_mu': jax.random.uniform(next(ks), (Ld, 3, 2, RW_D), jnp.float32, 0.0, 0.5),
        'rw_w0': w0_ramp + nrm((Ld, 2, RW_D), 0.1),
        'rw_w2': nrm((Ld, 2, RW_W_LORA, RW_D), 0.1 * RW_W_LORA ** -0.5),
        'rw_a0': nrm((Ld, 2, RW_D), 0.1),
        'rw_a2': nrm((Ld, 2, RW_A_LORA, RW_D), 0.1 * RW_A_LORA ** -0.5),
        'rw_kk': 0.85 + nrm((Ld, RW_D), 0.05),
        'rw_ka': 1.0 + nrm((Ld, RW_D), 0.05),
        'rw_rk': nrm((Ld, RW_H, RW_N), 0.1),
        'rw_g2': nrm((Ld, RW_G_LORA, RW_D), RW_G_LORA ** -0.5),
        'rw_ln_w': 1.0 + nrm((Ld, RW_D), 0.05),
        'rw_ln_b': nrm((Ld, RW_D), 0.01),
        'na_rpb': nrm((Ld, NA_H, 2 * NA_KR - 1, 2 * NA_KC - 1), 0.02),
        'w_out': nrm((Ld, MIX_D, D_MODEL), MIX_D ** -0.5),
        'norm2_g': 1.0 + nrm((Ld, D_MODEL), 0.05),
        'moe_wg': nrm((Ld, D_MODEL, MOE_GROUPS), D_MODEL ** -0.5),
        'moe_bg': nrm((Ld, MOE_GROUPS), 0.01),
        'moe_we': nrm((Ld, D_MODEL, MOE_EXPERTS), D_MODEL ** -0.5),
        'moe_be': nrm((Ld, MOE_EXPERTS), 0.01),
        'moe_w1': nrm((Ld, MOE_EXPERTS, D_MODEL, MOE_FF), D_MODEL ** -0.5),
        'moe_w3': nrm((Ld, MOE_EXPERTS, D_MODEL, MOE_FF), D_MODEL ** -0.5),
        'moe_w2': nrm((Ld, MOE_EXPERTS, MOE_FF, D_MODEL), MOE_FF ** -0.5),
        'norm_f_g': 1.0 + nrm((D_MODEL,), 0.05),
    }

def reference(x, norm1_g, w_in, hy_conv_w, hy_conv_b, hy_w1, hy_b1, hy_w2, hy_b2, hy_w3, hy_b3,
              hy_wout, hy_freq, hy_skip, rw_mu, rw_w0, rw_w2, rw_a0, rw_a2, rw_kk, rw_ka, rw_rk,
              rw_g2, rw_ln_w, rw_ln_b, na_rpb, w_out, norm2_g, moe_wg, moe_bg, moe_we, moe_be,
              moe_w1, moe_w3, moe_w2, norm_f_g):
    Bn, L, _ = x.shape
    z_pos, t_pos = hyena_positional_features(L)
    splits = np.cumsum(IN_SIZES)[:-1].tolist()
    for l in range(DEPTH):
        h = rmsnorm(x, norm1_g[l])
        proj = h @ w_in[l]
        hy_u, rw_rkv, rw_g, rw_w, rw_a, na_qkv = jnp.split(proj, splits, axis=-1)
        filt = hyena_filters(z_pos, t_pos, hy_w1[l], hy_b1[l], hy_w2[l], hy_b2[l],
                             hy_w3[l], hy_b3[l], hy_wout[l], hy_freq[l])
        y_hy = hyena_mixer(hy_u, hy_conv_w[l], hy_conv_b[l], filt, hy_skip[l])
        r, k, v = jnp.split(rw_rkv, 3, axis=-1)
        y_rw = rwkv7_mixer(r, k, v, rw_g, rw_w, rw_a, rw_mu[l], rw_w0[l], rw_w2[l], rw_a0[l],
                           rw_a2[l], rw_kk[l], rw_ka[l], rw_rk[l], rw_g2[l], rw_ln_w[l], rw_ln_b[l])
        q, kn, vn = (u.reshape(Bn, L, NA_H, NA_HD) for u in jnp.split(na_qkv, 3, axis=-1))
        y_na = neighborhood_attention(q, kn, vn, na_rpb[l])
        x = x + jnp.concatenate([y_hy, y_rw, y_na], axis=-1) @ w_out[l]
        h = rmsnorm(x, norm2_g[l]).reshape(Bn * L, D_MODEL)
        x = x + hier_moe(h, moe_wg[l], moe_bg[l], moe_we[l], moe_be[l],
                         moe_w1[l], moe_w3[l], moe_w2[l]).reshape(Bn, L, D_MODEL)
    return rmsnorm(x, norm_f_g)


_drawn_inputs = setup_inputs


def setup_inputs(seed=0):
    import zlib

    import numpy as np

    out = dict(_drawn_inputs(seed))
    spreads = {}
    factors = {'rw_w2': 7.403, 'rw_ln_b': 5.824, 'na_rpb': 22.305, 'moe_bg': 4.895, 'moe_be': 4.401}
    for name, (base, spread) in spreads.items():
        noise = np.random.default_rng([zlib.crc32(name.encode()), seed]).standard_normal(out[name].shape)
        drawn = base * np.exp(spread * noise) if base else spread * noise
        out[name] = __import__('jax').numpy.asarray(drawn.astype(out[name].dtype))
    for name, factor in factors.items():
        out[name] = (out[name] * factor).astype(out[name].dtype)
    return out
```

```python
import math

import numpy as np
import concourse.bass as bass
from concourse import mybir
from contextlib import ExitStack, contextmanager


class Memory:
    pass


F32 = mybir.dt.float32
I32 = mybir.dt.int32
U32 = mybir.dt.uint32
ALU = mybir.AluOpType
ACT = mybir.ActivationFunctionType
AX = mybir.AxisListType
ds = bass.ds

P = 128
D = 1024
L = 1024
KD = D // P
NT = L // P
HALF = 512
HY_D, RW_D, NA_D = D // 4, D // 2, D // 4
IN_D = 3 * HY_D + 3 * RW_D + 128 + 128 + 128 + 3 * NA_D
CT = IN_D // P
T_HY, T_R, T_K, T_V = 0, 6, 10, 14
T_G, T_W, T_A, T_Q, T_NK, T_NV = 18, 19, 20, 21, 23, 25
EPS = 1e-6
TWO_PI = 2.0 * np.pi
ROUND = float(1.5 * 2 ** 23)
PI2_HI = 6.28125
PI2_LO = float(TWO_PI - 6.28125)


def bcast(ap, n, at=1):
    shape = list(ap.shape)
    shape.insert(at, n)
    return ap.unsqueeze(at).to_broadcast(shape)


def project(nc, A, S, sem):
    ctx = ExitStack()
    with ctx:
        sb = lambda n, s, t=F32: ctx.enter_context(nc.sbuf_tensor(n, s, t))
        ps = lambda n, s: ctx.enter_context(nc.psum_tensor(n, s, F32))
        xt = [sb(f"a_x{j}", [P, D]) for j in range(2)]
        junk = sb("a_junk", [P, D])
        gb = sb("a_g", [P, D])
        ss = sb("a_ss", [P, 2])
        rs = sb("a_rs", [P, 2])
        w = [sb(f"a_w{j}", [P, KD, P]) for j in range(3)]
        hT = S.mix
        tp = [ps(f"a_tp{j}", [P, 4, P]) for j in range(2)]
        pp = [ps(f"a_pp{j}", [P, HALF]) for j in range(6)]
        x_in = [sem(f"x_in{j}") for j in range(2)]
        w_in = [sem(f"w_in{j}") for j in range(3)]
        g_in, x_free = sem("g_in"), sem("x_free")
        squares, mean_ready, root_ready = sem("squares"), sem("mean_ready"), sem("root_ready")
        x_normed, turned, kept_v, kept_a = sem("x_normed"), sem("turned"), sem("kept_v"), sem("kept_a")
        w_free = [sem(f"w_free{j}") for j in range(3)]
        p_full = [sem(f"p_full{j}") for j in range(3)]
        p_free_v, p_free_a = sem("p_free_v"), sem("p_free_a")
        with nc.Block() as block:
            @block.sync
            def _(e):
                e.dma_start(S.ident[:, :], A["ident"]).then_inc(g_in, 16)
                e.dma_start(gb[:, :], A["norm1_g"].to_broadcast([P, D])).then_inc(g_in, 16)
                for t in range(NT):
                    if t >= 2:
                        e.wait_ge(x_free, t - 1)
                    e.dma_start(xt[t % 2][:, :], A["x"][t * P:(t + 1) * P, :]).then_inc(x_in[t % 2], 16)
                with e.Fori(0, CT // 3) as i:
                    for j in range(3):
                        e.wait_ge(w_free[j], i + 1)
                        e.dma_start(w[j][:, :, :], A["w_in"][ds(i * 3 + j, 1), :, :, :]
                                    .rearrange("o p k c -> (o p) k c")).then_inc(w_in[j], 16)

            @block.scalar
            def _(e):
                for t in range(NT):
                    e.wait_ge(x_in[t % 2], 16 * (t // 2 + 1))
                    if t >= 1:
                        e.drain()
                    e.activation(junk[:, :], xt[t % 2][:, :], ACT.Square,
                                 accum_out=ss[:, t % 2:t % 2 + 1]).then_inc(squares, 1)
                    e.wait_ge(mean_ready, t + 1)
                    e.activation(rs[:, t % 2:t % 2 + 1], rs[:, t % 2:t % 2 + 1], ACT.Sqrt).then_inc(root_ready, 1)
                    e.wait_ge(turned, 2 * t + 1)
                    e.activation(hT[:, 0:4, t * P:(t + 1) * P], tp[0][:, :, :], ACT.Copy).then_inc(kept_a, 1)
                with e.Fori(0, CT // 3) as i:
                    for j in range(3):
                        e.wait_ge(p_full[j], i + 1)
                        e.activation(S.proj[:, ds(i * 3 + j, 1), 0:HALF].rearrange("p o c -> p (o c)"),
                                     pp[2 * j][:, :], ACT.Copy).then_inc(p_free_a, 1)

            @block.vector
            def _(e):
                e.wait_ge(g_in, 32)
                for t in range(NT):
                    b = t % 2
                    e.wait_ge(squares, t + 1)
                    e.tensor_scalar(rs[:, b:b + 1], ss[:, b:b + 1], 1.0 / D, EPS, ALU.mult, ALU.add
                                    ).then_inc(mean_ready, 1)
                    e.wait_ge(root_ready, t + 1)
                    e.reciprocal(rs[:, b:b + 1], rs[:, b:b + 1])
                    e.drain()
                    e.scalar_tensor_tensor(out=xt[b][:, :], in0=xt[b][:, :], scalar=rs[:, b:b + 1],
                                           in1=gb[:, :], op0=ALU.mult, op1=ALU.mult).then_inc(x_normed, 1)
                    e.wait_ge(turned, 2 * t + 2)
                    e.tensor_copy(hT[:, 4:8, t * P:(t + 1) * P], tp[1][:, :, :]).then_inc(kept_v, 1)
                with e.Fori(0, CT // 3) as i:
                    for j in range(3):
                        e.wait_ge(p_full[j], i + 1)
                        e.tensor_copy(S.proj[:, ds(i * 3 + j, 1), HALF:L].rearrange("p o c -> p (o c)"),
                                      pp[2 * j + 1][:, :]).then_inc(p_free_v, 1)

            @block.tensor
            def _(e):
                for j in range(3):
                    e.sem_inc(w_free[j], 1)
                for t in range(NT):
                    e.wait_ge(x_normed, t + 1)
                    if t >= 1:
                        e.wait_ge(kept_a, t)
                        e.wait_ge(kept_v, t)
                    for k in range(KD):
                        m = e.transpose(tp[k // 4][:, k % 4, :], xt[t % 2][:, k * P:(k + 1) * P], S.ident[:, :])
                        if k == 3:
                            m.then_inc(turned, 1)
                    m.then_inc(turned, 1)
                    e.wait_ge(turned, 2 * t + 2)
                    e.sem_inc(x_free, 1)
                e.wait_ge(kept_a, NT)
                e.wait_ge(kept_v, NT)

                def tile(j, i):
                    e.wait_ge(w_in[j], i * 16 + 16)
                    for h in range(2):
                        for k in range(KD):
                            m = e.matmul(pp[2 * j + h][:, :], w[j][:, k, :], hT[:, k, h * HALF:(h + 1) * HALF],
                                         start=(k == 0), stop=(k == KD - 1))
                    m.then_inc(p_full[j], 1)

                for j in range(3):
                    tile(j, 0)
                with e.Fori(1, CT // 3) as i:
                    for j in range(3):
                        e.wait_ge(p_full[j], i)
                        e.sem_inc(w_free[j], 1)
                        e.wait_ge(p_free_a, i * 3 + (j - 2))
                        e.wait_ge(p_free_v, i * 3 + (j - 2))
                        tile(j, i)


HY_C = HY_D // P
FT = L // P


def hyena(nc, A, S, sem):
    ctx = ExitStack()
    with ctx:
        sb = lambda n, s, t=F32: ctx.enter_context(nc.sbuf_tensor(n, s, t))
        ps = lambda n, s: ctx.enter_context(nc.psum_tensor(n, s, F32))
        vec = sb("h_vec", [P, 6, 4])
        skip = sb("h_skip", [P, HY_C])
        ztok = sb("h_ztok", [P, NT, HY_D])
        fsum = sb("h_fsum", [P, NT, HY_D])
        fdif = sb("h_fdif", [P, NT, HY_D])
        norm = sb("h_norm", [P, HY_C])
        x0, zc = S.mix[:, 2:4, :], S.mix[:, 4:6, :]
        tmp1, tmp2 = S.mix[:, 6, :], S.mix[:, 7, :]
        par_in = sem("h_par_in")

        c1 = ExitStack()
        with c1:
            sb1 = lambda n, s, t=F32: c1.enter_context(nc.sbuf_tensor(n, s, t))
            ps1 = lambda n, s: c1.enter_context(nc.psum_tensor(n, s, F32))
            pos = sb1("h_pos", [33, L])
            w1, w2, w3 = sb1("h_w1", [33, 64]), sb1("h_w2", [64, 64]), sb1("h_w3", [64, 64])
            fb = sb1("h_fb", [64, 4])
            wout = sb1("h_wout", [64, 2 * HY_D])
            decay = sb1("h_decay", [P, NT, HY_D])
            act = sb1("h_act", [64, L])
            arg, turns = sb1("h_arg", [64, L]), sb1("h_turns", [64, L])
            fl = [sb1(f"h_fl{j}", [P, 2, HY_D]) for j in range(2)]
            sq = [sb1(f"h_sq{j}", [P, 2 * HY_D]) for j in range(2)]
            sqsum = sb1("h_sqsum", [P, 2 * HY_D])
            pm = ps1("h_pm", [P, 2, HALF])
            pf = [ps1(f"h_pf{j}", [P, 2 * HY_D]) for j in range(2)]
            pz = [ps1(f"h_pz{j}", [P, 4, P]) for j in range(2)]
            pn = ps1("h_pn", [P, HALF])
            layer, arg_ready, sine = sem("h_layer"), sem("h_arg_ready"), sem("h_sine")
            raw, windowed, squared, summed = sem("h_raw"), sem("h_windowed"), sem("h_squared"), sem("h_summed")
            scaled, convolved, z_ready = sem("h_scaled"), sem("h_convolved"), sem("h_z_ready")
            z_turned, z_kept = sem("h_z_turned"), sem("h_z_kept")
            norm_sum, norm_eps, norm_root = sem("h_norm_sum"), sem("h_norm_eps"), sem("h_norm_root")
            n_par = 9
            with nc.Block() as block:
                @block.sync
                def _(e):
                    for to, of in ((pos, "hy_pos"), (w1, "hy_w1"), (w2, "hy_w2"), (w3, "hy_w3"), (fb, "hy_fb"),
                                   (wout, "hy_wout")):
                        e.dma_start(to[:, :], A[of]).then_inc(par_in, 16)
                    e.dma_start(decay[:, :, :], A["hy_decay"].rearrange("(t p) c -> p t c", p=P)).then_inc(par_in, 16)
                    e.dma_start(vec[:, :, :], A["hy_conv"]).then_inc(par_in, 16)
                    e.dma_start(skip[:, :], A["hy_skip"]).then_inc(par_in, 16)

                @block.tensor
                def _(e):
                    e.wait_ge(par_in, 16 * n_par)
                    for n, w in enumerate((w1, w2, w3)):
                        src = pos if n == 0 else act
                        if n:
                            e.wait_ge(sine, n)
                        for h in range(2):
                            m = e.matmul(pm[0:64, h, :], w[:, :], src[:, h * HALF:(h + 1) * HALF],
                                         start=True, stop=True)
                        m.then_inc(layer, 1)
                    e.wait_ge(sine, 3)
                    for t in range(NT):
                        if t >= 2:
                            e.wait_ge(windowed, t - 1)
                        e.matmul(pf[t % 2][:, :], act[:, t * P:(t + 1) * P], wout[:, :],
                                 start=True, stop=True).then_inc(raw, 1)
                    e.wait_ge(z_ready, 2)
                    for n in range(2 * HY_C):
                        c, h = n // 2, n % 2
                        if n >= 2:
                            e.wait_ge(z_kept, n - 1)
                        for q in range(4):
                            t = 4 * h + q
                            m = e.transpose(pz[n % 2][:, q, :], zc[:, c, t * P:(t + 1) * P], S.ident[:, :])
                        m.then_inc(z_turned, 1)
                    e.wait_ge(summed, NT + 1)
                    for c in range(HY_C):
                        for d in range(2):
                            m = e.matmul(pn[:, c:c + 1], sqsum[:, d * HY_D + c * P:d * HY_D + (c + 1) * P],
                                         S.ones[:, 0:1], start=(d == 0), stop=(d == 1))
                    m.then_inc(norm_sum, 1)

                @block.vector
                def _(e):
                    e.wait_ge(par_in, 16 * n_par)
                    a, k = arg[:, :], turns[:, :]
                    for n in range(3):
                        e.wait_ge(layer, n + 1)
                        e.tensor_scalar(a, pm[0:64, :, :].rearrange("p h c -> p (h c)"), fb[:, n:n + 1], fb[:, 3:4],
                                        ALU.add, ALU.mult)
                        e.drain()
                        e.tensor_scalar(k, a, 1.0 / TWO_PI, ROUND, ALU.mult, ALU.add)
                        e.drain()
                        e.tensor_scalar(k, k, -ROUND, None, ALU.add)
                        e.drain()
                        e.scalar_tensor_tensor(out=a, in0=k, scalar=-PI2_HI, in1=a, op0=ALU.mult, op1=ALU.add)
                        e.drain()
                        e.scalar_tensor_tensor(out=a, in0=k, scalar=-PI2_LO, in1=a, op0=ALU.mult, op1=ALU.add)
                        e.drain()
                        e.tensor_scalar(a, a, float(np.float32(3.1415925)), -float(np.float32(3.1415925)),
                                        ALU.min, ALU.max).then_inc(arg_ready, 1)
                    for t in range(NT):
                        b = t % 2
                        e.wait_ge(raw, t + 1)
                        if t >= 2:
                            e.wait_ge(squared, t - 1)
                        e.tensor_tensor(fl[b][:, :, :], pf[b][:, :].rearrange("p (d c) -> p d c", d=2),
                                        bcast(decay[:, t, :], 2), ALU.mult).then_inc(windowed, 1)
                        e.drain()
                        e.tensor_tensor(fsum[:, t, :], fl[b][:, 0, :], fl[b][:, 1, :], ALU.add)
                        e.tensor_tensor(fdif[:, t, :], fl[b][:, 0, :], fl[b][:, 1, :], ALU.subtract)
                        e.drain()
                    for n, c in enumerate((0, 1, 2, 4, 3, 5)):
                        o = (x0[:, 0, :], x0[:, 1, :], tmp1, tmp2, tmp1, tmp2)[n]
                        u = S.proj[:, T_HY + c, :]
                        e.wait_ge(scaled, n + 1)
                        e.scalar_tensor_tensor(out=o[:, 1:L], in0=u[:, 0:L - 1], scalar=vec[:, c, 0:1], in1=o[:, 1:L],
                                               op0=ALU.mult, op1=ALU.add)
                        e.drain()
                        e.scalar_tensor_tensor(out=o[:, 0:L - 1], in0=u[:, 1:L], scalar=vec[:, c, 2:3],
                                               in1=o[:, 0:L - 1], op0=ALU.mult, op1=ALU.add).then_inc(convolved, 1)
                        e.drain()
                        if n in (3, 5):
                            e.tensor_tensor(zc[:, (n - 3) // 2, :], tmp1, tmp2, ALU.mult).then_inc(z_ready, 1)
                            e.drain()
                    for n in range(2 * HY_C):
                        c, h = n // 2, n % 2
                        e.wait_ge(z_turned, n + 1)
                        e.tensor_copy(ztok[:, 4 * h:4 * h + 4, c * P:(c + 1) * P], pz[n % 2][:, :, :]).then_inc(z_kept, 1)
                    e.wait_ge(norm_sum, 1)
                    e.tensor_scalar(norm[:, :], pn[:, 0:HY_C], 1e-6, None, ALU.add).then_inc(norm_eps, 1)
                    e.wait_ge(norm_root, 1)
                    e.reciprocal(norm[:, :], norm[:, :])
                    e.drain()
                    e.tensor_scalar(norm[:, :], norm[:, :], 1.0 / L, None, ALU.mult)

                @block.scalar
                def _(e):
                    e.wait_ge(par_in, 16 * n_par)
                    for n in range(3):
                        e.wait_ge(arg_ready, n + 1)
                        e.activation(act[:, :], arg[:, :], ACT.Sin).then_inc(sine, 1)
                    for t in range(NT):
                        e.wait_ge(windowed, t + 1)
                        if t >= 2:
                            e.wait_ge(summed, t)
                        e.activation(sq[t % 2][:, :], fl[t % 2][:, :, :].rearrange("p d c -> p (d c)"),
                                     ACT.Square).then_inc(squared, 1)
                    for n, c in enumerate((0, 1, 2, 4, 3, 5)):
                        o = (x0[:, 0, :], x0[:, 1, :], tmp1, tmp2, tmp1, tmp2)[n]
                        if n >= 4:
                            e.wait_ge(z_ready, 1)
                        e.activation(o, S.proj[:, T_HY + c, :], ACT.Identity, bias=vec[:, c, 3:4],
                                     scale=vec[:, c, 1:2]).then_inc(scaled, 1)
                    e.wait_ge(norm_eps, 1)
                    e.activation(norm[:, :], norm[:, :], ACT.Sqrt).then_inc(norm_root, 1)

                @block.gpsimd
                def _(e):
                    e.memset(S.ones[:, :], 1.0)
                    e.memset(sqsum[:, :], 0.0).then_inc(summed, 1)
                    for t in range(NT):
                        e.wait_ge(squared, t + 1)
                        e.wait_ge(summed, t + 1)
                        e.tensor_tensor(sqsum[:, :], sqsum[:, :], sq[t % 2][:, :], ALU.add).then_inc(summed, 1)

        cu = [sb(f"h_cu{j}", [P, 2, NT, P]) for j in range(2)]
        cs = [sb(f"h_cs{j}", [P, 2, NT, P]) for j in range(2)]
        part = lambda c, a, b: S.proj[:, T_HY + c, a * HY_D:b * HY_D].rearrange("p (n c) -> p n c", c=HY_D)
        rows = S.proj[:, T_HY:T_HY + 2, :]
        kf = part(4, 0, 2)
        zk = part(3, 0, 2)
        pr = part(2, 0, 4)
        yf = part(3, 2, 4)
        pk = ps("h_pk", [P, 2, HY_D])
        pzf = ps("h_pzf", [P, 2, HY_D])
        py = [ps(f"h_py{j}", [P, HALF]) for j in range(4)]
        cu_in, cs_in = [sem(f"h_cu_in{j}") for j in range(2)], [sem(f"h_cs_in{j}") for j in range(2)]
        rows_in, rows_free = sem("h_rows_in"), sem("h_rows_free")
        k_full, z_full, k_kept, z_kept2 = sem("h_k_full"), sem("h_z_full"), sem("h_k_kept"), sem("h_z_kept2")
        y_ready, y_used, y_free, k_free = sem("h_y_ready"), sem("h_y_used"), sem("h_y_free"), sem("h_k_free")
        with nc.Block() as block:
            @block.sync
            def _(e):
                def load(f, j, of):
                    e.dma_start(cu[j][:, :, :, :], A["hy_cu"][of, :, :, :, :].rearrange("o p s n f -> (o p) s n f")
                                ).then_inc(cu_in[j], 16)
                    e.dma_start(cs[j][:, :, :, :], A["hy_cs"][of, :, :, :, :].rearrange("o p s n f -> (o p) s n f")
                                ).then_inc(cs_in[j], 16)

                def load_rows(of):
                    e.dma_start(rows[:, :, :], A["hy_rows"][of, :, :, :].rearrange("o p s t -> (o p) s t")
                                ).then_inc(rows_in, 16)
                load(0, 0, slice(0, 1))
                load(1, 1, slice(1, 2))
                load_rows(slice(0, 1))
                with e.Fori(1, FT // 2) as i:
                    for j in range(2):
                        e.wait_ge(z_full, i * 2 + (j - 1))
                        load(None, j, ds(i * 2 + j, 1))
                        e.wait_ge(y_used, i * 2 + (j - 1))
                        load_rows(ds(i * 2 + (j - 1), 1))
                e.wait_ge(y_used, FT - 1)
                load_rows(slice(FT - 1, FT))

            @block.tensor
            def _(e):
                def tile(j, i, first, last):
                    e.wait_ge(cu_in[j], i * 16 + 16)
                    if not first:
                        e.wait_ge(k_kept, i * 2 + j)
                    for s, f in ((0, fsum), (1, fdif)):
                        for n in range(NT):
                            m = e.matmul(pk[:, s, :], cu[j][:, s, n, :], f[:, n, :], start=(n == 0), stop=(n == NT - 1))
                    m.then_inc(k_full, 1)
                    e.wait_ge(cs_in[j], i * 16 + 16)
                    if not first:
                        e.wait_ge(z_kept2, i * 2 + j)
                    for s in range(2):
                        for n in range(NT):
                            m = e.matmul(pzf[:, s, :], cs[j][:, s, n, :], ztok[:, n, :], start=(n == 0), stop=(n == NT - 1))
                    m.then_inc(z_full, 1)
                    e.wait_ge(rows_in, i * 32 + (16 * j + 16))
                    e.wait_ge(y_ready, i * 2 + (j + 1))
                    for c in range(HY_C):
                        for h in range(2):
                            for s in range(2):
                                m = e.matmul(py[2 * c + h][:, :], yf[:, s, c * P:(c + 1) * P],
                                             rows[:, s, h * HALF:(h + 1) * HALF],
                                             start=first and s == 0, stop=last and s == 1, skip_group_check=True)
                    m.then_inc(y_used, 1)
                    e.wait_ge(y_used, i * 2 + (j + 1))
                    e.sem_inc(y_free, 1)
                tile(0, 0, True, False)
                tile(1, 0, False, False)
                with e.Fori(1, FT // 2 - 1) as i:
                    tile(0, i, False, False)
                    tile(1, i, False, False)
                tile(0, FT // 2 - 1, False, False)
                tile(1, FT // 2 - 1, False, True)

            @block.scalar
            def _(e):
                with e.Fori(0, FT) as i:
                    e.wait_ge(k_full, i + 1)
                    e.wait_ge(k_free, i + 1)
                    e.activation(kf[:, :, :], pk[:, :, :], ACT.Copy).then_inc(k_kept, 1)

            @block.vector
            def _(e):
                e.sem_inc(k_free, 1)
                e.sem_inc(y_free, 1)
                with e.Fori(0, FT) as i:
                    e.wait_ge(z_full, i + 1)
                    e.wait_ge(k_kept, i + 1)
                    k = kf
                    e.tensor_copy(zk[:, :, :], pzf[:, :, :]).then_inc(z_kept2, 1)
                    e.drain()
                    e.tensor_tensor(pr[:, 0:2, :], zk[:, :, :], k[:, :, :], ALU.mult)
                    e.tensor_tensor(pr[:, 2, :], zk[:, 0, :], k[:, 1, :], ALU.mult)
                    e.tensor_tensor(pr[:, 3, :], zk[:, 1, :], k[:, 0, :], ALU.mult)
                    e.drain()
                    e.sem_inc(k_free, 1)
                    e.wait_ge(y_free, i + 1)
                    e.tensor_tensor(yf[:, 0, :], pr[:, 0, :], pr[:, 1, :], ALU.subtract)
                    e.tensor_tensor(yf[:, 1, :], pr[:, 2, :], pr[:, 3, :], ALU.add).then_inc(y_ready, 1)
                    e.drain()
                e.wait_ge(y_used, FT)
                for c in range(HY_C):
                    e.tensor_scalar(zc[:, c, :], zc[:, c, :], skip[:, c:c + 1], None, ALU.mult)
                e.drain()
                for c in range(HY_C):
                    for h in range(2):
                        cut = slice(h * HALF, (h + 1) * HALF)
                        e.scalar_tensor_tensor(out=zc[:, c, cut], in0=py[2 * c + h][:, :], scalar=norm[:, c:c + 1],
                                               in1=zc[:, c, cut], op0=ALU.mult, op1=ALU.add)
                e.drain()
                for c in range(HY_C):
                    e.tensor_tensor(S.mix[:, c, :], zc[:, c, :], x0[:, c, :], ALU.mult)


HD = 64
ROWS = L // HD
KR = 8
NPAIR = NA_D // P
NB_T = 6


def attention(nc, A, S, sem):
    ctx = ExitStack()
    with ctx:
        sb = lambda n, s, t=F32: ctx.enter_context(nc.sbuf_tensor(n, s, t))
        ps = lambda n, s: ctx.enter_context(nc.psum_tensor(n, s, F32))
        bias = sb("n_bias", [P, NPAIR, 2 * KR - 1, HD])
        band = sb("n_band", [P, HD])
        vt = sb("n_vt", [P, ROWS - 1, NA_D])
        qd = [sb(f"n_qd{j}", [P, P]) for j in range(2)]
        sc = [sb(f"n_sc{j}", [P, HALF]) for j in range(2)]
        pt = [sb(f"n_pt{j}", [P, 4, P]) for j in range(2)]
        od = [sb(f"n_od{j}", [P, P]) for j in range(2)]
        top = sb("n_top", [P, 2])
        tot = sb("n_tot", [P, 2])
        s_ps = [ps(f"n_s{j}", [P, HALF]) for j in range(2)]
        t_ps = [ps(f"n_t{j}", [P, 4, P]) for j in range(2)]
        o_ps = [ps(f"n_o{j}", [P, P]) for j in range(2)]
        f_ps = [ps(f"n_f{j}", [P, P]) for j in range(2)]
        par_in, bias_ready, v_turned, v_kept = sem("n_par_in"), sem("n_bias_ready"), sem("n_v_turned"), sem("n_v_kept")
        q_ready, q_used = sem("n_q_ready"), sem("n_q_used")
        s_full, biased, top_ready, exps = sem("n_s_full"), sem("n_biased"), sem("n_top_ready"), sem("n_exps")
        p_turned, p_kept, o_full, o_kept = sem("n_p_turned"), sem("n_p_kept"), sem("n_o_full"), sem("n_o_kept")
        f_full, f_kept = sem("n_f_full"), sem("n_f_kept")
        s_free, o_free, p_free = sem("n_s_free"), sem("n_o_free"), sem("n_p_free")
        SPANS = ((0, KR // 2, lambda r: 0, lambda r: r * -1 + (KR - 1)),
                 (KR // 2, ROWS - KR // 2, lambda r: r - KR // 2, lambda r: KR // 2 - 1),
                 (ROWS - KR // 2, ROWS, lambda r: ROWS - KR, lambda r: r * -1 + (ROWS - 1)))

        def rows(e, body):
            with e.Fori(0, NPAIR) as pair:
                for lo, hi, start, drow in SPANS:
                    with e.Fori(lo // 2, hi // 2) as h:
                        for j in range(2):
                            r = h * 2 + j
                            body(pair * ROWS + r, j, pair, r, start(r), drow(r))

        with nc.Block() as block:
            @block.sync
            def _(e):
                e.dma_start(bias[:, :, :, :], A["na_bias"]).then_inc(par_in, 16)
                e.dma_start(band[:, :], A["na_band"]).then_inc(par_in, 16)

            @block.gpsimd
            def _(e):
                for j in range(2):
                    e.memset(qd[j][:, :], 0.0).then_inc(q_ready, 1)
                    e.memset(od[j][:, :], 0.0).then_inc(q_ready, 1)
                e.wait_ge(par_in, 32)
                for p in range(NPAIR):
                    e.tensor_tensor(bias[:, p, :, :], bias[:, p, :, :], bcast(band[:, :], 2 * KR - 1), ALU.add
                                    ).then_inc(bias_ready, 1)
                e.wait_ge(q_ready, 4)

                def queries(n, j, pair, r, s, dr):
                    e.drain()
                    e.wait_ge(q_used, n + 1)
                    q = S.proj[:, ds(pair + T_Q, 1), ds(r * HD, HD)].rearrange("p o c -> p (o c)")
                    e.tensor_copy(qd[j][0:HD, 0:HD], q[0:HD, :])
                    e.drain()
                    e.tensor_copy(qd[j][HD:P, HD:P], q[HD:P, :]).then_inc(q_ready, 1)
                rows(e, queries)

            @block.tensor
            def _(e):
                e.sem_inc(q_used, 2)
                e.sem_inc(p_free, 2)
                for s in range(0, ROWS - 1):
                    if s >= 2:
                        e.wait_ge(v_kept, s - 1)
                    for p in range(NPAIR):
                        m = e.transpose(t_ps[s % 2][:, p, :], S.proj[:, T_NV + p, s * HD:s * HD + P], S.ident[:, :])
                    m.then_inc(v_turned, 1)
                e.wait_ge(v_kept, ROWS - 1)

                def row(n, j, pair, r, s, dr):
                    e.wait_ge(q_ready, n + 5)
                    e.wait_ge(s_free, n + 1)
                    e.matmul(s_ps[j][:, :], qd[j][:, :],
                             S.proj[:, ds(pair + T_NK, 1), ds(s * HD, KR * HD)].rearrange("p o c -> p (o c)"),
                             start=True, stop=True).then_inc(s_full, 1)
                    e.wait_ge(s_full, n + 1)
                    e.sem_inc(q_used, 1)
                    e.wait_ge(exps, n + 1)
                    e.wait_ge(p_free, n + 1)
                    for c in range(4):
                        m = e.transpose(t_ps[j][:, c, :], sc[j][:, c * P:(c + 1) * P], S.ident[:, :])
                    m.then_inc(p_turned, 1)
                    e.wait_ge(p_kept, n + 1)
                    e.sem_inc(p_free, 1)
                    e.wait_ge(o_free, n + 1)
                    for c in range(4):
                        m = e.matmul(o_ps[j][:, :], pt[j][:, c, :],
                                     vt[:, ds(s + 2 * c, 1), ds(pair * P, P)].rearrange("p o c -> p (o c)"),
                                     start=(c == 0), stop=(c == 3))
                    m.then_inc(o_full, 1)
                    e.wait_ge(o_kept, n + 1)
                    e.transpose(f_ps[j][:, :], od[j][:, :], S.ident[:, :]).then_inc(f_full, 1)
                rows(e, row)

            @block.vector
            def _(e):
                for s in range(0, ROWS - 1):
                    e.wait_ge(v_turned, s + 1)
                    e.tensor_copy(vt[:, s, :].rearrange("p (a c) -> p a c", a=NPAIR), t_ps[s % 2][:, 0:NPAIR, :]
                                  ).then_inc(v_kept, 1)
                e.wait_ge(bias_ready, NPAIR)
                e.wait_ge(q_ready, 4)
                e.sem_inc(s_free, 2)
                e.sem_inc(o_free, 2)

                def row(n, j, pair, r, s, dr):
                    e.wait_ge(s_full, n + 1)
                    e.scalar_tensor_tensor(out=sc[j][:, :], in0=s_ps[j][:, :], scalar=HD ** -0.5,
                                           in1=bias[:, ds(pair, 1), ds(dr, KR), :].rearrange("p o a c -> p (o a c)"),
                                           op0=ALU.mult, op1=ALU.add).then_inc(biased, 1)
                    e.drain()
                    e.sem_inc(s_free, 1)
                    e.tensor_reduce(top[:, j:j + 1], sc[j][:, :], AX.X, ALU.max, negate=True).then_inc(top_ready, 1)
                    e.wait_ge(exps, n + 1)
                    e.reciprocal(tot[:, j:j + 1], tot[:, j:j + 1])
                    e.drain()
                    e.wait_ge(o_full, n + 1)
                    e.tensor_scalar(od[j][0:HD, 0:HD], o_ps[j][0:HD, 0:HD], tot[0:HD, j:j + 1], None, ALU.mult)
                    e.tensor_scalar(od[j][HD:P, HD:P], o_ps[j][HD:P, HD:P], tot[HD:P, j:j + 1], None, ALU.mult
                                    ).then_inc(o_kept, 1)
                    e.drain()
                    e.sem_inc(o_free, 1)
                rows(e, row)

            @block.scalar
            def _(e):
                def row(n, j, pair, r, s, dr):
                    e.wait_ge(top_ready, n + 1)
                    e.activation(sc[j][:, :], sc[j][:, :], ACT.Exp, bias=top[:, j:j + 1],
                                 accum_out=tot[:, j:j + 1]).then_inc(exps, 1)
                    e.wait_ge(p_turned, n + 1)
                    e.activation(pt[j][:, :, :], t_ps[j][:, :, :], ACT.Copy).then_inc(p_kept, 1)
                    e.wait_ge(f_full, n + 1)
                    for h in (slice(0, HD), slice(HD, P)):
                        m = e.activation(S.mix[h, ds(pair + NB_T, 1), ds(r * HD, HD)].rearrange("p o c -> p (o c)"),
                                         f_ps[j][h, h], ACT.Copy)
                    m.then_inc(f_kept, 1)
                rows(e, row)


PAIRS = RW_D // P
CH = 64
NCH = L // CH
DECAY_C = float(np.exp(-0.5))
MU_R, MU_K, MU_V, W0, A0, C_KK, C_KA, C_RK, C_LNW, C_LNB, C_MID, C_KA1, N_PAR = 0, 2, 4, 6, 8, 10, 11, 12, 13, 14, 15, 18, 19
OP_A, OP_R, OP_B, OP_K, OP_V, N_OP = 0, 1, 2, 3, 4, 5


def rwkv_operands(nc, A, S, sem):
    ctx = ExitStack()
    with ctx:
        sb = lambda n, s, t=F32: ctx.enter_context(nc.sbuf_tensor(n, s, t))
        ps = lambda n, s: ctx.enter_context(nc.psum_tensor(n, s, F32))
        own = [sb(f"r_t{j}", [P, L]) for j in range(10)]
        old = [S.proj[:, T_HY + j, :] for j in range(6)] + [S.mix[:, 6 + j, :] for j in range(2)]
        rr, kk, vv, kn, *rest = [t[:, :] for t in own]
        a2, x2, kd2 = rest[0:2], rest[2:4], rest[4:6]
        sg2, ep2, en2, ea2 = old[0:2], old[2:4], old[4:6], old[6:8]
        lw = sb("r_lw", [P, 3, P])
        reset = sb("r_reset", [P, L])
        heads = sb("r_heads", [P, P])
        half = sb("r_half", [P, 2, NCH])
        zp = [ps(f"r_z{j}", [P, 2, HALF]) for j in range(4)]
        flat = lambda t: t[:, :, :].rearrange("p h c -> p (h c)")
        par = S.rpar
        par_in, ready0, lora, mid0 = sem("r_par_in"), sem("r_ready0"), sem("r_lora_in"), sem("r_mid0")
        passed = sem("r_passed")
        mid, shifted, sig, sq_done, ssq_done = sem("r_mid"), sem("r_shifted"), sem("r_sig"), sem("r_sq"), sem("r_ssq")
        z_full, kmax, kroot, kn_done = sem("r_z_full"), sem("r_kmax"), sem("r_kroot"), sem("r_kn")
        x_done, xd_done, e_done, k_done = sem("r_x"), sem("r_xd"), sem("r_e"), sem("r_kdir")
        pb_done, bon_full, gate_full, gate_done = sem("r_pb"), sem("r_bon"), sem("r_gate_full"), sem("r_gate")
        ops_done, pool_done, stored, pair_free, rest_done = (sem("r_ops"), sem("r_pool"), sem("r_stored"),
                                                             sem("r_pair_free"), sem("r_rest"))
        pcol = lambda pair, c: par[:, ds(pair, 1), c:c + 1].rearrange("p o c -> p (o c)")
        src = lambda pair, t: S.proj[:, ds(pair + t, 1), :].rearrange("p o c -> p (o c)")
        with nc.Block() as block:
            @block.sync
            def _(e):
                e.dma_start(par[:, :, 0:C_MID], A["rw_par"]).then_inc(par_in, 16)
                e.dma_start(reset[:, :], A["rw_reset"]).then_inc(par_in, 16)
                e.dma_start(heads[:, :], A["rw_heads"]).then_inc(par_in, 16)
                with e.Fori(0, PAIRS) as p:
                    e.wait_ge(pair_free, p + 1)
                    e.dma_start(lw[:, :, :], A["rw_lora"][ds(p, 1), :, :, :].rearrange("o p s c -> (o p) s c")
                                ).then_inc(lora, 16)

                    def store(d, slot, of):
                        e.sem_inc(passed, 1)
                        e.dma_start(S.ops[ds(p, 1), d, :, :, slot, :].rearrange("o t p c -> (o p) t c"),
                                    of.rearrange("p (t c) -> p t c", c=P)).then_inc(stored, 16)
                    e.wait_ge(shifted, p * 3 + 3)
                    for d in range(2):
                        store(d, OP_V, vv)
                    for d in range(2):
                        e.wait_ge(ops_done, p * 4 + (2 * d + 1))
                        store(d, OP_A, ea2[d])
                        e.wait_ge(ops_done, p * 4 + (2 * d + 2))
                        store(d, OP_B, a2[d])
                        e.wait_ge(pool_done, p * 4 + (2 * d + 1))
                        store(d, OP_R, ep2[d])
                        e.wait_ge(pool_done, p * 4 + (2 * d + 2))
                        store(d, OP_K, en2[d])
                    e.wait_ge(stored, p * 160 + 160)
                    e.wait_ge(rest_done, p + 1)
                    e.sem_inc(pair_free, 1)

            @block.tensor
            def _(e):
                e.wait_ge(ready0, 2)
                with e.Fori(0, PAIRS) as p:
                    e.wait_ge(lora, p * 16 + 16)
                    for s, t in ((0, T_W), (1, T_A)):
                        for d in range(2):
                            r = slice(d * 64, d * 64 + 64)
                            for h in range(2):
                                m = e.matmul(zp[2 * s + d][:, h, :], lw[r, s, :], S.proj[r, t, h * HALF:(h + 1) * HALF],
                                             start=True, stop=True)
                            m.then_inc(z_full, 1)
                    e.wait_ge(sig, p * 4 + 2)
                    e.wait_ge(sq_done, p + 1)
                    for h in range(2):
                        m = e.matmul(zp[0][:, h, :], heads[:, :], kd2[0][:, h * HALF:(h + 1) * HALF], start=True, stop=True)
                    m.then_inc(ssq_done, 1)
                    for h in range(2):
                        m = e.matmul(zp[1][:, h, :], lw[:, 2, :], S.proj[:, T_G, h * HALF:(h + 1) * HALF],
                                     start=True, stop=True)
                    m.then_inc(gate_full, 1)
                    e.wait_ge(sig, p * 4 + 4)
                    e.wait_ge(pb_done, p + 1)
                    for h in range(2):
                        m = e.matmul(zp[2][:, h, :], heads[:, :], x2[0][:, h * HALF:(h + 1) * HALF], start=True, stop=True)
                    m.then_inc(bon_full, 1)

            @block.scalar
            def _(e):
                e.wait_ge(par_in, 48)
                e.activation(S.proj[:, T_W, :], S.proj[:, T_W, :], ACT.Tanh).then_inc(ready0, 1)
                e.activation(S.proj[:, T_G, :], S.proj[:, T_G, :], ACT.Sigmoid).then_inc(ready0, 1)
                e.wait_ge(mid0, 1)
                with e.Fori(0, PAIRS) as p:
                    e.wait_ge(pair_free, p + 1)
                    for n, (o, t) in enumerate(((rr, T_R), (kk, T_K), (vv, T_V))):
                        e.activation(o, src(p, t), ACT.Identity, scale=pcol(p, C_MID + n)).then_inc(mid, 1)
                    for s in range(2):
                        for d in range(2):
                            e.wait_ge(z_full, p * 4 + (2 * s + d + 1))
                            e.activation((sg2, a2)[s][d], flat(zp[2 * s + d]), ACT.Sigmoid,
                                         bias=pcol(p, (W0, A0)[s] + d)).then_inc(sig, 1)
                    e.wait_ge(shifted, p * 3 + 2)
                    e.activation(kd2[0], kk, ACT.Square, scale=pcol(p, C_KK)).then_inc(sq_done, 1)
                    e.wait_ge(kmax, p + 1)
                    e.activation(kn, kn, ACT.Sqrt).then_inc(kroot, 1)
                    for d in range(2):
                        e.wait_ge(x_done, p * 2 + (d + 1))
                        e.wait_ge(xd_done, p * 2 + (d + 1))
                        c = DECAY_C
                        if d == 0:
                            e.activation(ep2[0], x2[0], ACT.Exp, scale=-c)
                            e.activation(en2[0], x2[0], ACT.Exp, scale=c)
                            e.activation(ea2[0], sg2[0], ACT.Exp, scale=-c).then_inc(e_done, 1)
                        else:
                            e.activation(ep2[1], sg2[1], ACT.Exp, scale=-c)
                            e.activation(en2[1], sg2[1], ACT.Exp, scale=c)
                            e.activation(ea2[1], x2[1], ACT.Exp, scale=c).then_inc(e_done, 1)
                    e.drain()
                    e.wait_ge(gate_full, p + 1)
                    e.activation(x2[1], flat(zp[1]), ACT.Copy).then_inc(gate_done, 1)
                e.wait_ge(rest_done, PAIRS)
                e.activation(S.carry[:, :, :, :], S.carry[:, :, :, :], ACT.Exp, scale=-DECAY_C)

            @block.gpsimd
            def _(e):
                with e.Fori(0, PAIRS) as p:
                    e.wait_ge(shifted, p * 3 + 3)
                    for d in range(2):
                        e.wait_ge(e_done, p * 2 + (d + 1))
                        e.tensor_tensor(ep2[d], ep2[d], rr, ALU.mult).then_inc(pool_done, 1)
                        e.drain()
                        e.wait_ge(k_done, p * 2 + (d + 1))
                        e.wait_ge(ops_done, p * 4 + (2 * d + 2))
                        e.tensor_tensor(en2[d], en2[d], kd2[d], ALU.mult).then_inc(pool_done, 1)
                        e.drain()

            @block.vector
            def _(e):
                e.wait_ge(par_in, 48)
                e.memset(S.carry[:, :, :, :], 0.0)
                for n in range(3):
                    e.tensor_tensor(par[:, :, C_MID + n], par[:, :, 2 * n], par[:, :, 2 * n + 1], ALU.add)
                e.drain()
                e.tensor_scalar(par[:, :, C_MID:C_MID + 3], par[:, :, C_MID:C_MID + 3], -1.0, 1.0, ALU.mult, ALU.add)
                e.tensor_scalar(par[:, :, C_KA1], par[:, :, C_KA], -1.0, 1.0, ALU.mult, ALU.add)
                e.drain()
                e.sem_inc(mid0, 1)
                e.sem_inc(pair_free, 1)
                with e.Fori(0, PAIRS) as p:
                    for n, (o, t, c) in enumerate(((rr, T_R, MU_R), (kk, T_K, MU_K), (vv, T_V, MU_V))):
                        u = S.proj[:, ds(p + t, 1), :]
                        at = lambda a, b: u[:, :, a:b].rearrange("p o c -> p (o c)")
                        e.wait_ge(mid, p * 3 + (n + 1))
                        e.scalar_tensor_tensor(out=o[:, 1:L], in0=at(0, L - 1), scalar=pcol(p, c), in1=o[:, 1:L],
                                               op0=ALU.mult, op1=ALU.add)
                        e.drain()
                        e.scalar_tensor_tensor(out=o[:, 0:L - 1], in0=at(1, L), scalar=pcol(p, c + 1),
                                               in1=o[:, 0:L - 1], op0=ALU.mult, op1=ALU.add).then_inc(shifted, 1)
                    for d in range(2):
                        x = x2[d]
                        e.wait_ge(sig, p * 4 + (d + 1))
                        e.tensor_tensor_scan(x, reset[:, :], sg2[d], 0.0, ALU.mult, ALU.add)
                        e.drain()
                        xc = x.rearrange("p (n c) -> p n c", c=CH)
                        e.tensor_scalar(half[:, d, :], xc[:, :, CH - 1], 0.5, None, ALU.mult)
                        e.drain()
                        e.tensor_tensor(xc, xc, half[:, d, :].unsqueeze(2).to_broadcast([P, NCH, CH]), ALU.subtract
                                        ).then_inc(x_done, 1)
                        e.drain()
                        if d == 0:
                            e.tensor_tensor(sg2[0], x, sg2[0], ALU.subtract).then_inc(xd_done, 1)
                        else:
                            e.tensor_tensor(sg2[1], sg2[1], x, ALU.subtract).then_inc(xd_done, 1)
                        a, b = (half[:, d, 0:NCH - 1], half[:, d, 1:NCH])
                        to = S.carry[:, ds(p, 1), d, d:NCH - 1 + d].rearrange("p o c -> p (o c)")
                        e.tensor_tensor(to, a, b, ALU.add)
                    e.wait_ge(ssq_done, p + 1)
                    e.tensor_scalar(kn, flat(zp[0]), 1e-24, None, ALU.max).then_inc(kmax, 1)
                    for d in range(2):
                        if d == 0:
                            e.wait_ge(sig, p * 4 + 4)
                        e.tensor_scalar(kd2[d], a2[d], pcol(p, C_KA), pcol(p, C_KA1), ALU.mult, ALU.add)
                        e.drain()
                        e.tensor_tensor(kd2[d], kd2[d], kk, ALU.mult).then_inc(k_done, 1)
                    e.wait_ge(kroot, p + 1)
                    e.reciprocal(kn, kn)
                    e.drain()
                    e.scalar_tensor_tensor(out=kn, in0=kk, scalar=pcol(p, C_KK), in1=kn, op0=ALU.mult, op1=ALU.mult)
                    e.drain()
                    for d in range(2):
                        e.tensor_tensor(a2[d], a2[d], kn, ALU.mult)
                        e.wait_ge(e_done, p * 2 + (d + 1))
                        e.scalar_tensor_tensor(out=ea2[d], in0=kn, scalar=-1.0, in1=ea2[d], op0=ALU.mult, op1=ALU.mult
                                               ).then_inc(ops_done, 1)
                        e.drain()
                        e.tensor_tensor(a2[d], a2[d], en2[d], ALU.mult).then_inc(ops_done, 1)
                    e.tensor_tensor(x2[0], kd2[0], kd2[1], ALU.add)
                    e.drain()
                    e.scalar_tensor_tensor(out=x2[0], in0=x2[0], scalar=pcol(p, C_RK), in1=rr, op0=ALU.mult, op1=ALU.mult
                                           ).then_inc(pb_done, 1)
                    e.wait_ge(gate_done, p + 1)
                    e.wait_ge(bon_full, p + 1)
                    out = S.mix[:, ds(p + 2, 1), :].rearrange("p o c -> p (o c)")
                    e.tensor_tensor(out, flat(zp[2]), vv, ALU.mult)
                    e.drain()
                    e.scalar_tensor_tensor(out=out, in0=out, scalar=pcol(p, C_LNB), in1=x2[1], op0=ALU.add, op1=ALU.mult)
                    e.tensor_scalar(src(p, T_R), x2[1], pcol(p, C_LNW), None, ALU.mult)
                    e.drain()
                    e.sem_inc(rest_done, 1)


LEVELS = 6
TM_A, TM_B, TM_K, TM_V = 0, 1, 2, 3
G_AB, G_RB, G_AK, G_RK = 0, 1, 2, 3


def rwkv_scan(nc, A, S, sem):
    ctx = ExitStack()
    with ctx:
        sb = lambda n, s, t=F32: ctx.enter_context(nc.sbuf_tensor(n, s, t))
        ps = lambda n, s: ctx.enter_context(nc.psum_tensor(n, s, F32))
        op = [[sb(f"s_op{j}{d}", [P, N_OP, P]) for d in range(2)] for j in range(2)]
        mask = sb("s_mask", [P, 2, 4, P])
        level = sb("s_level", [P, LEVELS, P])
        eye2 = sb("s_eye2", [P, CH])
        tm = sb("s_tm", [P, 2, 3, P])
        g = sb("s_g", [P, 4, 4, P])
        al = sb("s_al", [P, LEVELS, 4, P])
        th, xx = sb("s_th", [P, 2, 2, 2, P]), sb("s_xx", [P, 4, P])
        tt, hh = (lambda u: th[:, u // 2, 0, u % 2, :]), (lambda u: th[:, u // 2, 1, u % 2, :])
        rv = sb("s_rv", [P, 4, P])
        pu = sb("s_pu", [P, 4, P])
        qt = sb("s_qt", [P, 2, P])
        mt, nn = sb("s_mt", [P, 2, 2, CH]), sb("s_nn", [P, 2, 2, CH])
        st = [sb(f"s_st{j}", [P, 2, CH]) for j in range(2)]
        sm = [sb(f"s_sm{j}", [P, 2, CH]) for j in range(2)]
        y = sb("s_y", [P, 2, NT, P])
        bank = [ps(f"s_bank{j}", [P, 4, P]) for j in range(8)]
        trb, gb, xb, thb = bank[0:2], bank[2:4], bank[4:6], bank[6:8]
        pub, mnb, akvb, cb, qb, yb = bank[0], (bank[1], bank[5]), bank[2], (bank[3], bank[2]), bank[4], bank[6:8]
        par_in = sem("s_par_in")
        op_in = [sem(f"s_op_in{j}") for j in range(2)]
        op_free = [sem(f"s_op_free{j}") for j in range(2)]
        pe_step, turned, g_full, g_kept = sem("s_pe_step"), sem("s_turned"), sem("s_g_full"), sem("s_g_kept")
        tm_kept, h_ready, t_full, t_kept = sem("s_tm_kept"), sem("s_h_ready"), sem("s_t_full"), sem("s_t_kept")
        al_ready, x_full, x_kept = sem("s_al_ready"), sem("s_x_full"), sem("s_x_kept")
        th_full, th_kept = sem("s_th_full"), sem("s_th_kept")
        akv_full, akv_kept, pu_full, pu_kept = sem("s_akv_full"), sem("s_akv_kept"), sem("s_pu_full"), sem("s_pu_kept")
        q_full, q_kept, m_full, m_kept = sem("s_q_full"), sem("s_q_kept"), sem("s_m_full"), sem("s_m_kept")
        n_full, n_kept = sem("s_n_full"), sem("s_n_kept")
        c_full, y_full, y_kept = sem("s_c_full"), sem("s_y_full"), sem("s_y_kept")
        reset_done, yt_full, y_normed, pair_out = sem("s_reset"), sem("s_yt_full"), sem("s_y_normed"), sem("s_pair_out")
        zeroed, cleared = sem("s_zeroed"), sem("s_cleared")
        eps_ready, root_ready, loads = sem("s_eps_ready"), sem("s_root"), sem("s_loads")
        pu_free, g_free, hl_kept, al_used = sem("s_pu_free"), sem("s_g_free"), sem("s_hl_kept"), sem("s_al_used")
        c_ready, c_mid, pe_done, y_free = sem("s_c_ready"), sem("s_c_mid"), sem("s_pe_done"), sem("s_y_free")
        stat = sb("s_stat", [P, 2, 2 * NT])
        c7 = NT - 1

        hs = [slice(0, CH), slice(CH, P)]
        with nc.Block() as block:
            @block.sync
            def _(e):
                e.dma_start(mask[:, :, :, :], A["rw_mask"]).then_inc(par_in, 16)
                e.dma_start(level[:, :, :], A["rw_level"]).then_inc(par_in, 16)
                e.dma_start(eye2[:, :], A["rw_eye2"]).then_inc(par_in, 16)
                e.wait_ge(zeroed, 1)
                clear_beyond(e, S, S.proj[:, T_HY, :], cleared)
                e.wait_ge(cleared, 16)
                with e.Fori(0, PAIRS) as pair:
                    with e.Fori(0, NT // 2) as h:
                        for j in range(2):
                            e.wait_ge(op_free[j], pair * (NT // 2) + h + 1)
                            e.sem_inc(loads, 1)
                            e.dma_start(op[j][0][:, :, :], S.ops[ds(pair, 1), 0, ds(h * 2 + j, 1), :, :, :]
                                        .rearrange("o u p s c -> (o u p) s c")).then_inc(op_in[j], 16)
                            e.dma_start(op[j][1][:, :, :], S.ops[ds(pair, 1), 1, ds(h * -2 + (c7 - j), 1), :, :, :]
                                        .rearrange("o u p s c -> (o u p) s c")).then_inc(op_in[j], 16)

            @block.tensor
            def _(e):
                e.wait_ge(par_in, 48)

                def tile(n, j, pair, i, half_n):
                    e.wait_ge(op_in[j], half_n * 32 + 32)
                    e.wait_ge(pu_free, n + 1)
                    for d in range(2):
                        for q, s in enumerate((OP_A, OP_B, OP_K, OP_V)):
                            m = e.transpose(trb[d][:, q, :], op[j][d][:, s, :], S.ident[:, :])
                        m.then_inc(turned, 1)
                    e.wait_ge(c_ready, n + pair + 1)
                    for u in range(4):
                        d, h = u // 2, u % 2
                        o = op[j][d]
                        e.wait_ge(g_free, n * 4 + (u + 1))
                        for q, s in ((0, OP_B), (2, OP_K)):
                            m = e.matmul(gb[u % 2][:, q:q + 2, :].rearrange("p q c -> p (q c)"), o[hs[h], s, :],
                                         o[hs[h], OP_A:OP_R + 1, :].rearrange("p q c -> p (q c)"), start=True, stop=True)
                        m.then_inc(g_full, 1)
                    e.wait_ge(h_ready, n + 1)
                    for u in range(4):
                        m = e.transpose(thb[u // 2][:, u % 2, :], hh(u), S.ident[:, :])
                    m.then_inc(t_full, 1)
                    e.wait_ge(g_kept, n * 4 + 4)
                    e.wait_ge(tm_kept, n * 4 + 4)
                    for u in range(4):
                        d, h = u // 2, u % 2
                        m = e.matmul(akvb[:, u, 0:CH], g[:, G_AK, u, :], tm[:, d, TM_V - 1, h * CH:h * CH + CH],
                                     start=True, stop=True)
                    m.then_inc(akv_full, 1)
                    e.wait_ge(t_kept, n + 1)
                    for l in range(1, LEVELS):
                        e.wait_ge(al_ready, n * LEVELS + (l + 1))
                        for d in range(2):
                            if l > 1:
                                e.wait_ge(th_kept, n * 8 + (2 * (l - 2) + d + 1))
                            for u in (2 * d, 2 * d + 1):
                                m = e.matmul(xb[d][:, u % 2, :], al[:, l, u, :], tt(u), start=True, stop=True)
                            m.then_inc(x_full, 1)
                        for d in range(2):
                            e.wait_ge(x_kept, n * 10 + (2 * (l - 1) + d + 1))
                            for u in (2 * d, 2 * d + 1):
                                if l < LEVELS - 1:
                                    e.matmul(thb[d][:, u % 2, :], hh(u), xx[:, u, :], start=True, stop=True)
                                m = e.matmul(thb[d][:, 2 + u % 2, :], xx[:, u, :], hh(u), start=True, stop=True)
                            m.then_inc(th_full, 1)
                    e.wait_ge(hl_kept, n * 2 + 2)
                    e.wait_ge(akv_kept, n + 1)
                    for u in range(4):
                        m = e.matmul(pub[:, u, :], hh(u), rv[:, u, :], start=True, stop=True)
                    m.then_inc(pu_full, 1)
                    e.wait_ge(pu_kept, n + 1)
                    e.sem_inc(pe_step, 1)
                    for d in range(2):
                        for c in range(2):
                            for h in range(2):
                                u, col = 2 * d + h, slice(h * CH, h * CH + CH)
                                e.matmul(mnb[c][hs[h], d, 0:CH], pu[hs[c], u, 0:CH], tm[hs[c], d, TM_B - 1, col],
                                         start=True, stop=True)
                                e.matmul(mnb[c][hs[h], d, CH:P], tm[hs[c], d, TM_B - 1, col], pu[hs[c], u, CH:P],
                                         start=True, stop=False)
                                m = e.matmul(mnb[c][hs[h], d, CH:P], tm[hs[c], d, TM_K - 1, col],
                                             tm[hs[c], d, TM_V - 1, col], start=False, stop=True)
                    m.then_inc(m_full, 1)
                    for d in range(2):
                        for h in range(2):
                            m = e.matmul(qb[hs[h], d, :], pu[:, 2 * d + h, 0:CH], g[:, G_RB, 2 * d + h, :],
                                         start=True, stop=True)
                    m.then_inc(q_full, 1)
                    for c in range(2):
                        e.wait_ge(m_kept, n + 1)
                        e.wait_ge(n_kept, n + 1)
                        if c == 0:
                            e.wait_ge(c_ready, n + pair + 1)
                        else:
                            e.wait_ge(c_mid, n + 1)
                        e.sem_inc(pe_step, 1)
                        src = (st[j], sm[j])[c]
                        for d in range(2):
                            cc = c if d == 0 else 1 - c
                            for h in range(2):
                                m = e.matmul(cb[c][hs[h], d, 0:CH], mt[hs[h], d, cc, :], src[hs[h], d, :],
                                             start=True, stop=True)
                        m.then_inc(c_full, 1)
                    e.wait_ge(q_kept, n + 1)
                    for u in range(4):
                        d, h = u // 2, u % 2
                        o = yb[h][:, d, 0:CH]
                        e.matmul(o, g[:, G_RB, u, :], pu[:, u, CH:P], start=True, stop=False, skip_group_check=True)
                        e.matmul(o, g[:, G_RK, u, :], tm[:, d, TM_V - 1, h * CH:h * CH + CH], start=False, stop=False,
                                 skip_group_check=True)
                        for c in range(2):
                            s0 = (st[j], sm[j])[c if d == 0 else 1 - c]
                            m = e.matmul(yb[h][hs[c], d, 0:CH], qt[hs[h], d, c * CH:c * CH + CH], s0[hs[h], d, :],
                                         start=False, stop=(c == 1), skip_group_check=True)
                    m.then_inc(y_full, 1)
                    e.wait_ge(y_full, n + 1)
                    e.sem_inc(op_free[j], 1)
                    e.sem_inc(pe_done, 1)
                    e.wait_ge(y_kept, n + 1)

                for j in range(2):
                    e.sem_inc(op_free[j], 1)
                with e.Fori(0, PAIRS) as pair:
                    with e.Fori(0, NT // 2) as h:
                        for j in range(2):
                            tile(pair * NT + h * 2 + j, j, pair, h * 2 + j, pair * (NT // 2) + h)
                    for q in range(2):
                        e.wait_ge(y_normed, pair + 1)
                        for t in range(4):
                            m = e.transpose(gb[q][:, t, :], y[:, 0, 4 * q + t, :], S.ident[:, :])
                        m.then_inc(yt_full, 1)

            @block.vector
            def _(e):
                e.wait_ge(par_in, 48)
                e.sem_inc(pu_free, 1)
                e.sem_inc(g_free, 2)

                def tile(n, j, pair, i, h):
                    for u in range(4):
                        d = u // 2
                        e.wait_ge(g_full, n * 4 + (u + 1))
                        if u == 0:
                            e.wait_ge(al_used, n + 1)
                        e.tensor_tensor(g[:, :, u, :], gb[u % 2][:, :, :], mask[:, d, :, :], ALU.mult).then_inc(g_kept, 1)
                        e.drain()
                        e.sem_inc(g_free, 1)
                    e.wait_ge(al_ready, n * LEVELS + 1)
                    for d in range(2):
                        m = e.tensor_tensor(th[:, d, 1, :, :], al[:, 0, 2 * d:2 * d + 2, :], bcast(S.ident[:, :], 2), ALU.add)
                    m.then_inc(h_ready, 1)
                    for l in range(1, LEVELS):
                        for d in range(2):
                            us = slice(2 * d, 2 * d + 2)
                            e.wait_ge(x_full, n * 10 + (2 * (l - 1) + d + 1))
                            e.tensor_tensor(xx[:, us, :], xb[d][:, 0:2, :], bcast(S.ident[:, :], 2), ALU.add).then_inc(x_kept, 1)
                        if l == LEVELS - 1:
                            for d in range(2):
                                e.wait_ge(th_full, n * 10 + (8 + d + 1))
                                e.tensor_copy(th[:, d, 1, :, :], thb[d][:, 2:4, :]).then_inc(hl_kept, 1)
                    e.wait_ge(pu_full, n + 1)
                    e.tensor_copy(pu[:, :, :], pub[:, :, :]).then_inc(pu_kept, 1)
                    e.wait_ge(m_full, n + 1)
                    for c in range(2):
                        m = e.tensor_tensor(mt[:, :, c, :], mnb[c][:, 0:2, 0:CH], bcast(eye2[:, :], 2), ALU.add)
                    m.then_inc(m_kept, 1)
                    e.wait_ge(n_kept, n + 1)
                    e.sem_inc(pu_free, 1)
                    e.wait_ge(q_full, n + 1)
                    for d in range(2):
                        m = e.tensor_tensor(qt[:, d, :], qb[:, d, :], op[j][d][:, OP_R, :], ALU.add)
                    m.then_inc(q_kept, 1)
                    for c in range(2):
                        e.wait_ge(c_full, n * 2 + (c + 1))
                        to = (sm[j], st[1 - j])[c]
                        for d in range(2):
                            cc = c if d == 0 else 1 - c
                            chunk = h * 4 + (2 * j + c) if d == 0 else h * -4 + (NCH - 1 - 2 * j - c)
                            m = e.scalar_tensor_tensor(out=to[:, d, :], in0=cb[c][:, d, 0:CH],
                                                       scalar=S.carry[:, ds(pair, 1), d, ds(chunk, 1)].rearrange("p a c -> p (a c)"),
                                                       in1=nn[:, d, cc, :], op0=ALU.mult, op1=ALU.add)
                        if c == 0:
                            m.then_inc(c_mid, 1)
                        else:
                            m.then_inc(c_ready, 1)

                def start(pair):
                    e.memset(st[0][:, :, :], 0.0).then_inc(c_ready, 1)
                    e.drain()

                def end(pair):
                    e.wait_ge(y_kept, pair * NT + NT)
                    yy = y[:, 0, :, :].rearrange("p t (h c) -> p (t h) c", c=CH)
                    e.tensor_tensor(y[:, 0, :, :], y[:, 0, :, :], y[:, 1, :, :], ALU.add)
                    e.drain()
                    e.tensor_reduce(stat[:, 0, :], yy, AX.X, ALU.add)
                    e.drain()
                    e.tensor_scalar(stat[:, 0, :], stat[:, 0, :], 1.0 / CH, None, ALU.mult)
                    e.drain()
                    e.tensor_tensor(yy, yy, stat[:, 0, :].unsqueeze(2).to_broadcast([P, 2 * NT, CH]), ALU.subtract)
                    e.drain()
                    sq = y[:, 1, :, :].rearrange("p t (h c) -> p (t h) c", c=CH)
                    e.tensor_tensor(sq, yy, yy, ALU.mult)
                    e.drain()
                    e.tensor_reduce(stat[:, 1, :], sq, AX.X, ALU.add)
                    e.drain()
                    e.tensor_scalar(stat[:, 1, :], stat[:, 1, :], 1.0 / CH, 64e-5, ALU.mult, ALU.add).then_inc(eps_ready, 1)
                    e.wait_ge(root_ready, pair + 1)
                    e.reciprocal(stat[:, 1, :], stat[:, 1, :])
                    e.drain()
                    e.tensor_tensor(yy, yy, stat[:, 1, :].unsqueeze(2).to_broadcast([P, 2 * NT, CH]), ALU.mult
                                    ).then_inc(y_normed, 1)
                    for q in range(2):
                        cut = slice(q * HALF, (q + 1) * HALF)
                        e.wait_ge(yt_full, pair * 2 + (q + 1))
                        t = y[:, 1, 4 * q:4 * q + 4, :].rearrange("p t c -> p (t c)")
                        e.tensor_tensor(t, gb[q][:, :, :].rearrange("p t c -> p (t c)"),
                                        S.proj[:, ds(pair + T_R, 1), cut].rearrange("p o c -> p (o c)"), ALU.mult)
                        e.drain()
                        m = S.mix[:, ds(pair + 2, 1), cut].rearrange("p o c -> p (o c)")
                        e.tensor_tensor(m, m, t, ALU.add)
                    e.drain()
                    e.sem_inc(pair_out, 1)

                with e.Fori(0, PAIRS) as pair:
                    start(pair)
                    with e.Fori(0, NT // 2) as h:
                        for j in range(2):
                            tile(pair * NT + h * 2 + j, j, pair, h * 2 + j, h)
                    end(pair)

            @block.scalar
            def _(e):
                e.sem_inc(y_free, 1)

                def tile(n, j, pair, i, h):
                    for d in range(2):
                        e.wait_ge(turned, n * 2 + (d + 1))
                        if d == 0:
                            e.wait_ge(y_free, n + 1)
                        e.activation(tm[:, d, :, :], trb[d][:, TM_B:, :], ACT.Copy).then_inc(tm_kept, 1)
                        e.activation(rv[:, 2 * d:2 * d + 2, 0:CH], trb[d][:, TM_A, :].rearrange("p (h c) -> p h c", h=2),
                                     ACT.Copy).then_inc(tm_kept, 1)
                    e.wait_ge(t_full, n + 1)
                    for d in range(2):
                        m = e.activation(th[:, d, 0, :, :], thb[d][:, 0:2, :], ACT.Copy)
                    m.then_inc(t_kept, 1)
                    e.wait_ge(akv_full, n + 1)
                    e.activation(rv[:, :, CH:P], akvb[:, :, 0:CH], ACT.Copy).then_inc(akv_kept, 1)
                    for l in range(1, LEVELS - 1):
                        for d in range(2):
                            e.wait_ge(th_full, n * 10 + (2 * (l - 1) + d + 1))
                            e.activation(th[:, d, :, :, :], thb[d][:, :, :].rearrange("p (x u) c -> p x u c", x=2), ACT.Copy
                                         ).then_inc(th_kept, 1)
                    e.wait_ge(m_kept, n + 1)
                    for d in range(2):
                        for c in range(2):
                            chunk = h * 4 + (2 * j + c) if d == 0 else h * -4 + (NCH - 1 - 2 * j - (1 - c))
                            m = e.activation(nn[:, d, c, :], mnb[c][:, d, CH:P], ACT.Copy,
                                             scale=S.carry[:, ds(pair, 1), d, ds(chunk, 1)].rearrange("p a c -> p (a c)"))
                    m.then_inc(n_kept, 1)
                    e.wait_ge(y_full, n + 1)
                    back = h * -2 + (c7 - j)
                    for d, at in ((0, h * 2 + j), (1, back)):
                        for k in range(2):
                            m = e.activation(y[:, d, ds(at, 1), k * CH:k * CH + CH].rearrange("p o c -> p (o c)"),
                                             yb[k][:, d, 0:CH], ACT.Copy)
                    m.then_inc(y_kept, 1)
                    e.wait_ge(y_kept, n + 1)
                    e.sem_inc(y_free, 1)

                with e.Fori(0, PAIRS) as pair:
                    with e.Fori(0, NT // 2) as h:
                        for j in range(2):
                            tile(pair * NT + h * 2 + j, j, pair, h * 2 + j, h)
                    e.wait_ge(eps_ready, pair + 1)
                    e.activation(stat[:, 1, :], stat[:, 1, :], ACT.Sqrt).then_inc(root_ready, 1)
                    e.wait_ge(pair_out, pair + 1)

            @block.gpsimd
            def _(e):
                e.memset(S.proj[:, T_HY, :], 0.0).then_inc(zeroed, 1)
                e.sem_inc(al_used, 1)
                with e.Fori(0, PAIRS) as pair:
                    with e.Fori(0, NT // 2) as h:
                        for j in range(2):
                            n = pair * NT + h * 2 + j
                            e.wait_ge(g_kept, n * 4 + 4)
                            for l in range(LEVELS):
                                e.tensor_tensor(al[:, l, :, :], g[:, G_AB, :, :], bcast(level[:, l, :], 4), ALU.mult
                                                ).then_inc(al_ready, 1)
                            e.wait_ge(pe_done, n + 1)
                            e.sem_inc(al_used, 1)


def clear_beyond(e, S, zero, done):
    e.dma_start(S.ys[EXPERTS:BLOCKS, :, :].rearrange("b p d -> p b d"), bcast(zero, OVER)).then_inc(done, 16)


GROUPS, PER_GROUP = 4, 8
EXPERTS = GROUPS * PER_GROUP
NL = GROUPS + EXPERTS
FF = 512
KF = FF // P
BLK = P
OVER = 2 * L // BLK - 1
BLOCKS = EXPERTS + OVER


def output_and_router(nc, A, S, sem):
    ctx = ExitStack()
    with ctx:
        sb = lambda n, s, t=F32: ctx.enter_context(nc.sbuf_tensor(n, s, t))
        ps = lambda n, s: ctx.enter_context(nc.psum_tensor(n, s, F32))
        wo = S.proj[:, 8:16, :]
        wr = sb("o_wr", [P, KD, NL])
        br = sb("o_br", [P, NL])
        gb = sb("o_g", [P, D])
        mixt = [S.proj[:, 16 + j, :].rearrange("p (k c) -> p k c", c=P) for j in range(2)]
        xin = [S.proj[:, 18 + j, :] for j in range(2)]
        h2 = [S.proj[:, 20 + j, :] for j in range(2)]
        h2t = [S.proj[:, 22 + j, :].rearrange("p (k c) -> p k c", c=P) for j in range(2)]
        junk = S.proj[:, 24, :]
        ss, rs = sb("o_ss", [P, 2]), sb("o_rs", [P, 2])
        acc = [[ps(f"o_acc{j}{h}", [P, HALF]) for h in range(2)] for j in range(2)]
        tp = [ps(f"o_tp{j}", [P, 4, P]) for j in range(2)]
        lg = ps("o_lg", [P, NL])
        par_in = sem("o_par_in")
        x_in = [sem(f"o_x_in{j}") for j in range(2)]
        x_free = sem("o_x_free")
        mix_ready, mix_used, acc_full, acc_free = (sem("o_mix_ready"), sem("o_mix_used"), sem("o_acc_full"),
                                                   sem("o_acc_free"))
        x2_ready, squares, mean_ready, root_ready = sem("o_x2"), sem("o_sq"), sem("o_mean"), sem("o_root")
        h2_ready, h2_stored, turned, kept = sem("o_h2"), [sem("o_h2_stored0", True), sem("o_h2_stored1", True)], sem("o_turned"), sem("o_kept")
        lg_full, lg_kept, h2_turned = sem("o_lg_full"), sem("o_lg_kept"), sem("o_h2_turned")
        with nc.Block() as block:
            @block.sync
            def _(e):
                e.dma_start(wo, A["w_out"]).then_inc(par_in, 16)
                e.dma_start(wr[:, :, :], A["w_router"]).then_inc(par_in, 16)
                e.dma_start(br[:, :], A["b_router"].to_broadcast([P, NL])).then_inc(par_in, 16)
                e.dma_start(gb[:, :], A["norm2_g"].to_broadcast([P, D])).then_inc(par_in, 16)
                for t in range(NT):
                    if t >= 2:
                        e.wait_ge(x2_ready, t - 1)
                    e.dma_start(xin[t % 2], A["x"][t * P:(t + 1) * P, :]).then_inc(x_in[t % 2], 16)
                for j in range(2):
                    e.wait_ge(h2_stored[j], 16 * NT // 2)

            @block.gpsimd
            def _(e):
                for t in range(NT):
                    if t >= 2:
                        e.wait_ge(mix_used, t - 1)
                    e.tensor_copy(mixt[t % 2], S.mix[:, :, t * P:(t + 1) * P]).then_inc(mix_ready, 1)
                    e.wait_ge(h2_ready, t + 1)
                    e.dma_start(S.h2d[t * P:(t + 1) * P, :], h2[t % 2]).then_inc(h2_stored[t % 2], 16)

            @block.tensor
            def _(e):
                e.wait_ge(par_in, 64)

                def project_tile(t):
                    b = t % 2
                    e.wait_ge(mix_ready, t + 1)
                    if t >= 2:
                        e.wait_ge(x2_ready, t - 1)
                    for h in range(2):
                        for k in range(KD):
                            m = e.matmul(acc[b][h][:, :], mixt[b][:, k, :], wo[:, k, h * HALF:(h + 1) * HALF],
                                         start=(k == 0), stop=(k == KD - 1))
                    m.then_inc(acc_full, 1)
                    e.wait_ge(acc_full, t + 1)
                    e.sem_inc(mix_used, 1)

                project_tile(0)
                for t in range(NT):
                    b = t % 2
                    if t + 1 < NT:
                        project_tile(t + 1)
                    e.wait_ge(h2_ready, t + 1)
                    if t >= 1:
                        e.wait_ge(kept, 2 * t)
                    for k in range(KD):
                        m = e.transpose(tp[k // 4][:, k % 4, :], h2[b][:, k * P:(k + 1) * P], S.ident[:, :])
                    m.then_inc(turned, 1)
                    e.wait_ge(turned, t + 1)
                    e.sem_inc(h2_turned, 1)
                    e.wait_ge(kept, 2 * t + 2)
                    if t >= 1:
                        e.wait_ge(lg_kept, t)
                    for k in range(KD):
                        m = e.matmul(lg[:, :], h2t[b][:, k, :], wr[:, k, :], start=(k == 0), stop=(k == KD - 1))
                    m.then_inc(lg_full, 1)

            @block.vector
            def _(e):
                e.wait_ge(par_in, 64)
                for t in range(NT):
                    b = t % 2
                    e.wait_ge(acc_full, t + 1)
                    e.wait_ge(x_in[b], 16 * (t // 2 + 1))
                    for h in range(2):
                        cut = slice(h * HALF, (h + 1) * HALF)
                        m = e.tensor_tensor(S.x2[:, t, cut], acc[b][h][:, :], xin[b][:, cut], ALU.add)
                    m.then_inc(x2_ready, 1)
                    e.wait_ge(squares, t + 1)
                    e.tensor_scalar(rs[:, b:b + 1], ss[:, b:b + 1], 1.0 / D, EPS, ALU.mult, ALU.add).then_inc(mean_ready, 1)
                    e.wait_ge(root_ready, t + 1)
                    e.reciprocal(rs[:, b:b + 1], rs[:, b:b + 1])
                    e.drain()
                    if t >= 2:
                        e.wait_ge(h2_stored[b], 16 * (t // 2))
                        e.wait_ge(h2_turned, t - 1)
                    e.scalar_tensor_tensor(out=h2[b], in0=S.x2[:, t, :], scalar=rs[:, b:b + 1], in1=gb[:, :],
                                           op0=ALU.mult, op1=ALU.mult).then_inc(h2_ready, 1)
                    e.wait_ge(turned, t + 1)
                    if t >= 2:
                        e.wait_ge(lg_full, t - 1)
                    e.tensor_copy(h2t[b][:, 0:4, :], tp[0][:, :, :]).then_inc(kept, 1)
                    e.wait_ge(lg_full, t + 1)
                    e.tensor_tensor(S.logits[:, t, :], lg[:, :], br[:, :], ALU.add).then_inc(lg_kept, 1)

            @block.scalar
            def _(e):
                for t in range(NT):
                    b = t % 2
                    e.wait_ge(x2_ready, t + 1)
                    e.drain()
                    e.activation(junk, S.x2[:, t, :], ACT.Square, accum_out=ss[:, b:b + 1]).then_inc(squares, 1)
                    e.wait_ge(mean_ready, t + 1)
                    e.activation(rs[:, b:b + 1], rs[:, b:b + 1], ACT.Sqrt).then_inc(root_ready, 1)
                    e.wait_ge(turned, t + 1)
                    if t >= 2:
                        e.wait_ge(lg_full, t - 1)
                    e.activation(h2t[b][:, 4:8, :], tp[1][:, :, :], ACT.Copy).then_inc(kept, 1)


def route(nc, A, S, sem):
    ctx = ExitStack()
    with ctx:
        sb = lambda n, s, t=F32: ctx.enter_context(nc.sbuf_tensor(n, s, t))
        ps = lambda n, s: ctx.enter_context(nc.psum_tensor(n, s, F32))
        G, E, Q = GROUPS, PER_GROUP, EXPERTS
        tri = sb("q_tri", [P, 2, P])
        down = sb("q_down", [P, E])
        far = sb("q_far", [P, Q])
        gm, ge, gsum = sb("q_gm", [P, NT]), sb("q_ge", [P, NT, G]), sb("q_gsum", [P, NT])
        og = sb("q_og", [P, NT, G])
        prod = sb("q_prod", [P, NT, Q])
        es, top, rank8 = sb("q_es", [P, NT, E]), sb("q_top", [P, 2, NT]), sb("q_rank8", [P, NT, E])
        oe = [sb(f"q_oe{k}", [P, NT, E]) for k in range(2)]
        eo = [sb(f"q_eo{k}", [P, NT, Q]) for k in range(2)]
        m = sb("q_m", [P, NT, Q])
        rank = sb("q_rank", [P, NT, Q])
        counts = sb("q_counts", [P, NT + 1, Q])
        extra, ends, starts = sb("q_extra", [P, Q]), sb("q_ends", [P, Q]), sb("q_starts", [P, Q])
        first = sb("q_first", [P, Q])
        slot, slot_o, is_over, eid = sb("q_slot", [P, NT]), sb("q_slot_o", [P, NT]), sb("q_is_over", [P, NT]), sb("q_eid", [P, NT])
        owner = sb("q_owner", [P, OVER])
        ids0 = sb("q_ids0", [P, BLOCKS], U32)
        token = sb("q_token", [P, NT], U32)
        idrow, idrowf = sb("q_idrow", [BLOCKS, P], U32), sb("q_idrowf", [BLOCKS, P])
        pr, pt, pi = ps("q_pr", [P, NT, Q]), ps("q_pt", [P, NT, Q]), ps("q_pi", [P, BLOCKS])
        par_in, zeroed, cleared = sem("q_par_in"), sem("q_zeroed"), sem("q_cleared")
        gexp, esub, eexp, m_ready, ranked = sem("q_gexp"), sem("q_esub"), sem("q_eexp"), sem("q_m"), sem("q_ranked")
        places, scattered, rows_in, rowf, turned = (sem("q_places"), sem("q_scattered", True), sem("q_rows_in"),
                                                    sem("q_rowf"), sem("q_turned"))
        gready, tokens = sem("q_gready"), sem("q_tokens")
        lo = S.logits
        el = lo[:, :, G:NL].rearrange("p t (g e) -> p t g e", g=G)
        with nc.Block() as block:
            @block.sync
            def _(e):
                e.dma_start(tri[:, :, :], A["rt_tri"]).then_inc(par_in, 16)
                e.dma_start(down[:, :], A["rt_down"].to_broadcast([P, E])).then_inc(par_in, 16)
                e.dma_start(far[:, :], A["rt_far"].to_broadcast([P, Q])).then_inc(par_in, 16)
                e.wait_ge(zeroed, 1)
                e.dma_start(S.tok.rearrange("(p b) o -> p (b o)", p=P), ids0[:, :]).then_inc(cleared, 16)
                e.wait_ge(scattered, 16 * 2 * NT)
                e.dma_start(idrow[:, :], S.tok.rearrange("(b p) o -> b (p o)", p=P)).then_inc(rows_in, 16)
                e.wait_ge(rows_in, 16)

            @block.gpsimd
            def _(e):
                e.memset(ids0[:, :], 0).then_inc(zeroed, 1)
                e.iota(token[:, :], [[P, NT]], base=0, channel_multiplier=1).then_inc(tokens, 1)
                e.wait_ge(tokens, 1)
                e.wait_ge(cleared, 16)
                e.wait_ge(places, 2)
                for t in range(NT):
                    for k in range(2):
                        e.indirect_dma_start(S.tok, bass.IndirectOffsetOnAxis(ap=S.place[:, t, k:k + 1], axis=0),
                                             token[:, t:t + 1], None).then_inc(scattered, 16)

            @block.tensor
            def _(e):
                e.wait_ge(par_in, 48)
                e.wait_ge(m_ready, 1)
                e.matmul(pr[:, :, :].rearrange("p t q -> p (t q)"), tri[:, 0, :], m[:, :, :].rearrange("p t q -> p (t q)"),
                         start=True, stop=True)
                e.matmul(pt[:, :, :].rearrange("p t q -> p (t q)"), tri[:, 1, :], m[:, :, :].rearrange("p t q -> p (t q)"),
                         start=True, stop=True).then_inc(ranked, 1)
                e.wait_ge(rowf, 1)
                e.transpose(pi[:, :], idrowf[:, :], S.ident[0:BLOCKS, 0:BLOCKS]).then_inc(turned, 1)

            @block.scalar
            def _(e):
                e.wait_ge(gready, 1)
                e.activation(ge[:, :, :], ge[:, :, :], ACT.Exp).then_inc(gexp, 1)
                e.wait_ge(esub, 1)
                e.activation(S.gate[:, :, 1], S.gate[:, :, 1], ACT.Exp).then_inc(eexp, 1)

            @block.vector
            def _(e):
                tt, sc = e.tensor_tensor, e.tensor_scalar
                d = e.drain
                e.wait_ge(par_in, 48)

                def first_max(out, val, best, n, tmp):
                    tt(out, val, best.unsqueeze(2).to_broadcast([P, NT, n]), ALU.is_equal)
                    d()
                    tt(out, out, bcast(down[:, 0:n], NT), ALU.mult)
                    d()
                    e.tensor_reduce(tmp, out, AX.X, ALU.max)
                    d()
                    tt(out, bcast(down[:, 0:n], NT), tmp.unsqueeze(2).to_broadcast([P, NT, n]), ALU.is_equal)
                    d()

                e.tensor_reduce(gm[:, :], lo[:, :, 0:G], AX.X, ALU.max)
                d()
                tt(ge[:, :, :], lo[:, :, 0:G], gm[:, :].unsqueeze(2).to_broadcast([P, NT, G]), ALU.subtract
                   ).then_inc(gready, 1)
                first_max(og[:, :, :], lo[:, :, 0:G], gm[:, :], G, gsum[:, :])
                tt(prod[:, :, :].rearrange("p t (g e) -> p t g e", g=G), el,
                   og[:, :, :].unsqueeze(3).to_broadcast([P, NT, G, E]), ALU.mult)
                d()
                e.tensor_reduce(es[:, :, :], prod[:, :, :].rearrange("p t (g e) -> p t e g", g=G), AX.X, ALU.add)
                d()
                for k in range(2):
                    e.tensor_reduce(top[:, k, :], es[:, :, :], AX.X, ALU.max)
                    d()
                    first_max(oe[k][:, :, :], es[:, :, :], top[:, k, :], E, gm[:, :])
                    if k == 0:
                        e.scalar_tensor_tensor(out=es[:, :, :], in0=oe[0][:, :, :], scalar=-3e38, in1=es[:, :, :],
                                               op0=ALU.mult, op1=ALU.add)
                        d()
                tt(S.gate[:, :, 1], top[:, 1, :], top[:, 0, :], ALU.subtract).then_inc(esub, 1)
                e.wait_ge(gexp, 1)
                e.tensor_reduce(gsum[:, :], ge[:, :, :], AX.X, ALU.add)
                e.wait_ge(eexp, 1)
                sc(gm[:, :], S.gate[:, :, 1], 1.0, None, ALU.add)
                d()
                tt(gsum[:, :], gsum[:, :], gm[:, :], ALU.mult)
                d()
                e.reciprocal(S.gate[:, :, 0], gsum[:, :])
                d()
                tt(S.gate[:, :, 1], S.gate[:, :, 1], S.gate[:, :, 0], ALU.mult)
                for k in range(2):
                    for g in range(G):
                        tt(eo[k][:, :, g * E:(g + 1) * E], oe[k][:, :, :],
                           og[:, :, g:g + 1].to_broadcast([P, NT, E]), ALU.mult)
                d()
                tt(m[:, :, :], eo[0][:, :, :], eo[1][:, :, :], ALU.add).then_inc(m_ready, 1)
                e.wait_ge(ranked, 1)
                e.memset(counts[:, 0, :], 0.0)
                d()
                for t in range(NT):
                    tt(counts[:, t + 1, :], counts[:, t, :], pt[:, t, :], ALU.add)
                    d()
                tt(rank[:, :, :], pr[:, :, :], counts[:, 0:NT, :], ALU.add)
                total = counts[:, NT, :]
                sc(extra[:, :], total, float(BLK), None, ALU.is_gt)
                for k in range(2, L // BLK):
                    sc(first[:, :], total, float(k * BLK), None, ALU.is_gt)
                    d()
                    tt(extra[:, :], extra[:, :], first[:, :], ALU.add)
                    d()
                e.memset(first[:, :], 1.0)
                d()
                e.tensor_tensor_scan(ends[:, :], first[:, :], extra[:, :], 0.0, ALU.mult, ALU.add)
                d()
                tt(starts[:, :], ends[:, :], extra[:, :], ALU.subtract)
                d()
                sc(starts[:, :], starts[:, :], float(BLK), float((EXPERTS - 1) * BLK), ALU.mult, ALU.add)
                sc(first[:, :], far[:, :], float(BLK), None, ALU.mult)
                d()
                for k in range(2):
                    def pick(out, what):
                        tt(prod[:, :, :], eo[k][:, :, :], what, ALU.mult)
                        d()
                        e.tensor_reduce(out, prod[:, :, :], AX.X, ALU.add)
                        d()
                    pick(slot[:, :], rank[:, :, :])
                    pick(eid[:, :], bcast(first[:, :], NT))
                    pick(slot_o[:, :], bcast(starts[:, :], NT))
                    sc(is_over[:, :], slot[:, :], float(BLK), None, ALU.is_ge)
                    tt(slot_o[:, :], slot_o[:, :], eid[:, :], ALU.subtract)
                    tt(slot[:, :], slot[:, :], eid[:, :], ALU.add)
                    d()
                    tt(slot_o[:, :], slot_o[:, :], is_over[:, :], ALU.mult)
                    d()
                    tt(slot[:, :], slot[:, :], slot_o[:, :], ALU.add)
                    d()
                    e.tensor_copy(S.place[:, :, k], slot[:, :]).then_inc(places, 1)
                for b in range(OVER):
                    sc(first[:, :], ends[:, :], float(b), None, ALU.is_le)
                    d()
                    e.tensor_reduce(owner[:, b:b + 1], first[:, :], AX.X, ALU.add)
                    d()
                sc(owner[:, :], owner[:, :], float(EXPERTS - 1), None, ALU.min)
                d()
                e.tensor_copy(S.over[:, 0:OVER], owner[:, :])
                e.tensor_copy(S.over[:, OVER:OVER + 1], ends[:, Q - 1:Q])
                e.wait_ge(rows_in, 16)
                e.tensor_copy(idrowf[:, :], idrow[:, :]).then_inc(rowf, 1)
                e.wait_ge(turned, 1)
                e.tensor_copy(S.ids[:, 0:BLOCKS], pi[:, :])


def experts(nc, A, S, sem):
    ctx = ExitStack()
    with ctx:
        sb = lambda n, s, t=F32: ctx.enter_context(nc.sbuf_tensor(n, s, t))
        ps = lambda n, s: ctx.enter_context(nc.psum_tensor(n, s, F32))
        flat = S.proj[:, 8:CT, :].rearrange("p c t -> p (c t)")
        cut = lambda a, n: flat[:, a * L:(a + n) * L]
        w1 = [cut(4 * j, 4).rearrange("p (k f) -> p k f", f=FF) for j in range(2)]
        w3 = [cut(8 + 4 * j, 4).rearrange("p (k f) -> p k f", f=FF) for j in range(2)]
        w2 = [S.mix[:, 4 * j:4 * j + 4, :].rearrange("p c t -> p (c t)").rearrange("p (k d) -> p k d", d=D) for j in range(2)]
        xg = [sb(f"e_xg{j}", [P, D]) for j in range(2)]
        idx = [sb(f"e_idx{j}", [P, 1], U32) for j in range(2)]
        xt = [sb(f"e_xt{j}", [P, KD, P]) for j in range(2)]
        act, at = sb("e_act", [P, FF]), sb("e_at", [P, KF, P])
        yo = [sb(f"e_yo{j}", [P, D]) for j in range(2)]
        tp = [ps(f"e_tp{j}", [P, 4, P]) for j in range(2)]
        ph = [ps(f"e_ph{j}", [P, FF]) for j in range(2)]
        pa = ps("e_pa", [P, KF, P])
        py = [ps(f"e_py{j}", [P, HALF]) for j in range(2)]
        stages = (sem("e_idx_ready"), [sem("e_x_in0", True), sem("e_x_in1", True)], [sem("e_w_in0"), sem("e_w_in1")],
                  sem("e_turned"), sem("e_kept"), sem("e_h_full"), sem("e_silu"), sem("e_act_ready"), sem("e_a_turned"),
                  sem("e_a_kept"), sem("e_y_full"), sem("e_y_kept"), [sem("e_stored0"), sem("e_stored1")],
                  sem("e_w_free"), sem("e_x_used"), sem("e_y_free"))
        (idx_ready, x_in, w_in, turned, kept, h_full, silu, act_ready, a_turned, a_kept, y_full, y_kept, stored,
         w_free, x_used, y_free) = stages
        NP = EXPERTS // 2
        stepped = sem("e_stepped")
        tp_free, ph_free, pa_free, passed = sem("e_tp_free"), sem("e_ph_free"), sem("e_pa_free"), sem("e_passed")
        yp_free = sem("e_yp_free")

        with nc.Block() as block:
            @block.sync
            def _(e):
                e.sem_inc(w_free, 2)
                with e.Fori(0, NP) as i:
                    for j in range(2):
                        e.wait_ge(w_free, i * 2 + (j + 1))
                        e.sem_inc(passed, 1)
                        for to, of in ((w1, "moe_w1"), (w3, "moe_w3"), (w2, "moe_w2")):
                            e.dma_start(to[j], A[of][ds(i * 2 + j, 1), :, :, :].rearrange("o p k c -> (o p) k c")
                                        ).then_inc(w_in[j], 16)

            @block.gpsimd
            def _(e):
                e.sem_inc(x_used, 2)

                def gather(j, b, n, half_n):
                    e.wait_ge(x_used, n + 1)
                    e.tensor_copy(idx[j][:, :], S.ids[:, ds(b, 1)]).then_inc(idx_ready, 1)
                    e.wait_ge(idx_ready, n + 1)
                    e.sem_inc(stepped, 1)
                    e.indirect_dma_start(xg[j][:, :], None, S.h2d,
                                         bass.IndirectOffsetOnAxis(ap=idx[j][:, :], axis=0)).then_inc(x_in[j], 16)
                with e.Fori(0, NP) as i:
                    for j in range(2):
                        gather(j, i * 2 + j, i * 2 + j, i)
                e.wait_ge(x_in[0], NP * 16)
                e.wait_ge(x_in[1], NP * 16)

            @block.tensor
            def _(e):
                def turn(j, n, half_n):
                    e.wait_ge(x_in[j], half_n * 16 + 16)
                    e.wait_ge(tp_free, n + 1)
                    for k in range(KD):
                        m = e.transpose(tp[k // 4][:, k % 4, :], xg[j][:, k:D:KD], S.ident[:, :])
                    m.then_inc(turned, 1)

                def mlp(j, n, half_n, after=None):
                    e.wait_ge(w_in[j], half_n * 48 + 48)
                    e.wait_ge(kept, n * 2 + 2)
                    e.wait_ge(ph_free, n + 1)
                    for s, w in ((0, w1[j]), (1, w3[j])):
                        for k in range(KD):
                            m = e.matmul(ph[s][:, :], xt[j][:, k, :], w[:, k, :], start=(k == 0), stop=(k == KD - 1))
                        m.then_inc(h_full, 1)
                    if after:
                        after()
                    e.wait_ge(act_ready, n + 1)
                    e.wait_ge(pa_free, n + 1)
                    for k in range(KF):
                        m = e.transpose(pa[:, k, :], act[:, k:FF:KF], S.ident[:, :])
                    m.then_inc(a_turned, 1)
                    e.wait_ge(a_kept, n + 1)
                    e.wait_ge(yp_free, n * 2 + 2)
                    for h in range(2):
                        for k in range(KF):
                            m = e.matmul(py[h][:, :], at[:, k, :], w2[j][:, k, h * HALF:(h + 1) * HALF],
                                         start=(k == 0), stop=(k == KF - 1))
                        m.then_inc(y_full, 1)
                    e.wait_ge(y_full, n * 2 + 2)
                    e.sem_inc(w_free, 1)

                turn(0, 0, 0)
                e.wait_ge(turned, 1)
                e.sem_inc(x_used, 1)
                with e.Fori(0, NP - 1) as i:
                    def next1():
                        turn(1, i * 2 + 1, i)
                        e.wait_ge(turned, i * 2 + 2)
                        e.sem_inc(x_used, 1)

                    def next0():
                        turn(0, i * 2 + 2, i + 1)
                        e.wait_ge(turned, i * 2 + 3)
                        e.sem_inc(x_used, 1)
                    mlp(0, i * 2, i, next1)
                    mlp(1, i * 2 + 1, i, next0)
                mlp(0, EXPERTS - 2, NP - 1, lambda: turn(1, EXPERTS - 1, NP - 1))
                mlp(1, EXPERTS - 1, NP - 1)

            @block.scalar
            def _(e):
                e.sem_inc(tp_free, 1)
                e.sem_inc(pa_free, 1)
                e.sem_inc(yp_free, 2)

                def keep_x(j, n):
                    e.wait_ge(turned, n + 1)
                    e.activation(xt[j][:, 0:4, :], tp[0][:, :, :], ACT.Copy).then_inc(kept, 1)
                    e.wait_ge(kept, n * 2 + 2)
                    e.sem_inc(tp_free, 1)

                def expert(j, n, half_n, last=False):
                    e.wait_ge(h_full, n * 2 + 1)
                    e.activation(act[:, :], ph[0][:, :], ACT.Silu).then_inc(silu, 1)
                    if not last:
                        keep_x(1 - j, n + 1)
                    e.wait_ge(a_turned, n + 1)
                    e.activation(at[:, :, :], pa[:, :, :], ACT.Copy).then_inc(a_kept, 1)
                    e.drain()
                    e.sem_inc(pa_free, 1)
                    e.wait_ge(y_full, n * 2 + 1)
                    e.wait_ge(stored[j], half_n * 16 + 16)
                    e.activation(yo[j][:, 0:HALF], py[0][:, :], ACT.Copy).then_inc(y_kept, 1)
                    e.wait_ge(y_kept, n * 2 + 2)
                    e.sem_inc(yp_free, 2)
                    e.dma_start(S.ys[ds(n, 1), :, :].rearrange("o p d -> (o p) d"), yo[j][:, :]).then_inc(stored[j], 16)
                e.sem_inc(stored[0], 16)
                e.sem_inc(stored[1], 16)
                keep_x(0, 0)
                with e.Fori(0, NP - 1) as i:
                    for j in range(2):
                        expert(j, i * 2 + j, i)
                expert(0, EXPERTS - 2, NP - 1)
                expert(1, EXPERTS - 1, NP - 1, True)
                for j in range(2):
                    e.wait_ge(stored[j], NP * 16 + 16)

            @block.vector
            def _(e):
                e.sem_inc(ph_free, 1)

                def keep_x(j, n):
                    e.wait_ge(turned, n + 1)
                    e.tensor_copy(xt[j][:, 4:8, :], tp[1][:, :, :]).then_inc(kept, 1)

                def expert(j, n, half_n, last=False):
                    e.wait_ge(h_full, n * 2 + 2)
                    e.wait_ge(silu, n + 1)
                    e.tensor_tensor(act[:, :], act[:, :], ph[1][:, :], ALU.mult).then_inc(act_ready, 1)
                    e.wait_ge(act_ready, n + 1)
                    e.sem_inc(ph_free, 1)
                    if not last:
                        keep_x(1 - j, n + 1)
                    e.wait_ge(y_full, n * 2 + 2)
                    e.wait_ge(stored[j], half_n * 16 + 16)
                    e.tensor_copy(yo[j][:, HALF:D], py[1][:, :]).then_inc(y_kept, 1)
                keep_x(0, 0)
                with e.Fori(0, NP - 1) as i:
                    for j in range(2):
                        expert(j, i * 2 + j, i)
                expert(0, EXPERTS - 2, NP - 1)
                expert(1, EXPERTS - 1, NP - 1, True)

        v = [sem(f"f_{n}", n == "x_in") for n in ("idx", "x_in", "w_in", "turned", "kept", "h_full", "silu", "act", "a_turned",
                                     "a_kept", "y_full", "y_kept", "stored")]
        f_idx, f_x, f_w, f_turned, f_kept, f_h, f_silu, f_act, f_at, f_ak, f_y, f_yk, f_st = v
        count_at, owner_at = S.over[0:1, OVER:OVER + 1], S.over

        def beyond(e, body):
            n = e.value_load(count_at, min_val=0, max_val=OVER)
            with e.If(n > 0):
                with e.Fori(0, OVER) as b:
                    body(b)

        with nc.Block() as block:
            @block.sync
            def _(e):
                def body(b):
                    e.wait_ge(f_st, b * 16 + 16)
                    e.sem_inc(passed, 1)
                    owner = e.value_load(owner_at[0:1, ds(b, 1)], min_val=0, max_val=EXPERTS - 1)
                    for to, of in ((w1, "moe_w1"), (w3, "moe_w3"), (w2, "moe_w2")):
                        e.dma_start(to[0], A[of][ds(owner, 1), :, :, :].rearrange("o p k c -> (o p) k c")).then_inc(f_w, 16)
                e.sem_inc(f_st, 16)
                beyond(e, body)

            @block.gpsimd
            def _(e):
                def body(b):
                    e.wait_ge(f_st, b * 16 + 16)
                    e.tensor_copy(idx[0][:, :], S.ids[:, ds(b + EXPERTS, 1)]).then_inc(f_idx, 1)
                    e.wait_ge(f_idx, b + 1)
                    e.sem_inc(stepped, 1)
                    e.indirect_dma_start(xg[0][:, :], None, S.h2d,
                                         bass.IndirectOffsetOnAxis(ap=idx[0][:, :], axis=0)).then_inc(f_x, 16)
                beyond(e, body)

            @block.tensor
            def _(e):
                def body(b):
                    e.wait_ge(f_x, b * 16 + 16)
                    for k in range(KD):
                        m = e.transpose(tp[k // 4][:, k % 4, :], xg[0][:, k:D:KD], S.ident[:, :])
                    m.then_inc(f_turned, 1)
                    e.wait_ge(f_w, b * 48 + 48)
                    e.wait_ge(f_kept, b + 1)
                    for s, w in ((0, w1[0]), (1, w3[0])):
                        for k in range(KD):
                            m = e.matmul(ph[s][:, :], xt[0][:, k, :], w[:, k, :], start=(k == 0), stop=(k == KD - 1))
                    m.then_inc(f_h, 1)
                    e.wait_ge(f_act, b + 1)
                    for k in range(KF):
                        m = e.transpose(pa[:, k, :], act[:, k:FF:KF], S.ident[:, :])
                    m.then_inc(f_at, 1)
                    e.wait_ge(f_ak, b + 1)
                    for h in range(2):
                        for k in range(KF):
                            m = e.matmul(py[h][:, :], at[:, k, :], w2[0][:, k, h * HALF:(h + 1) * HALF],
                                         start=(k == 0), stop=(k == KF - 1))
                    m.then_inc(f_y, 1)
                beyond(e, body)

            @block.vector
            def _(e):
                def body(b):
                    e.wait_ge(f_turned, b + 1)
                    e.tensor_copy(xt[0][:, 0:4, :], tp[0][:, :, :])
                    e.tensor_copy(xt[0][:, 4:8, :], tp[1][:, :, :]).then_inc(f_kept, 1)
                    e.wait_ge(f_silu, b + 1)
                    e.tensor_tensor(act[:, :], act[:, :], ph[1][:, :], ALU.mult).then_inc(f_act, 1)
                    e.wait_ge(f_at, b + 1)
                    e.tensor_copy(at[:, :, :], pa[:, :, :]).then_inc(f_ak, 1)
                    e.wait_ge(f_y, b + 1)
                    e.tensor_copy(yo[0][:, 0:HALF], py[0][:, :])
                    e.tensor_copy(yo[0][:, HALF:D], py[1][:, :]).then_inc(f_yk, 1)
                beyond(e, body)

            @block.scalar
            def _(e):
                def body(b):
                    e.wait_ge(f_h, b + 1)
                    e.activation(act[:, :], ph[0][:, :], ACT.Silu).then_inc(f_silu, 1)
                    e.wait_ge(f_yk, b + 1)
                    e.sem_inc(passed, 1)
                    e.dma_start(S.ys[ds(b + EXPERTS, 1), :, :].rearrange("o p d -> (o p) d"), yo[0][:, :]).then_inc(f_st, 16)
                    e.wait_ge(f_st, b * 16 + 32)
                beyond(e, body)


def combine(nc, A, S, sem, out):
    ctx = ExitStack()
    with ctx:
        sb = lambda n, s, t=F32: ctx.enter_context(nc.sbuf_tensor(n, s, t))
        gb = S.proj[:, 8, :]
        NB = 3
        ya = [[S.proj[:, 9 + 2 * j + k, :] for k in range(2)] for j in range(NB)]
        junk = S.proj[:, 16, :]
        ss, rs = sb("z_ss", [P, NT]), sb("z_rs", [P, NT])
        par_in, stored = sem("z_par_in"), sem("z_stored")
        y_in = [sem(f"z_y_in{j}", True) for j in range(NB)]
        summed, squares, mean_ready, root_ready, normed = (sem("z_summed"), sem("z_squares"), sem("z_mean"),
                                                           sem("z_root"), sem("z_normed"))
        with nc.Block() as block:
            @block.sync
            def _(e):
                e.dma_start(gb, A["norm_f_g"].to_broadcast([P, D])).then_inc(par_in, 16)
                for t in range(NT):
                    e.wait_ge(normed, t + 1)
                    e.dma_start(out[t * P:(t + 1) * P, :], S.x2[:, t, :]).then_inc(stored, 16)
                e.wait_ge(stored, 16 * NT)

            @block.gpsimd
            def _(e):
                for t in range(NT):
                    if t >= NB:
                        e.wait_ge(summed, 2 * (t - NB) + 2)
                    for k in range(2):
                        e.indirect_dma_start(ya[t % NB][k], None, S.ys.rearrange("b p d -> (b p) d"),
                                             bass.IndirectOffsetOnAxis(ap=S.place[:, t, k:k + 1], axis=0)
                                             ).then_inc(y_in[t % NB], 16)

            @block.vector
            def _(e):
                e.wait_ge(par_in, 16)

                def add(t):
                    e.wait_ge(y_in[t % NB], 32 * (t // NB + 1))
                    for k in range(2):
                        e.scalar_tensor_tensor(out=S.x2[:, t, :], in0=ya[t % NB][k], scalar=S.gate[:, t, k:k + 1],
                                               in1=S.x2[:, t, :], op0=ALU.mult, op1=ALU.add).then_inc(summed, 1)
                        e.wait_ge(summed, 2 * t + k + 1)
                add(0)
                for t in range(NT):
                    if t + 1 < NT:
                        add(t + 1)
                    e.wait_ge(squares, t + 1)
                    e.tensor_scalar(rs[:, t:t + 1], ss[:, t:t + 1], 1.0 / D, EPS, ALU.mult, ALU.add).then_inc(mean_ready, 1)
                    e.wait_ge(root_ready, t + 1)
                    e.reciprocal(rs[:, t:t + 1], rs[:, t:t + 1])
                    e.drain()
                    e.scalar_tensor_tensor(out=S.x2[:, t, :], in0=S.x2[:, t, :], scalar=rs[:, t:t + 1], in1=gb,
                                           op0=ALU.mult, op1=ALU.mult).then_inc(normed, 1)

            @block.scalar
            def _(e):
                for t in range(NT):
                    e.wait_ge(summed, 2 * t + 2)
                    e.drain()
                    e.activation(junk, S.x2[:, t, :], ACT.Square, accum_out=ss[:, t:t + 1]).then_inc(squares, 1)
                    e.wait_ge(mean_ready, t + 1)
                    e.activation(rs[:, t:t + 1], rs[:, t:t + 1], ACT.Sqrt).then_inc(root_ready, 1)


@contextmanager
def semaphores(nc, whole):
    with ExitStack() as ctx:
        used = []

        def sem(name, kept=False):
            s = (whole if kept else ctx).enter_context(nc.semaphore(name))
            if not kept:
                used.append(s)
            return s
        yield sem
        with nc.Block() as block:
            @block.sync
            def _(e):
                for s in used:
                    e.sem_clear(s)


def program(nc, A, out):
    ctx = ExitStack()
    with ctx:
        sb = lambda n, s, t=F32: ctx.enter_context(nc.sbuf_tensor(n, s, t))
        S = Memory()
        S.proj = sb("proj", [P, CT, L])
        S.mix = sb("mix", [P, KD, L])
        S.ident, S.ones = sb("ident", [P, P]), sb("ones", [P, 1])
        S.rpar = sb("rpar", [P, PAIRS, N_PAR])
        S.carry = sb("carry", [P, PAIRS, 2, NCH])
        S.logits, S.gate = sb("logits", [P, NT, NL]), sb("gate", [P, NT, 2])
        S.place = sb("place", [P, NT, 2], U32)
        S.ids = sb("ids", [P, BLOCKS + 1], U32)
        S.over = sb("over", [P, OVER + 1], I32)
        S.x2 = S.proj[:, 0:NT, :]
        dram = lambda n, s, t=F32: nc.dram_tensor(n, s, t, kind="Internal").ap()
        S.ops = dram("scan_operands", (PAIRS, 2, NT, P, N_OP, P))
        S.h2d = dram("h2_rows", (L, D))
        S.tok = dram("token_of_place", (BLOCKS * BLK, 1), U32)
        S.ys = dram("expert_rows", (BLOCKS, BLK, D))
        with semaphores(nc, ctx) as sem:
            project(nc, A, S, sem)
        with semaphores(nc, ctx) as sem:
            hyena(nc, A, S, sem)
        with semaphores(nc, ctx) as sem:
            rwkv_operands(nc, A, S, sem)
        with semaphores(nc, ctx) as sem:
            rwkv_scan(nc, A, S, sem)
        with semaphores(nc, ctx) as sem:
            attention(nc, A, S, sem)
        with semaphores(nc, ctx) as sem:
            output_and_router(nc, A, S, sem)
        with semaphores(nc, ctx) as sem:
            route(nc, A, S, sem)
        with semaphores(nc, ctx) as sem:
            experts(nc, A, S, sem)
        with semaphores(nc, ctx) as sem:
            combine(nc, A, S, sem, out)


def hyena_consts(I):
    L=1024; D=256
    o={}
    f4=np.float32
    t=np.linspace(0.0,1.0,L,dtype=f4)[:,None]
    w=(f4(2.0*math.pi/L)*np.arange(L,dtype=f4))[:,None]
    f=np.linspace(1e-4,15,16,dtype=f4)[None,:]
    z=np.concatenate([t,np.cos(f*w),-np.sin(f*w)],-1).astype(f4)
    o['hy_pos']=np.ascontiguousarray(z.T)
    for k in ('w1','w2','w3','wout'): o['hy_'+k]=I['hy_'+k][0]
    o['hy_fb']=np.stack([I['hy_b1'][0],I['hy_b2'][0],I['hy_b3'][0],I['hy_freq'][0]],1)
    dl=np.abs(np.linspace(math.log(1e-2)/1.5,math.log(1e-2)/0.3,D,dtype=f4))
    o['hy_decay']=np.exp(-t*dl).astype(f4)
    cw=I['hy_conv_w'][0]; 
    cv=np.concatenate([cw,I['hy_conv_b']],0)
    o['hy_conv']=np.ascontiguousarray(cv.reshape(4,6,128).transpose(2,1,0))
    o['hy_skip']=np.ascontiguousarray(I['hy_skip'][0].reshape(2,128).T)
    n=np.arange(L,dtype=np.float64)
    a=np.pi*np.outer(n,2*n+1)/2048
    b=np.pi*np.outer(2*n+1,2*n+1)/4096
    def cols(m):
        return m.reshape(2,8,128,8,128).transpose(3,2,0,1,4)
    o['hy_cu']=np.ascontiguousarray(cols(np.stack([np.cos(a),np.sin(a)]))).astype(f4)
    o['hy_cs']=np.ascontiguousarray(cols(np.stack([np.cos(b),np.sin(b)]))).astype(f4)
    o['hy_rows']=np.ascontiguousarray(np.stack([np.cos(b),np.sin(b)]).reshape(2,8,128,L).transpose(1,2,0,3)).astype(f4)
    return o
def na_consts(I):
    o={}
    rpb=I['na_rpb'][0]
    pad=np.zeros((4,15,127),np.float32); pad[:,:,48:79]=rpb
    b=np.stack([pad[:,:,63-q:127-q] for q in range(64)],1)
    o['na_bias']=np.ascontiguousarray(b.reshape(2,128,15,64).transpose(1,0,2,3))
    q=np.arange(64); st=np.clip(q-8,0,48); c=np.arange(64)
    band=np.where((c[None]>=st[:,None])&(c[None]<st[:,None]+16),0,-1e30).astype(np.float32)
    o['na_band']=np.concatenate([band,band],0)
    return o
def rw_consts(I):
    o={}
    L=1024
    mu=I['rw_mu'][0]
    rows=[mu[0,0],mu[0,1],mu[1,0],mu[1,1],mu[2,0],mu[2,1],I['rw_w0'][0,0],I['rw_w0'][0,1],I['rw_a0'][0,0],I['rw_a0'][0,1],
          I['rw_kk'][0],I['rw_ka'][0],I['rw_rk'][0].reshape(-1),I['rw_ln_w'][0],I['rw_ln_b'][0]]
    o['rw_par']=np.ascontiguousarray(np.stack(rows).reshape(15,4,128).transpose(2,1,0))
    lo=np.stack([I['rw_w2'][0].reshape(128,4,128),I['rw_a2'][0].reshape(128,4,128),I['rw_g2'][0].reshape(128,4,128)])
    o['rw_lora']=np.ascontiguousarray(lo.transpose(2,1,0,3))
    r=np.ones((128,L),np.float32); r[:,::64]=0
    o['rw_reset']=r
    o['rw_heads']=np.kron(np.eye(2),np.ones((64,64))).astype(np.float32)
    s=np.arange(128)[:,None]; t=np.arange(128)[None]
    same=(s//64==t//64)
    m=np.stack([np.stack([same&(s<t),same&(s<=t),same&(s<t),same&(s<=t)]),np.stack([same&(s>t),same&(s>=t),same&(s>t),same&(s>=t)])])
    o['rw_mask']=np.ascontiguousarray(m.transpose(2,0,1,3)).astype(np.float32)
    lv=np.stack([(s//(2*b)==t//(2*b))&(s//b!=t//b) for b in (1,2,4,8,16,32)])
    o['rw_level']=np.ascontiguousarray(lv.transpose(1,0,2)).astype(np.float32)
    o['rw_eye2']=np.concatenate([np.eye(64),np.eye(64)],0).astype(np.float32)
    return o
def moe_consts(I):
    o={}
    o['w_out']=np.ascontiguousarray(I['w_out'][0].reshape(8,128,1024).transpose(1,0,2))
    wr=np.concatenate([I['moe_wg'][0],I['moe_we'][0]],1)
    o['w_router']=np.ascontiguousarray(wr.reshape(8,128,36).transpose(1,0,2))
    o['b_router']=np.concatenate([I['moe_bg'],I['moe_be']],1)
    o['norm2_g']=I['norm2_g']; o['norm_f_g']=I['norm_f_g'][None]
    s=np.arange(128)[:,None]; t=np.arange(128)[None]
    o['rt_tri']=np.ascontiguousarray(np.stack([s<t,s<1e9+0*t],1)).astype(np.float32)
    o['rt_down']=np.arange(8,0,-1).astype(np.float32)[None]
    o['rt_far']=np.arange(32).astype(np.float32)[None]
    o['moe_w1']=I['moe_w1'][0].reshape(32,128,8,512); o['moe_w3']=I['moe_w3'][0].reshape(32,128,8,512)
    o['moe_w2']=I['moe_w2'][0].reshape(32,128,4,1024)
    return o


def kernel(**inputs):
    import concourse.bacc as bacc
    from concourse.bass_utils import run_bass_kernel_spmd

    I = {name: np.asarray(a) for name, a in inputs.items()}
    arrays = {"x": I["x"][0], "norm1_g": I["norm1_g"], "ident": np.eye(P, dtype=np.float32),
              "w_in": np.ascontiguousarray(I["w_in"][0].reshape(KD, P, CT, P).transpose(2, 1, 0, 3))}
    for part in (hyena_consts(I), na_consts(I), rw_consts(I), moe_consts(I)):
        arrays.update(part)
    arrays = {f"in_{name}": np.ascontiguousarray(a) for name, a in arrays.items()}
    nc = bacc.Bacc("TRN2", target_bir_lowering=False, num_devices=1)
    A = {name[3:]: nc.dram_tensor(name, a.shape, mybir.dt.from_np(a.dtype), kind="ExternalInput").ap()
         for name, a in arrays.items()}
    out = nc.dram_tensor("out_rows", (L, D), F32, kind="ExternalOutput").ap()
    program(nc, A, out)
    r = run_bass_kernel_spmd(nc, [arrays], core_ids=[0])
    return r.results[0]["out_rows"].reshape(1, L, D)
```

```python
import math

import numpy as np
import concourse.bass as bass
from concourse import mybir
from contextlib import ExitStack, contextmanager


class Memory:
    pass


F32 = mybir.dt.float32
F32R = mybir.dt.float32r
I32 = mybir.dt.int32
U32 = mybir.dt.uint32
ALU = mybir.AluOpType
ACT = mybir.ActivationFunctionType
AX = mybir.AxisListType
ds = bass.ds

P = 128
D = 1024
L = 1024
KD = D // P
NT = L // P
HALF = 512
HY_D, RW_D, NA_D = D // 4, D // 2, D // 4
IN_D = 3 * HY_D + 3 * RW_D + 128 + 128 + 128 + 3 * NA_D
CT = IN_D // P
T_HY, T_R, T_K, T_V = 0, 6, 10, 14
T_G, T_W, T_A, T_Q, T_NK, T_NV = 18, 19, 20, 21, 23, 25
EPS = 1e-6
TWO_PI = 2.0 * np.pi
ROUND = float(1.5 * 2 ** 23)
PI2_HI = 6.28125
PI2_LO = float(TWO_PI - 6.28125)


def bcast(ap, n, at=1):
    shape = list(ap.shape)
    shape.insert(at, n)
    return ap.unsqueeze(at).to_broadcast(shape)


def split_matmul(e, out, lhs, rhs, first, last):
    for n, (a, b) in enumerate(((0, 0), (0, 1), (1, 0))):
        m = e.matmul(out, lhs[a], rhs[b], start=first and n == 0, stop=last and n == 2)
    return m


def project(nc, A, S, sem):
    ctx = ExitStack()
    with ctx:
        sb = lambda n, s, t=F32: ctx.enter_context(nc.sbuf_tensor(n, s, t))
        ps = lambda n, s: ctx.enter_context(nc.psum_tensor(n, s, F32))
        xt = [S.proj[:, CT - 1 - j, :] for j in range(2)]
        junk, gb = S.proj[:, CT - 3, :], S.proj[:, CT - 4, :]
        ss = sb("a_ss", [P, 2])
        rs = sb("a_rs", [P, 2])
        wh, wl = ([sb(f"a_{n}{j}", [P, KD, P], F32R) for j in range(3)] for n in ("wh", "wl"))
        xh, xl = sb("a_xh", [P, KD, L], F32R), sb("a_xl", [P, KD, L], F32R)
        raw = lambda j, i: S.proj[:, ds(i * 3 + j, 1), :].rearrange("p o (k c) -> p (o k) c", c=P)
        bank = [ps(f"a_b{j}", [P, HALF]) for j in range(8)]
        pp = bank[0:6]
        tp = [[bank[b].rearrange("p (q c) -> p q c", q=4) for b in two] for two in ((6, 7), (0, 1))]
        x_in = [sem(f"x_in{j}") for j in range(2)]
        w_in = [sem(f"w_in{j}") for j in range(3)]
        g_in, x_free = sem("g_in"), sem("x_free")
        squares, mean_ready, root_ready = sem("squares"), sem("mean_ready"), sem("root_ready")
        x_normed, turned, x_high, x_low = sem("x_normed"), sem("turned"), sem("x_high"), sem("x_low")
        w_free, w_high, w_low, p_full = ([sem(f"{n}{j}") for j in range(3)] for n in ("w_free", "w_high", "w_low", "p_full"))
        p_free_v, p_free_a = sem("p_free_v"), sem("p_free_a")

        def steps(split, keep):
            split(0, 0)
            split(1, 0)

            def three(i, left=3):
                for j in range(3):
                    if j < left:
                        split((j + 2) % 3, i + (j + 2) // 3)
                    keep(j, i)
            return three

        with nc.Block() as block:
            @block.sync
            def _(e):
                e.dma_start(S.ident[:, :], A["ident"]).then_inc(g_in, 16)
                e.dma_start(gb, A["norm1_g"].to_broadcast([P, D])).then_inc(g_in, 16)
                for t in range(NT):
                    if t >= 2:
                        e.wait_ge(x_free, t - 1)
                    e.dma_start(xt[t % 2], A["x"][t * P:(t + 1) * P, :]).then_inc(x_in[t % 2], 16)
                with e.Fori(0, CT // 3) as i:
                    for j in range(3):
                        e.wait_ge(w_free[j], i + 1)
                        e.dma_start(raw(j, i), A["w_in"][ds(i * 3 + j, 1), :, :, :]
                                    .rearrange("o p k c -> (o p) k c")).then_inc(w_in[j], 16)

            @block.scalar
            def _(e):
                def high(t):
                    e.wait_ge(turned, t + 1)
                    for q in range(2):
                        m = e.activation(xh[:, 4 * q:4 * q + 4, t * P:(t + 1) * P], tp[t % 2][q], ACT.Copy)
                    m.then_inc(x_high, 1)

                for t in range(NT):
                    e.wait_ge(x_in[t % 2], 16 * (t // 2 + 1))
                    if t >= 1:
                        e.drain()
                    e.activation(junk, xt[t % 2], ACT.Square, accum_out=ss[:, t % 2:t % 2 + 1]).then_inc(squares, 1)
                    e.wait_ge(mean_ready, t + 1)
                    e.activation(rs[:, t % 2:t % 2 + 1], rs[:, t % 2:t % 2 + 1], ACT.Sqrt).then_inc(root_ready, 1)
                    if t >= 1:
                        high(t - 1)
                high(NT - 1)

                def split(j, i):
                    e.wait_ge(w_in[j], i * 16 + 16)
                    e.activation(wh[j][:, :, :], raw(j, i), ACT.Copy).then_inc(w_high[j], 1)

                def keep(j, i):
                    e.wait_ge(p_full[j], i + 1)
                    e.sem_inc(w_free[j], 1)
                    e.activation(S.proj[:, ds(i * 3 + j, 1), 0:HALF].rearrange("p o c -> p (o c)"),
                                 pp[2 * j][:, :], ACT.Copy).then_inc(p_free_a, 1)
                three = steps(split, keep)
                with e.Fori(0, CT // 3 - 1) as i:
                    three(i)
                three(CT // 3 - 1, 1)

            @block.vector
            def _(e):
                def low(t):
                    e.wait_ge(x_high, t + 1)
                    for q in range(2):
                        cut = (slice(None), slice(4 * q, 4 * q + 4), slice(t * P, (t + 1) * P))
                        m = e.tensor_tensor(xl[cut], tp[t % 2][q], xh[cut].bitcast(F32), ALU.subtract)
                    m.then_inc(x_low, 1)

                e.wait_ge(g_in, 32)
                for t in range(NT):
                    b = t % 2
                    e.wait_ge(squares, t + 1)
                    e.tensor_scalar(rs[:, b:b + 1], ss[:, b:b + 1], 1.0 / D, EPS, ALU.mult, ALU.add
                                    ).then_inc(mean_ready, 1)
                    e.wait_ge(root_ready, t + 1)
                    e.reciprocal(rs[:, b:b + 1], rs[:, b:b + 1])
                    e.drain()
                    e.scalar_tensor_tensor(out=xt[b], in0=xt[b], scalar=rs[:, b:b + 1],
                                           in1=gb, op0=ALU.mult, op1=ALU.mult).then_inc(x_normed, 1)
                    if t >= 1:
                        low(t - 1)
                low(NT - 1)

                def split(j, i):
                    e.wait_ge(w_high[j], i + 1)
                    e.tensor_tensor(wl[j][:, :, :], raw(j, i), wh[j][:, :, :].bitcast(F32), ALU.subtract
                                    ).then_inc(w_low[j], 1)

                def keep(j, i):
                    e.wait_ge(p_full[j], i + 1)
                    e.tensor_copy(S.proj[:, ds(i * 3 + j, 1), HALF:L].rearrange("p o c -> p (o c)"),
                                  pp[2 * j + 1][:, :]).then_inc(p_free_v, 1)
                three = steps(split, keep)
                with e.Fori(0, CT // 3 - 1) as i:
                    three(i)
                three(CT // 3 - 1, 1)

            @block.tensor
            def _(e):
                for j in range(3):
                    e.sem_inc(w_free[j], 1)
                for t in range(NT):
                    e.wait_ge(x_normed, t + 1)
                    if t >= 2:
                        e.wait_ge(x_low, t - 1)
                    for k in range(KD):
                        m = e.transpose(tp[t % 2][k // 4][:, k % 4, :], xt[t % 2][:, k * P:(k + 1) * P], S.ident[:, :])
                    m.then_inc(turned, 1)
                    e.wait_ge(turned, t + 1)
                    e.sem_inc(x_free, 1)
                e.wait_ge(x_low, NT)

                def tile(j, i):
                    e.wait_ge(w_low[j], i + 1)
                    for h in range(2):
                        cut = slice(h * HALF, (h + 1) * HALF)
                        for k in range(KD):
                            m = split_matmul(e, pp[2 * j + h][:, :], (wh[j][:, k, :], wl[j][:, k, :]),
                                             (xh[:, k, cut], xl[:, k, cut]), k == 0, k == KD - 1)
                    m.then_inc(p_full[j], 1)

                for j in range(3):
                    tile(j, 0)
                with e.Fori(1, CT // 3) as i:
                    for j in range(3):
                        e.wait_ge(p_free_a, i * 3 + (j - 2))
                        e.wait_ge(p_free_v, i * 3 + (j - 2))
                        tile(j, i)


HY_C = HY_D // P
FT = L // P


def hyena(nc, A, S, sem):
    ctx = ExitStack()
    with ctx:
        sb = lambda n, s, t=F32: ctx.enter_context(nc.sbuf_tensor(n, s, t))
        ps = lambda n, s: ctx.enter_context(nc.psum_tensor(n, s, F32))
        vec = sb("h_vec", [P, 6, 4])
        skip = sb("h_skip", [P, HY_C])
        ztok = sb("h_ztok", [P, NT, HY_D])
        fsum = sb("h_fsum", [P, NT, HY_D])
        fdif = sb("h_fdif", [P, NT, HY_D])
        norm = sb("h_norm", [P, HY_C])
        x0, zc = S.mix[:, 2:4, :], S.mix[:, 4:6, :]
        tmp1, tmp2 = S.mix[:, 6, :], S.mix[:, 7, :]
        par_in = sem("h_par_in")

        c1 = ExitStack()
        with c1:
            sb1 = lambda n, s, t=F32: c1.enter_context(nc.sbuf_tensor(n, s, t))
            ps1 = lambda n, s: c1.enter_context(nc.psum_tensor(n, s, F32))
            pos = sb1("h_pos", [33, L])
            w1, w2, w3 = sb1("h_w1", [33, 64]), sb1("h_w2", [64, 64]), sb1("h_w3", [64, 64])
            fb = sb1("h_fb", [64, 4])
            wout = sb1("h_wout", [64, 2 * HY_D])
            decay = sb1("h_decay", [P, NT, HY_D])
            act = sb1("h_act", [64, L])
            arg, turns = sb1("h_arg", [64, L]), sb1("h_turns", [64, L])
            fl = [sb1(f"h_fl{j}", [P, 2, HY_D]) for j in range(2)]
            sq = [sb1(f"h_sq{j}", [P, 2 * HY_D]) for j in range(2)]
            sqsum = sb1("h_sqsum", [P, 2 * HY_D])
            pm = ps1("h_pm", [P, 2, HALF])
            pf = [ps1(f"h_pf{j}", [P, 2 * HY_D]) for j in range(2)]
            pz = [ps1(f"h_pz{j}", [P, 4, P]) for j in range(2)]
            pn = ps1("h_pn", [P, HALF])
            layer, arg_ready, sine = sem("h_layer"), sem("h_arg_ready"), sem("h_sine")
            raw, windowed, squared, summed = sem("h_raw"), sem("h_windowed"), sem("h_squared"), sem("h_summed")
            scaled, convolved, z_ready = sem("h_scaled"), sem("h_convolved"), sem("h_z_ready")
            z_turned, z_kept = sem("h_z_turned"), sem("h_z_kept")
            norm_sum, norm_eps, norm_root = sem("h_norm_sum"), sem("h_norm_eps"), sem("h_norm_root")
            n_par = 9
            with nc.Block() as block:
                @block.sync
                def _(e):
                    for to, of in ((pos, "hy_pos"), (w1, "hy_w1"), (w2, "hy_w2"), (w3, "hy_w3"), (fb, "hy_fb"),
                                   (wout, "hy_wout")):
                        e.dma_start(to[:, :], A[of]).then_inc(par_in, 16)
                    e.dma_start(decay[:, :, :], A["hy_decay"].rearrange("(t p) c -> p t c", p=P)).then_inc(par_in, 16)
                    e.dma_start(vec[:, :, :], A["hy_conv"]).then_inc(par_in, 16)
                    e.dma_start(skip[:, :], A["hy_skip"]).then_inc(par_in, 16)

                @block.tensor
                def _(e):
                    e.wait_ge(par_in, 16 * n_par)
                    for n, w in enumerate((w1, w2, w3)):
                        src = pos if n == 0 else act
                        if n:
                            e.wait_ge(sine, n)
                        for h in range(2):
                            m = e.matmul(pm[0:64, h, :], w[:, :], src[:, h * HALF:(h + 1) * HALF],
                                         start=True, stop=True)
                        m.then_inc(layer, 1)
                    e.wait_ge(sine, 3)
                    for t in range(NT):
                        if t >= 2:
                            e.wait_ge(windowed, t - 1)
                        e.matmul(pf[t % 2][:, :], act[:, t * P:(t + 1) * P], wout[:, :],
                                 start=True, stop=True).then_inc(raw, 1)
                    e.wait_ge(z_ready, 2)
                    for n in range(2 * HY_C):
                        c, h = n // 2, n % 2
                        if n >= 2:
                            e.wait_ge(z_kept, n - 1)
                        for q in range(4):
                            t = 4 * h + q
                            m = e.transpose(pz[n % 2][:, q, :], zc[:, c, t * P:(t + 1) * P], S.ident[:, :])
                        m.then_inc(z_turned, 1)
                    e.wait_ge(summed, NT + 1)
                    for c in range(HY_C):
                        for d in range(2):
                            m = e.matmul(pn[:, c:c + 1], sqsum[:, d * HY_D + c * P:d * HY_D + (c + 1) * P],
                                         S.ones[:, 0:1], start=(d == 0), stop=(d == 1))
                    m.then_inc(norm_sum, 1)

                @block.vector
                def _(e):
                    e.wait_ge(par_in, 16 * n_par)
                    a, k = arg[:, :], turns[:, :]
                    for n in range(3):
                        e.wait_ge(layer, n + 1)
                        e.tensor_scalar(a, pm[0:64, :, :].rearrange("p h c -> p (h c)"), fb[:, n:n + 1], fb[:, 3:4],
                                        ALU.add, ALU.mult)
                        e.drain()
                        e.tensor_scalar(k, a, 1.0 / TWO_PI, ROUND, ALU.mult, ALU.add)
                        e.drain()
                        e.tensor_scalar(k, k, -ROUND, None, ALU.add)
                        e.drain()
                        e.scalar_tensor_tensor(out=a, in0=k, scalar=-PI2_HI, in1=a, op0=ALU.mult, op1=ALU.add)
                        e.drain()
                        e.scalar_tensor_tensor(out=a, in0=k, scalar=-PI2_LO, in1=a, op0=ALU.mult, op1=ALU.add)
                        e.drain()
                        e.tensor_scalar(a, a, float(np.float32(3.1415925)), -float(np.float32(3.1415925)),
                                        ALU.min, ALU.max).then_inc(arg_ready, 1)
                    for t in range(NT):
                        b = t % 2
                        e.wait_ge(raw, t + 1)
                        if t >= 2:
                            e.wait_ge(squared, t - 1)
                        e.tensor_tensor(fl[b][:, :, :], pf[b][:, :].rearrange("p (d c) -> p d c", d=2),
                                        bcast(decay[:, t, :], 2), ALU.mult).then_inc(windowed, 1)
                        e.drain()
                        e.tensor_tensor(fsum[:, t, :], fl[b][:, 0, :], fl[b][:, 1, :], ALU.add)
                        e.tensor_tensor(fdif[:, t, :], fl[b][:, 0, :], fl[b][:, 1, :], ALU.subtract)
                        e.drain()
                    for n, c in enumerate((0, 1, 2, 4, 3, 5)):
                        o = (x0[:, 0, :], x0[:, 1, :], tmp1, tmp2, tmp1, tmp2)[n]
                        u = S.proj[:, T_HY + c, :]
                        e.wait_ge(scaled, n + 1)
                        e.scalar_tensor_tensor(out=o[:, 1:L], in0=u[:, 0:L - 1], scalar=vec[:, c, 0:1], in1=o[:, 1:L],
                                               op0=ALU.mult, op1=ALU.add)
                        e.drain()
                        e.scalar_tensor_tensor(out=o[:, 0:L - 1], in0=u[:, 1:L], scalar=vec[:, c, 2:3],
                                               in1=o[:, 0:L - 1], op0=ALU.mult, op1=ALU.add).then_inc(convolved, 1)
                        e.drain()
                        if n in (3, 5):
                            e.tensor_tensor(zc[:, (n - 3) // 2, :], tmp1, tmp2, ALU.mult).then_inc(z_ready, 1)
                            e.drain()
                    for n in range(2 * HY_C):
                        c, h = n // 2, n % 2
                        e.wait_ge(z_turned, n + 1)
                        e.tensor_copy(ztok[:, 4 * h:4 * h + 4, c * P:(c + 1) * P], pz[n % 2][:, :, :]).then_inc(z_kept, 1)
                    e.wait_ge(norm_sum, 1)
                    e.tensor_scalar(norm[:, :], pn[:, 0:HY_C], 1e-6, None, ALU.add).then_inc(norm_eps, 1)
                    e.wait_ge(norm_root, 1)
                    e.reciprocal(norm[:, :], norm[:, :])
                    e.drain()
                    e.tensor_scalar(norm[:, :], norm[:, :], 1.0 / L, None, ALU.mult)

                @block.scalar
                def _(e):
                    e.wait_ge(par_in, 16 * n_par)
                    for n in range(3):
                        e.wait_ge(arg_ready, n + 1)
                        e.activation(act[:, :], arg[:, :], ACT.Sin).then_inc(sine, 1)
                    for t in range(NT):
                        e.wait_ge(windowed, t + 1)
                        if t >= 2:
                            e.wait_ge(summed, t)
                        e.activation(sq[t % 2][:, :], fl[t % 2][:, :, :].rearrange("p d c -> p (d c)"),
                                     ACT.Square).then_inc(squared, 1)
                    for n, c in enumerate((0, 1, 2, 4, 3, 5)):
                        o = (x0[:, 0, :], x0[:, 1, :], tmp1, tmp2, tmp1, tmp2)[n]
                        if n >= 4:
                            e.wait_ge(z_ready, 1)
                        e.activation(o, S.proj[:, T_HY + c, :], ACT.Identity, bias=vec[:, c, 3:4],
                                     scale=vec[:, c, 1:2]).then_inc(scaled, 1)
                    e.wait_ge(norm_eps, 1)
                    e.activation(norm[:, :], norm[:, :], ACT.Sqrt).then_inc(norm_root, 1)

                @block.gpsimd
                def _(e):
                    e.memset(S.ones[:, :], 1.0)
                    e.memset(sqsum[:, :], 0.0).then_inc(summed, 1)
                    for t in range(NT):
                        e.wait_ge(squared, t + 1)
                        e.wait_ge(summed, t + 1)
                        e.tensor_tensor(sqsum[:, :], sqsum[:, :], sq[t % 2][:, :], ALU.add).then_inc(summed, 1)

        cu = [sb(f"h_cu{j}", [P, 2, NT, P]) for j in range(2)]
        cs = [sb(f"h_cs{j}", [P, 2, NT, P]) for j in range(2)]
        part = lambda c, a, b: S.proj[:, T_HY + c, a * HY_D:b * HY_D].rearrange("p (n c) -> p n c", c=HY_D)
        rows = S.proj[:, T_HY:T_HY + 2, :]
        kf = part(4, 0, 2)
        zk = part(3, 0, 2)
        pr = part(2, 0, 4)
        yf = part(3, 2, 4)
        pk = ps("h_pk", [P, 2, HY_D])
        pzf = ps("h_pzf", [P, 2, HY_D])
        py = [ps(f"h_py{j}", [P, HALF]) for j in range(4)]
        cu_in, cs_in = [sem(f"h_cu_in{j}") for j in range(2)], [sem(f"h_cs_in{j}") for j in range(2)]
        rows_in, rows_free = sem("h_rows_in"), sem("h_rows_free")
        k_full, z_full, k_kept, z_kept2 = sem("h_k_full"), sem("h_z_full"), sem("h_k_kept"), sem("h_z_kept2")
        y_ready, y_used, y_free, k_free = sem("h_y_ready"), sem("h_y_used"), sem("h_y_free"), sem("h_k_free")
        with nc.Block() as block:
            @block.sync
            def _(e):
                def load(f, j, of):
                    e.dma_start(cu[j][:, :, :, :], A["hy_cu"][of, :, :, :, :].rearrange("o p s n f -> (o p) s n f")
                                ).then_inc(cu_in[j], 16)
                    e.dma_start(cs[j][:, :, :, :], A["hy_cs"][of, :, :, :, :].rearrange("o p s n f -> (o p) s n f")
                                ).then_inc(cs_in[j], 16)

                def load_rows(of):
                    e.dma_start(rows[:, :, :], A["hy_rows"][of, :, :, :].rearrange("o p s t -> (o p) s t")
                                ).then_inc(rows_in, 16)
                load(0, 0, slice(0, 1))
                load(1, 1, slice(1, 2))
                load_rows(slice(0, 1))
                with e.Fori(1, FT // 2) as i:
                    for j in range(2):
                        e.wait_ge(z_full, i * 2 + (j - 1))
                        load(None, j, ds(i * 2 + j, 1))
                        e.wait_ge(y_used, i * 2 + (j - 1))
                        load_rows(ds(i * 2 + (j - 1), 1))
                e.wait_ge(y_used, FT - 1)
                load_rows(slice(FT - 1, FT))

            @block.tensor
            def _(e):
                def tile(j, i, first, last):
                    e.wait_ge(cu_in[j], i * 16 + 16)
                    if not first:
                        e.wait_ge(k_kept, i * 2 + j)
                    for s, f in ((0, fsum), (1, fdif)):
                        for n in range(NT):
                            m = e.matmul(pk[:, s, :], cu[j][:, s, n, :], f[:, n, :], start=(n == 0), stop=(n == NT - 1))
                    m.then_inc(k_full, 1)
                    e.wait_ge(cs_in[j], i * 16 + 16)
                    if not first:
                        e.wait_ge(z_kept2, i * 2 + j)
                    for s in range(2):
                        for n in range(NT):
                            m = e.matmul(pzf[:, s, :], cs[j][:, s, n, :], ztok[:, n, :], start=(n == 0), stop=(n == NT - 1))
                    m.then_inc(z_full, 1)
                    e.wait_ge(rows_in, i * 32 + (16 * j + 16))
                    e.wait_ge(y_ready, i * 2 + (j + 1))
                    for c in range(HY_C):
                        for h in range(2):
                            for s in range(2):
                                m = e.matmul(py[2 * c + h][:, :], yf[:, s, c * P:(c + 1) * P],
                                             rows[:, s, h * HALF:(h + 1) * HALF],
                                             start=first and s == 0, stop=last and s == 1, skip_group_check=True)
                    m.then_inc(y_used, 1)
                    e.wait_ge(y_used, i * 2 + (j + 1))
                    e.sem_inc(y_free, 1)
                tile(0, 0, True, False)
                tile(1, 0, False, False)
                with e.Fori(1, FT // 2 - 1) as i:
                    tile(0, i, False, False)
                    tile(1, i, False, False)
                tile(0, FT // 2 - 1, False, False)
                tile(1, FT // 2 - 1, False, True)

            @block.scalar
            def _(e):
                with e.Fori(0, FT) as i:
                    e.wait_ge(k_full, i + 1)
                    e.wait_ge(k_free, i + 1)
                    e.activation(kf[:, :, :], pk[:, :, :], ACT.Copy).then_inc(k_kept, 1)

            @block.vector
            def _(e):
                e.sem_inc(k_free, 1)
                e.sem_inc(y_free, 1)
                with e.Fori(0, FT) as i:
                    e.wait_ge(z_full, i + 1)
                    e.wait_ge(k_kept, i + 1)
                    k = kf
                    e.tensor_copy(zk[:, :, :], pzf[:, :, :]).then_inc(z_kept2, 1)
                    e.drain()
                    e.tensor_tensor(pr[:, 0:2, :], zk[:, :, :], k[:, :, :], ALU.mult)
                    e.tensor_tensor(pr[:, 2, :], zk[:, 0, :], k[:, 1, :], ALU.mult)
                    e.tensor_tensor(pr[:, 3, :], zk[:, 1, :], k[:, 0, :], ALU.mult)
                    e.drain()
                    e.sem_inc(k_free, 1)
                    e.wait_ge(y_free, i + 1)
                    e.tensor_tensor(yf[:, 0, :], pr[:, 0, :], pr[:, 1, :], ALU.subtract)
                    e.tensor_tensor(yf[:, 1, :], pr[:, 2, :], pr[:, 3, :], ALU.add).then_inc(y_ready, 1)
                    e.drain()
                e.wait_ge(y_used, FT)
                for c in range(HY_C):
                    e.tensor_scalar(zc[:, c, :], zc[:, c, :], skip[:, c:c + 1], None, ALU.mult)
                e.drain()
                for c in range(HY_C):
                    for h in range(2):
                        cut = slice(h * HALF, (h + 1) * HALF)
                        e.scalar_tensor_tensor(out=zc[:, c, cut], in0=py[2 * c + h][:, :], scalar=norm[:, c:c + 1],
                                               in1=zc[:, c, cut], op0=ALU.mult, op1=ALU.add)
                e.drain()
                for c in range(HY_C):
                    e.tensor_tensor(S.mix[:, c, :], zc[:, c, :], x0[:, c, :], ALU.mult)


HD = 64
ROWS = L // HD
KR = 8
NPAIR = NA_D // P
NB_T = 6


def attention(nc, A, S, sem):
    ctx = ExitStack()
    with ctx:
        sb = lambda n, s, t=F32: ctx.enter_context(nc.sbuf_tensor(n, s, t))
        ps = lambda n, s: ctx.enter_context(nc.psum_tensor(n, s, F32))
        bias = sb("n_bias", [P, NPAIR, 2 * KR - 1, HD])
        band = sb("n_band", [P, HD])
        vt = sb("n_vt", [P, ROWS - 1, NA_D])
        qd = [sb(f"n_qd{p}", [P, P]) for p in range(NPAIR)]
        sc = [sb(f"n_sc{p}", [P, HALF]) for p in range(NPAIR)]
        pt = [sb(f"n_pt{p}", [P, 4, P]) for p in range(NPAIR)]
        od = [sb(f"n_od{p}", [P, P]) for p in range(NPAIR)]
        top = sb("n_top", [P, NPAIR])
        tot = sb("n_tot", [P, NPAIR])
        inv = sb("n_inv", [P, NPAIR])
        s_ps = [ps(f"n_s{p}", [P, HALF]) for p in range(NPAIR)]
        t_ps = [ps(f"n_t{p}", [P, 4, P]) for p in range(NPAIR)]
        o_ps = [ps(f"n_o{p}", [P, P]) for p in range(NPAIR)]
        f_ps = [ps(f"n_f{p}", [P, P]) for p in range(NPAIR)]
        each = lambda name: [sem(f"{name}{p}") for p in range(NPAIR)]
        par_in, bias_ready, v_turned, v_kept = sem("n_par_in"), sem("n_bias_ready"), sem("n_v_turned"), sem("n_v_kept")
        zeroed = sem("n_zeroed")
        q_ready, s_full, top_ready, exps = each("n_q_ready"), each("n_s_full"), each("n_top_ready"), each("n_exps")
        p_turned, p_kept, o_full, o_kept = each("n_p_turned"), each("n_p_kept"), each("n_o_full"), each("n_o_kept")
        f_full, f_kept = each("n_f_full"), each("n_f_kept")
        MID, END = KR // 2, ROWS - KR // 2

        def rows(e, spans, body):
            for lo, hi, at in spans:
                with e.Fori(lo, hi) as r:
                    body(r, at(r))

        with nc.Block() as block:
            @block.sync
            def _(e):
                e.dma_start(bias[:, :, :, :], A["na_bias"]).then_inc(par_in, 16)
                e.dma_start(band[:, :], A["na_band"]).then_inc(par_in, 16)

            @block.gpsimd
            def _(e):
                for p in range(NPAIR):
                    e.memset(qd[p][:, :], 0.0)
                    e.memset(od[p][:, :], 0.0).then_inc(zeroed, 1)
                e.wait_ge(par_in, 32)
                for p in range(NPAIR):
                    e.tensor_tensor(bias[:, p, :, :], bias[:, p, :, :], bcast(band[:, :], 2 * KR - 1), ALU.add
                                    ).then_inc(bias_ready, 1)
                e.drain()
                with e.Fori(0, ROWS) as r:
                    for p in range(NPAIR):
                        e.wait_ge(s_full[p], r + 1)
                        q = S.proj[:, T_Q + p, ds(r * HD, HD)]
                        e.tensor_copy(qd[p][0:HD, 0:HD], q[0:HD, :])
                        e.drain()
                        e.tensor_copy(qd[p][HD:P, HD:P], q[HD:P, :]).then_inc(q_ready[p], 1)

            @block.tensor
            def _(e):
                for s in range(0, ROWS - 1):
                    if s >= 2:
                        e.wait_ge(v_kept, s - 1)
                    for p in range(NPAIR):
                        m = e.transpose(t_ps[s % 2][:, p, :], S.proj[:, T_NV + p, s * HD:s * HD + P], S.ident[:, :])
                    m.then_inc(v_turned, 1)
                e.wait_ge(v_kept, ROWS - 1)

                def scores(p, n, s):
                    e.wait_ge(q_ready[p], n + 1)
                    e.matmul(s_ps[p][:, :], qd[p][:, :], S.proj[:, T_NK + p, ds(s * HD, KR * HD)],
                             start=True, stop=True).then_inc(s_full[p], 1)

                def row(r, s, next_s):
                    for p in range(NPAIR):
                        e.wait_ge(exps[p], r + 1)
                        for c in range(4):
                            m = e.transpose(t_ps[p][:, c, :], sc[p][:, c * P:(c + 1) * P], S.ident[:, :])
                        m.then_inc(p_turned[p], 1)
                    if next_s is not None:
                        for p in range(NPAIR):
                            scores(p, r + 1, next_s)
                    for p in range(NPAIR):
                        e.wait_ge(p_kept[p], r + 1)
                        for c in range(4):
                            m = e.matmul(o_ps[p][:, :], pt[p][:, c, :],
                                         vt[:, ds(s + 2 * c, 1), p * P:p * P + P].rearrange("p o c -> p (o c)"),
                                         start=(c == 0), stop=(c == 3))
                        m.then_inc(o_full[p], 1)
                    for p in range(NPAIR):
                        e.wait_ge(o_kept[p], r + 1)
                        e.transpose(f_ps[p][:, :], od[p][:, :], S.ident[:, :]).then_inc(f_full[p], 1)

                for p in range(NPAIR):
                    e.sem_inc(s_full[p], 1)
                for p in range(NPAIR):
                    scores(p, 0, 0)
                rows(e, ((0, MID, lambda r: (0, 0)), (MID, END, lambda r: (r - MID, r + (1 - MID))),
                         (END, ROWS - 1, lambda r: (ROWS - KR, ROWS - KR))), lambda r, at: row(r, *at))
                row(ROWS - 1, ROWS - KR, None)

            @block.vector
            def _(e):
                for s in range(0, ROWS - 1):
                    e.wait_ge(v_turned, s + 1)
                    e.tensor_copy(vt[:, s, :].rearrange("p (a c) -> p a c", a=NPAIR), t_ps[s % 2][:, 0:NPAIR, :]
                                  ).then_inc(v_kept, 1)
                e.wait_ge(bias_ready, NPAIR)
                e.wait_ge(zeroed, NPAIR)

                def biased(n, drow):
                    for p in range(NPAIR):
                        e.wait_ge(s_full[p], n + 2)
                        e.scalar_tensor_tensor(out=sc[p][:, :], in0=s_ps[p][:, :], scalar=HD ** -0.5,
                                               in1=bias[:, p, ds(drow, KR), :].rearrange("p a c -> p (a c)"),
                                               op0=ALU.mult, op1=ALU.add)
                        e.drain()
                        e.tensor_reduce(top[:, p:p + 1], sc[p][:, :], AX.X, ALU.max, negate=True).then_inc(top_ready[p], 1)

                def totals(r):
                    e.drain()
                    for p in range(NPAIR):
                        e.wait_ge(exps[p], r + 1)
                        e.reciprocal(inv[:, p:p + 1], tot[:, p:p + 1])

                def outputs(r):
                    e.drain()
                    for p in range(NPAIR):
                        e.wait_ge(o_full[p], r + 1)
                        e.tensor_scalar(od[p][0:HD, 0:HD], o_ps[p][0:HD, 0:HD], inv[0:HD, p:p + 1], None, ALU.mult)
                        e.tensor_scalar(od[p][HD:P, HD:P], o_ps[p][HD:P, HD:P], inv[HD:P, p:p + 1], None, ALU.mult
                                        ).then_inc(o_kept[p], 1)
                    for p in range(NPAIR):
                        e.wait_ge(f_full[p], r + 1)
                        for h in (slice(0, HD), slice(HD, P)):
                            m = e.tensor_copy(S.mix[h, NB_T + p, ds(r * HD, HD)], f_ps[p][h, h])
                        m.then_inc(f_kept[p], 1)

                def row(r, next_drow):
                    totals(r)
                    biased(r + 1, next_drow)
                    outputs(r)

                biased(0, KR - 1)
                rows(e, ((0, MID, lambda r: r * -1 + (KR - 2)), (MID, END - 1, lambda r: MID - 1),
                         (END - 1, ROWS - 1, lambda r: r * -1 + (ROWS - 2))), row)
                totals(ROWS - 1)
                outputs(ROWS - 1)

            @block.scalar
            def _(e):
                with e.Fori(0, ROWS) as r:
                    for p in range(NPAIR):
                        e.wait_ge(top_ready[p], r + 1)
                        e.activation(sc[p][:, :], sc[p][:, :], ACT.Exp, bias=top[:, p:p + 1],
                                     accum_out=tot[:, p:p + 1]).then_inc(exps[p], 1)
                    for p in range(NPAIR):
                        e.wait_ge(p_turned[p], r + 1)
                        e.activation(pt[p][:, :, :], t_ps[p][:, :, :], ACT.Copy).then_inc(p_kept[p], 1)


PAIRS = RW_D // P
CH = 64
NCH = L // CH
DECAY_C = float(np.exp(-0.5))
MU_R, MU_K, MU_V, W0, A0, C_KK, C_KA, C_RK, C_LNW, C_LNB, C_MID, C_KA1, N_PAR = 0, 2, 4, 6, 8, 10, 11, 12, 13, 14, 15, 18, 19
OP_A, OP_R, OP_B, OP_K, OP_V, N_OP = 0, 1, 2, 3, 4, 5


def rwkv_operands(nc, A, S, sem):
    ctx = ExitStack()
    with ctx:
        sb = lambda n, s, t=F32: ctx.enter_context(nc.sbuf_tensor(n, s, t))
        ps = lambda n, s: ctx.enter_context(nc.psum_tensor(n, s, F32))
        own = [sb(f"r_t{j}", [P, L]) for j in range(10)]
        old = [S.proj[:, T_HY + j, :] for j in range(6)] + [S.proj[:, T_Q + j, :] for j in range(2)]
        rr, kk, vv, kn, *rest = [t[:, :] for t in own]
        a2, x2, kd2 = rest[0:2], rest[2:4], rest[4:6]
        sg2, ep2, en2, ea2 = old[0:2], old[2:4], old[4:6], old[6:8]
        lw = sb("r_lw", [P, 3, P])
        reset = sb("r_reset", [P, L])
        heads = sb("r_heads", [P, P])
        half = sb("r_half", [P, 2, NCH])
        zp = [ps(f"r_z{j}", [P, 2, HALF]) for j in range(4)]
        flat = lambda t: t[:, :, :].rearrange("p h c -> p (h c)")
        par = S.rpar
        par_in, ready0, lora, mid0 = sem("r_par_in"), sem("r_ready0"), sem("r_lora_in"), sem("r_mid0")
        passed = sem("r_passed")
        mid, shifted, sig, sq_done, ssq_done = sem("r_mid"), sem("r_shifted"), sem("r_sig"), sem("r_sq"), sem("r_ssq")
        z_full, kmax, kroot, kn_done = sem("r_z_full"), sem("r_kmax"), sem("r_kroot"), sem("r_kn")
        x_done, xd_done, e_done, k_done = sem("r_x"), sem("r_xd"), sem("r_e"), sem("r_kdir")
        pb_done, bon_full, gate_full, gate_done = sem("r_pb"), sem("r_bon"), sem("r_gate_full"), sem("r_gate")
        ops_done, pool_done, stored, pair_free, rest_done = (sem("r_ops"), sem("r_pool"), sem("r_stored"),
                                                             sem("r_pair_free"), sem("r_rest"))
        pcol = lambda pair, c: par[:, ds(pair, 1), c:c + 1].rearrange("p o c -> p (o c)")
        src = lambda pair, t: S.proj[:, ds(pair + t, 1), :].rearrange("p o c -> p (o c)")
        with nc.Block() as block:
            @block.sync
            def _(e):
                e.dma_start(par[:, :, 0:C_MID], A["rw_par"]).then_inc(par_in, 16)
                e.dma_start(reset[:, :], A["rw_reset"]).then_inc(par_in, 16)
                e.dma_start(heads[:, :], A["rw_heads"]).then_inc(par_in, 16)
                with e.Fori(0, PAIRS) as p:
                    e.wait_ge(pair_free, p + 1)
                    e.dma_start(lw[:, :, :], A["rw_lora"][ds(p, 1), :, :, :].rearrange("o p s c -> (o p) s c")
                                ).then_inc(lora, 16)

                    def store(d, slot, of):
                        e.sem_inc(passed, 1)
                        e.dma_start(S.ops[ds(p, 1), d, :, :, slot, :].rearrange("o t p c -> (o p) t c"),
                                    of.rearrange("p (t c) -> p t c", c=P)).then_inc(stored, 16)
                    e.wait_ge(shifted, p * 3 + 3)
                    for d in range(2):
                        store(d, OP_V, vv)
                    for d in range(2):
                        e.wait_ge(ops_done, p * 4 + (2 * d + 1))
                        store(d, OP_A, ea2[d])
                        e.wait_ge(ops_done, p * 4 + (2 * d + 2))
                        store(d, OP_B, a2[d])
                        e.wait_ge(pool_done, p * 4 + (2 * d + 1))
                        store(d, OP_R, ep2[d])
                        e.wait_ge(pool_done, p * 4 + (2 * d + 2))
                        store(d, OP_K, en2[d])
                    e.wait_ge(stored, p * 160 + 160)
                    e.wait_ge(rest_done, p + 1)
                    e.sem_inc(pair_free, 1)

            @block.tensor
            def _(e):
                e.wait_ge(ready0, 2)
                with e.Fori(0, PAIRS) as p:
                    e.wait_ge(lora, p * 16 + 16)
                    for s, t in ((0, T_W), (1, T_A)):
                        for d in range(2):
                            r = slice(d * 64, d * 64 + 64)
                            for h in range(2):
                                m = e.matmul(zp[2 * s + d][:, h, :], lw[r, s, :], S.proj[r, t, h * HALF:(h + 1) * HALF],
                                             start=True, stop=True)
                            m.then_inc(z_full, 1)
                    e.wait_ge(sig, p * 4 + 2)
                    e.wait_ge(sq_done, p + 1)
                    for h in range(2):
                        m = e.matmul(zp[0][:, h, :], heads[:, :], kd2[0][:, h * HALF:(h + 1) * HALF], start=True, stop=True)
                    m.then_inc(ssq_done, 1)
                    for h in range(2):
                        m = e.matmul(zp[1][:, h, :], lw[:, 2, :], S.proj[:, T_G, h * HALF:(h + 1) * HALF],
                                     start=True, stop=True)
                    m.then_inc(gate_full, 1)
                    e.wait_ge(sig, p * 4 + 4)
                    e.wait_ge(pb_done, p + 1)
                    for h in range(2):
                        m = e.matmul(zp[2][:, h, :], heads[:, :], x2[0][:, h * HALF:(h + 1) * HALF], start=True, stop=True)
                    m.then_inc(bon_full, 1)

            @block.scalar
            def _(e):
                e.wait_ge(par_in, 48)
                e.activation(S.proj[:, T_W, :], S.proj[:, T_W, :], ACT.Tanh).then_inc(ready0, 1)
                e.activation(S.proj[:, T_G, :], S.proj[:, T_G, :], ACT.Sigmoid).then_inc(ready0, 1)
                e.wait_ge(mid0, 1)
                with e.Fori(0, PAIRS) as p:
                    e.wait_ge(pair_free, p + 1)
                    for n, (o, t) in enumerate(((rr, T_R), (kk, T_K), (vv, T_V))):
                        e.activation(o, src(p, t), ACT.Identity, scale=pcol(p, C_MID + n)).then_inc(mid, 1)
                    for s in range(2):
                        for d in range(2):
                            e.wait_ge(z_full, p * 4 + (2 * s + d + 1))
                            e.activation((sg2, a2)[s][d], flat(zp[2 * s + d]), ACT.Sigmoid,
                                         bias=pcol(p, (W0, A0)[s] + d)).then_inc(sig, 1)
                    e.wait_ge(shifted, p * 3 + 2)
                    e.activation(kd2[0], kk, ACT.Square, scale=pcol(p, C_KK)).then_inc(sq_done, 1)
                    e.wait_ge(kmax, p + 1)
                    e.activation(kn, kn, ACT.Sqrt).then_inc(kroot, 1)
                    for d in range(2):
                        e.wait_ge(x_done, p * 2 + (d + 1))
                        e.wait_ge(xd_done, p * 2 + (d + 1))
                        c = DECAY_C
                        if d == 0:
                            e.activation(ep2[0], x2[0], ACT.Exp, scale=-c)
                            e.activation(en2[0], x2[0], ACT.Exp, scale=c)
                            e.activation(ea2[0], sg2[0], ACT.Exp, scale=-c).then_inc(e_done, 1)
                        else:
                            e.activation(ep2[1], sg2[1], ACT.Exp, scale=-c)
                            e.activation(en2[1], sg2[1], ACT.Exp, scale=c)
                            e.activation(ea2[1], x2[1], ACT.Exp, scale=c).then_inc(e_done, 1)
                    e.drain()
                    e.wait_ge(gate_full, p + 1)
                    e.activation(x2[1], flat(zp[1]), ACT.Copy).then_inc(gate_done, 1)
                e.wait_ge(rest_done, PAIRS)
                e.activation(S.carry[:, :, :, :], S.carry[:, :, :, :], ACT.Exp, scale=-DECAY_C)

            @block.gpsimd
            def _(e):
                with e.Fori(0, PAIRS) as p:
                    e.wait_ge(shifted, p * 3 + 3)
                    for d in range(2):
                        e.wait_ge(e_done, p * 2 + (d + 1))
                        e.tensor_tensor(ep2[d], ep2[d], rr, ALU.mult).then_inc(pool_done, 1)
                        e.drain()
                        e.wait_ge(k_done, p * 2 + (d + 1))
                        e.wait_ge(ops_done, p * 4 + (2 * d + 2))
                        e.tensor_tensor(en2[d], en2[d], kd2[d], ALU.mult).then_inc(pool_done, 1)
                        e.drain()

            @block.vector
            def _(e):
                e.wait_ge(par_in, 48)
                e.memset(S.carry[:, :, :, :], 0.0)
                for n in range(3):
                    e.tensor_tensor(par[:, :, C_MID + n], par[:, :, 2 * n], par[:, :, 2 * n + 1], ALU.add)
                e.drain()
                e.tensor_scalar(par[:, :, C_MID:C_MID + 3], par[:, :, C_MID:C_MID + 3], -1.0, 1.0, ALU.mult, ALU.add)
                e.tensor_scalar(par[:, :, C_KA1], par[:, :, C_KA], -1.0, 1.0, ALU.mult, ALU.add)
                e.drain()
                e.sem_inc(mid0, 1)
                e.sem_inc(pair_free, 1)
                with e.Fori(0, PAIRS) as p:
                    for n, (o, t, c) in enumerate(((rr, T_R, MU_R), (kk, T_K, MU_K), (vv, T_V, MU_V))):
                        u = S.proj[:, ds(p + t, 1), :]
                        at = lambda a, b: u[:, :, a:b].rearrange("p o c -> p (o c)")
                        e.wait_ge(mid, p * 3 + (n + 1))
                        e.scalar_tensor_tensor(out=o[:, 1:L], in0=at(0, L - 1), scalar=pcol(p, c), in1=o[:, 1:L],
                                               op0=ALU.mult, op1=ALU.add)
                        e.drain()
                        e.scalar_tensor_tensor(out=o[:, 0:L - 1], in0=at(1, L), scalar=pcol(p, c + 1),
                                               in1=o[:, 0:L - 1], op0=ALU.mult, op1=ALU.add).then_inc(shifted, 1)
                    for d in range(2):
                        x = x2[d]
                        e.wait_ge(sig, p * 4 + (d + 1))
                        e.tensor_tensor_scan(x, reset[:, :], sg2[d], 0.0, ALU.mult, ALU.add)
                        e.drain()
                        xc = x.rearrange("p (n c) -> p n c", c=CH)
                        e.tensor_scalar(half[:, d, :], xc[:, :, CH - 1], 0.5, None, ALU.mult)
                        e.drain()
                        e.tensor_tensor(xc, xc, half[:, d, :].unsqueeze(2).to_broadcast([P, NCH, CH]), ALU.subtract
                                        ).then_inc(x_done, 1)
                        e.drain()
                        if d == 0:
                            e.tensor_tensor(sg2[0], x, sg2[0], ALU.subtract).then_inc(xd_done, 1)
                        else:
                            e.tensor_tensor(sg2[1], sg2[1], x, ALU.subtract).then_inc(xd_done, 1)
                        a, b = (half[:, d, 0:NCH - 1], half[:, d, 1:NCH])
                        to = S.carry[:, ds(p, 1), d, d:NCH - 1 + d].rearrange("p o c -> p (o c)")
                        e.tensor_tensor(to, a, b, ALU.add)
                    e.wait_ge(ssq_done, p + 1)
                    e.tensor_scalar(kn, flat(zp[0]), 1e-24, None, ALU.max).then_inc(kmax, 1)
                    for d in range(2):
                        if d == 0:
                            e.wait_ge(sig, p * 4 + 4)
                        e.tensor_scalar(kd2[d], a2[d], pcol(p, C_KA), pcol(p, C_KA1), ALU.mult, ALU.add)
                        e.drain()
                        e.tensor_tensor(kd2[d], kd2[d], kk, ALU.mult).then_inc(k_done, 1)
                    e.wait_ge(kroot, p + 1)
                    e.reciprocal(kn, kn)
                    e.drain()
                    e.scalar_tensor_tensor(out=kn, in0=kk, scalar=pcol(p, C_KK), in1=kn, op0=ALU.mult, op1=ALU.mult)
                    e.drain()
                    for d in range(2):
                        e.tensor_tensor(a2[d], a2[d], kn, ALU.mult)
                        e.wait_ge(e_done, p * 2 + (d + 1))
                        e.scalar_tensor_tensor(out=ea2[d], in0=kn, scalar=-1.0, in1=ea2[d], op0=ALU.mult, op1=ALU.mult
                                               ).then_inc(ops_done, 1)
                        e.drain()
                        e.tensor_tensor(a2[d], a2[d], en2[d], ALU.mult).then_inc(ops_done, 1)
                    e.tensor_tensor(x2[0], kd2[0], kd2[1], ALU.add)
                    e.drain()
                    e.scalar_tensor_tensor(out=x2[0], in0=x2[0], scalar=pcol(p, C_RK), in1=rr, op0=ALU.mult, op1=ALU.mult
                                           ).then_inc(pb_done, 1)
                    e.wait_ge(gate_done, p + 1)
                    e.wait_ge(bon_full, p + 1)
                    out = S.mix[:, ds(p + 2, 1), :].rearrange("p o c -> p (o c)")
                    e.tensor_tensor(out, flat(zp[2]), vv, ALU.mult)
                    e.drain()
                    e.scalar_tensor_tensor(out=out, in0=out, scalar=pcol(p, C_LNB), in1=x2[1], op0=ALU.add, op1=ALU.mult)
                    e.tensor_scalar(src(p, T_R), x2[1], pcol(p, C_LNW), None, ALU.mult)
                    e.drain()
                    e.sem_inc(rest_done, 1)


LEVELS = 6
TILES = PAIRS * NT
OF_B, OF_K, BY_A, BY_R = 0, 1, 0, 1


def rwkv_scan(nc, A, S, sem):
    ctx = ExitStack()
    with ctx:
        sb = lambda n, s, t=F32: ctx.enter_context(nc.sbuf_tensor(n, s, t))
        ps = lambda n, s: ctx.enter_context(nc.psum_tensor(n, s, F32))
        room = lambda t, n: S.proj[:, t:t + n, :].rearrange("p t c -> p (t c)")
        n_op, n_ar, n_g = 2 * N_OP * P, 2 * 2 * 2 * P, 2 * 4 * 2 * P
        op = [room(1, 5)[:, j * n_op:(j + 1) * n_op].rearrange("p (d s c) -> p d s c", d=2, s=N_OP) for j in range(2)]
        ar = [room(1, 5)[:, 2 * n_op + j * n_ar:2 * n_op + (j + 1) * n_ar]
              .rearrange("p (d h q c) -> p d h q c", d=2, h=2, q=2) for j in range(2)]
        y = room(T_K, 8).rearrange("p (d n c) -> p d n c", d=2, n=TILES)
        g = [room(T_G + 2 * j, 2).rearrange("p (k u q c) -> p k u q c", k=2, u=4, q=2) for j in range(2)]
        al = room(T_G + 4, 3).rearrange("p (l u c) -> p l u c", l=LEVELS, u=4)
        mask = sb("s_mask", [P, 2, 4, P])
        level = sb("s_level", [P, LEVELS, P])
        heads = sb("s_heads", [P, P])
        carry = sb("s_carry", [P, 2, TILES * 2])
        h1, t1 = sb("s_h1", [P, 4, P]), sb("s_t1", [P, 4, P])
        th, xx = sb("s_th", [P, 2, 2, 2, P]), sb("s_xx", [P, 4, P])
        hf = sb("s_hf", [P, 4, P])
        bk = [sb(f"s_bk{j}", [P, 2, 2, 2, P]) for j in range(2)]
        rv = [sb(f"s_rv{j}", [P, 2, 2, 2, CH]) for j in range(2)]
        vp = [sb(f"s_vp{j}", [P, 2, 2, 2, CH]) for j in range(2)]
        r2 = [sb(f"s_r2{j}", [P, 2, P]) for j in range(2)]
        pp, up = sb("s_pp", [P, 2, P]), sb("s_up", [P, 2, 2, 2, CH])
        qt, mt = sb("s_qt", [P, 2, P]), sb("s_mt", [P, 2, 2, P])
        st = [sb(f"s_st{j}", [P, 2, P]) for j in range(2)]
        mid = sb("s_mid", [P, 2, P])
        stat = sb("s_stat", [P, 2, 2, 2 * NT])
        xb = [ps(f"s_x{d}", [P, 4, P]) for d in range(2)]
        thb = [ps(f"s_thb{d}", [P, 4, P]) for d in range(2)]
        w = [ps(f"s_w{k}", [P, 4, P]) for k in range(4)]
        pub = w[0][:, :, :].rearrange("p (d x) (h c) -> p d x h c", d=2, h=2)
        mb, gb, tb = w[0], (w[0], w[2]), w[0]
        yb, qb, akvb, nb = w[1], w[2], w[2], w[3]
        trb = (w[3], w[1])
        hs = [slice(0, CH), slice(CH, P)]
        pad = lambda t, d, h: t[:, d, :, :, :].rearrange("p h x c -> p (h x c)")[:, h * CH:h * CH + P]
        tt = lambda u: th[:, u // 2, 0, u % 2, :]
        hh = lambda u: th[:, u // 2, 1, u % 2, :]
        par_in = sem("s_par_in")
        zeroed = sem("s_zeroed")
        with nc.Block() as block:
            @block.sync
            def _(e):
                e.dma_start(mask[:, :, :, :], A["rw_mask"]).then_inc(par_in, 16)
                e.dma_start(level[:, :, :], A["rw_level"]).then_inc(par_in, 16)
                e.dma_start(heads[:, :], A["rw_heads"]).then_inc(par_in, 16)
                e.wait_ge(par_in, 48)

            @block.gpsimd
            def _(e):
                for j in range(2):
                    e.memset(ar[j].rearrange("p d h q c -> p (d h q c)"), 0.0)
                    e.memset(bk[j][:, :, :, :, :], 0.0)
                    e.memset(vp[j][:, :, :, :, :], 0.0)
                e.memset(S.proj[:, T_HY, :], 0.0)

            @block.vector
            def _(e):
                e.memset(up[:, :, :, :, :], 0.0)
                e.memset(mt[:, :, :, :], 0.0)
                e.memset(st[0][:, :, :], 0.0)
                cv = carry[:, :, :].rearrange("p d (a c) -> p d a c", c=NCH)
                for c in range(NCH):
                    e.tensor_copy(cv[:, 0, :, c], S.carry[:, :, 0, c])
                    e.tensor_copy(cv[:, 1, :, c], S.carry[:, :, 1, NCH - 1 - c])
                e.drain()
                e.memset(cv[:, :, :, NCH - 1], 0.0)

        op_in = [sem(f"s_op_in{j}") for j in range(2)]
        op_free, passed, cleared = sem("s_op_free"), sem("s_passed"), sem("s_cleared")
        g_full, g_kept, turned, tm_kept = sem("s_g_full"), sem("s_g_kept"), sem("s_turned"), sem("s_tm_kept")
        h1_ready, al_ready, t1_full, t1_kept = sem("s_h1_ready"), sem("s_al_ready"), sem("s_t1_full"), sem("s_t1_kept")
        x_full, x_kept, th_full, th_kept = sem("s_x_full"), sem("s_x_kept"), sem("s_th_full"), sem("s_th_kept")
        hf_kept, akv_full, akv_kept = sem("s_hf_kept"), sem("s_akv_full"), sem("s_akv_kept")
        pu_full, pu_kept, m_full, m_kept = sem("s_pu_full"), sem("s_pu_kept"), sem("s_m_full"), sem("s_m_kept")
        q_full, q_kept, c_full, c_kept = sem("s_q_full"), sem("s_q_kept"), sem("s_c_full"), sem("s_c_kept")
        y_full, y_kept = sem("s_y_full"), sem("s_y_kept")

        def tiles(e, first, body, last):
            first((0, 0, 0))
            body((0, 0, 0), None, (1, 1, 0))
            with e.Fori(0, TILES // 2 - 1) as h:
                body((h * 2 + 1, 1, h), (h * 2, 0, h), (h * 2 + 2, 0, h + 1))
                body((h * 2 + 2, 0, h + 1), (h * 2 + 1, 1, h), (h * 2 + 3, 1, h + 1))
            n = TILES - 1
            body((n, 1, n // 2), (n - 1, 0, n // 2), None)
            last((n, 1, n // 2))

        with nc.Block() as block:
            @block.sync
            def _(e):
                with e.Fori(0, PAIRS) as pair:
                    with e.Fori(0, NT // 2) as h:
                        for j in range(2):
                            e.wait_ge(op_free, pair * NT + h * 2 + (j + 1))
                            e.sem_inc(passed, 1)
                            for d in range(2):
                                t = h * 2 + j if d == 0 else h * -2 + (NT - 1 - j)
                                src = S.ops[ds(pair, 1), d, ds(t, 1), :, :, :].rearrange("o u p s c -> (o u p) s c")
                                e.dma_start(op[j][:, d, :, :], src).then_inc(op_in[j], 16)
                                for k in range(2):
                                    e.dma_start(ar[j][hs[k], d, k, :, :], src[hs[k], OP_A:OP_R + 1, :]
                                                ).then_inc(op_in[j], 16)
                clear_beyond(e, S, S.proj[:, T_HY, :], cleared)
                e.wait_ge(cleared, 16)

            @block.tensor
            def _(e):
                mm = e.matmul

                def inverse_applied(m, j):
                    e.wait_ge(hf_kept, m * 2 + 2)
                    e.wait_ge(akv_kept, m + 1)
                    for u in range(4):
                        d, h = u // 2, u % 2
                        i = mm(pub[:, d, :, h, :], hf[:, u, :], rv[j][:, d, :, h, :], start=True, stop=True)
                    i.then_inc(pu_full, 1)
                    for u in range(4):
                        d, h = u // 2, u % 2
                        mm(yb[:, d, :], g[j][:, OF_K, u, BY_R, :], pad(vp[j], d, h), start=(u == 0), stop=False,
                           skip_group_check=True)

                def chunk_maps(m, j):
                    e.wait_ge(pu_kept, m + 1)
                    for d in range(2):
                        for c in range(2):
                            i = mm(mb[:, 2 * d + c, :], pp[:, d, :], bk[j][:, c, d, OF_B, :], start=True, stop=True)
                    i.then_inc(m_full, 1)
                    for d in range(2):
                        for h in range(2):
                            i = mm(qb[hs[h], d, :], pp[:, d, h * CH:h * CH + CH], g[j][:, OF_B, 2 * d + h, BY_R, :],
                                   start=True, stop=True)
                    i.then_inc(q_full, 1)

                def chunk_sums(m, j):
                    for d in range(2):
                        for c in range(2):
                            o = nb[:, 2 * d + c, :]
                            mm(o, bk[j][:, c, d, OF_B, :], up[:, d, :, 0, :], start=(d + c == 0), stop=False, skip_group_check=True)
                            mm(o, bk[j][:, c, d, OF_K, :], vp[j][:, d, :, 0, :], start=False, stop=False,
                               skip_group_check=True)

                def states(m, j, c):
                    if c == 0:
                        e.wait_ge(m_kept, m + 1)
                    e.wait_ge(c_kept, m * 2 + (c + 1))
                    for d in range(2):
                        k = c if d == 0 else 1 - c
                        i = mm(nb[:, 2 * d + k, :], mt[:, d, k, :], (st[j], mid)[c][:, d, :], start=False, stop=True,
                               skip_group_check=True)
                    i.then_inc(c_full, 1)

                def outputs_by_u(m, j):
                    for u in range(4):
                        d, h = u // 2, u % 2
                        mm(yb[:, d, :], g[j][:, OF_B, u, BY_R, :], pad(up, d, h), start=False, stop=False,
                           skip_group_check=True)

                def outputs_by_state(m, j):
                    e.wait_ge(q_kept, m + 1)
                    for d in range(2):
                        for c in range(2):
                            s0 = (st[j], mid)[c if d == 0 else 1 - c]
                            i = mm(yb[hs[c], d, :], qt[:, d, c * CH:c * CH + CH], s0[:, d, :], start=False, stop=True,
                                   skip_group_check=True)
                    i.then_inc(y_full, 1)

                def products(f, j, half, d, back):
                    if d == 0:
                        e.wait_ge(op_in[j], half * 96 + 96)
                        if back is not None:
                            e.wait_ge(q_kept, back[0] + 1)
                    else:
                        e.wait_ge(g_kept, f * 2 + 1)
                    for k, s in ((OF_B, OP_B), (OF_K, OP_K)):
                        i = mm(gb[k][:, :, :].rearrange("p q c -> p (q c)"), op[j][:, d, s, :],
                               ar[j][:, d, :, :, :].rearrange("p h q c -> p (h q c)"), start=True, stop=True)
                    i.then_inc(g_full, 1)

                def turn(f, j, d, back):
                    if back is not None:
                        if d == 0:
                            e.wait_ge(c_kept, back[0] * 2 + 3)
                        else:
                            e.wait_ge(y_kept, back[0] + 1)
                    for q, s in enumerate((OP_A, OP_B, OP_K, OP_V)):
                        i = e.transpose(trb[d][:, q, :], op[j][:, d, s, :], S.ident[:, :])
                    i.then_inc(turned, 1)

                def turn_blocks(f, j):
                    e.wait_ge(g_kept, f * 2 + 2)
                    e.wait_ge(h1_ready, f + 1)
                    for u in range(4):
                        i = e.transpose(tb[:, u, :], h1[:, u, :], S.ident[:, :])
                    i.then_inc(t1_full, 1)

                def a_k_v(f, j):
                    e.wait_ge(tm_kept, f * 2 + 2)
                    for u in range(4):
                        d, h = u // 2, u % 2
                        i = mm(akvb[:, d, :], g[j][:, OF_K, u, BY_A, :], pad(vp[j], d, h), start=(h == 0), stop=(h == 1))
                    i.then_inc(akv_full, 1)

                def tile(now, back, front):
                    n, _, _ = now
                    nothing = lambda: None
                    fill = [nothing] * 10
                    if back is not None:
                        m, j = back[0:2]
                        fill[0] = lambda: inverse_applied(m, j)
                        fill[1] = lambda: chunk_maps(m, j)
                        fill[2] = lambda: chunk_sums(m, j)
                        fill[3] = lambda: (states(m, j, 0), outputs_by_u(m, j))
                        fill[5] = lambda: states(m, j, 1)
                        fill[7] = lambda: outputs_by_state(m, j)
                    if front is not None:
                        f, k, half = front
                        fill[4] = lambda: products(f, k, half, 0, back)
                        fill[6] = lambda: products(f, k, half, 1, back)
                        q7 = fill[7]
                        fill[7] = lambda: (q7(), turn(f, k, 0, back))
                        fill[8] = lambda: (turn(f, k, 1, back), turn_blocks(f, k))
                        fill[9] = lambda: a_k_v(f, k)
                    e.wait_ge(t1_kept, n + 1)
                    for l in range(1, LEVELS):
                        first, last = l == 1, l == LEVELS - 1
                        e.wait_ge(al_ready, n * (LEVELS - 1) + l)
                        for d in range(2):
                            if not first:
                                e.wait_ge(th_kept, n * 8 + (2 * (l - 2) + d + 1))
                            for u in (2 * d, 2 * d + 1):
                                i = mm(xb[d][:, u % 2, :], al[:, l, u, :], t1[:, u, :] if first else tt(u),
                                       start=True, stop=True)
                            i.then_inc(x_full, 1)
                        fill[2 * l - 2]()
                        for d in range(2):
                            e.wait_ge(x_kept, n * 10 + (2 * (l - 1) + d + 1))
                            for u in (2 * d, 2 * d + 1):
                                h0 = h1[:, u, :] if first else hh(u)
                                if not last:
                                    mm(thb[d][:, u % 2, :], h0, xx[:, u, :], start=True, stop=True)
                                i = mm(thb[d][:, 2 + u % 2, :], xx[:, u, :], h0, start=True, stop=True)
                            i.then_inc(th_full, 1)
                        fill[2 * l - 1]()

                def first(t):
                    f, j, half = t
                    products(f, j, half, 0, None)
                    products(f, j, half, 1, None)
                    turn(f, j, 0, None)
                    turn(f, j, 1, None)
                    turn_blocks(f, j)
                    a_k_v(f, j)

                def last(t):
                    m, j, _ = t
                    e.wait_ge(y_kept, m)
                    e.wait_ge(c_kept, m * 2 + 1)
                    inverse_applied(m, j)
                    chunk_maps(m, j)
                    chunk_sums(m, j)
                    states(m, j, 0)
                    outputs_by_u(m, j)
                    states(m, j, 1)
                    outputs_by_state(m, j)
                tiles(e, first, tile, last)

            @block.vector
            def _(e):
                def maps(m, j):
                    e.wait_ge(m_full, m + 1)
                    for h in range(2):
                        cut = slice(h * CH, h * CH + CH)
                        i = e.tensor_tensor(mt[hs[h], :, :, cut].rearrange("p d k c -> p (d k) c"), mb[hs[h], :, cut],
                                            bcast(S.ident[hs[h], cut], 4), ALU.add)
                    i.then_inc(m_kept, 1)
                    e.wait_ge(q_full, m + 1)
                    e.tensor_tensor(qt[:, :, :], qb[:, 0:2, :], r2[j][:, :, :], ALU.add).then_inc(q_kept, 1)

                def states(m, j, c):
                    e.wait_ge(c_full, m * 2 + (c + 1))
                    for d in range(2):
                        k = c if d == 0 else 1 - c
                        i = e.scalar_tensor_tensor(out=(mid, st[1 - j])[c][:, d, :], in0=nb[:, 2 * d + k, :],
                                                   scalar=carry[:, d, ds(m * 2 + c, 1)], in1=heads[:, :],
                                                   op0=ALU.mult, op1=ALU.mult)
                    i.then_inc(c_kept, 1)

                def products(f, j, d):
                    e.wait_ge(g_full, f * 2 + (d + 1))
                    for k in range(2):
                        i = e.tensor_tensor(g[j][:, k, 2 * d:2 * d + 2, :, :],
                                            gb[k][:, :, :].rearrange("p (h q) c -> p h q c", h=2),
                                            bcast(mask[:, d, 2 * k:2 * k + 2, :], 2), ALU.mult)
                    i.then_inc(g_kept, 1)

                def tile(now, back, front):
                    n = now[0]
                    for l in range(1, LEVELS):
                        for d in range(2):
                            us = slice(2 * d, 2 * d + 2)
                            e.wait_ge(x_full, n * 10 + (2 * (l - 1) + d + 1))
                            e.tensor_tensor(xx[:, us, :], xb[d][:, 0:2, :], bcast(S.ident[:, :], 2), ALU.add
                                            ).then_inc(x_kept, 1)
                        if l == 1 and back is not None:
                            maps(*back[0:2])
                        if l == 2 and back is not None:
                            states(*back[0:2], 0)
                        if l == 3 and front is not None:
                            products(*front[0:2], 0)
                        if l == 3 and back is not None:
                            states(*back[0:2], 1)
                        if l == 4 and front is not None:
                            products(*front[0:2], 1)
                    for d in range(2):
                        e.wait_ge(th_full, n * 10 + (8 + d + 1))
                        e.tensor_copy(hf[:, 2 * d:2 * d + 2, :], thb[d][:, 2:4, :]).then_inc(hf_kept, 1)

                def first(t):
                    products(*t[0:2], 0)
                    products(*t[0:2], 1)

                def last(t):
                    maps(*t[0:2])
                    states(*t[0:2], 0)
                    states(*t[0:2], 1)

                e.sem_inc(c_kept, 1)
                tiles(e, first, tile, last)

            @block.scalar
            def _(e):
                def inverse_applied(m, j):
                    e.wait_ge(pu_full, m + 1)
                    e.activation(pp[:, :, :], pub[:, :, 0, :, :].rearrange("p d h c -> p d (h c)"), ACT.Copy)
                    e.activation(up[:, :, :, 0, :], pub[:, :, 1, :, :], ACT.Copy).then_inc(pu_kept, 1)

                def outputs(m, j):
                    e.wait_ge(y_full, m + 1)
                    e.activation(y[:, :, ds(m, 1), :].rearrange("p d o c -> p d (o c)"), yb[:, 0:2, :], ACT.Copy
                                 ).then_inc(y_kept, 1)

                def turned_kept(f, j, d):
                    e.wait_ge(turned, f * 2 + (d + 1))
                    e.activation(vp[j][:, d, :, 0, :], trb[d][:, 3, :].rearrange("p (h c) -> p h c", h=2), ACT.Copy)
                    e.activation(rv[j][:, d, 0, :, :], trb[d][:, 0, :].rearrange("p (h c) -> p h c", h=2), ACT.Copy)
                    for c in range(2):
                        i = e.activation(bk[j][hs[c], c, d, :, :], trb[d][hs[c], 1:3, :], ACT.Copy)
                    i.then_inc(tm_kept, 1)
                    if d == 1:
                        e.activation(r2[j][:, :, :], op[j][:, :, OP_R, :], ACT.Copy).then_inc(op_free, 1)

                def blocks(f, j):
                    e.wait_ge(t1_full, f + 1)
                    e.activation(t1[:, :, :], tb[:, :, :], ACT.Copy).then_inc(t1_kept, 1)

                def a_k_v(f, j):
                    e.wait_ge(akv_full, f + 1)
                    e.activation(rv[j][:, :, 1, :, :].rearrange("p d h c -> p d (h c)"), akvb[:, 0:2, :], ACT.Copy
                                 ).then_inc(akv_kept, 1)

                def first(t):
                    f, j, _ = t
                    turned_kept(f, j, 0)
                    turned_kept(f, j, 1)
                    blocks(f, j)
                    a_k_v(f, j)

                def tile(now, back, front):
                    n = now[0]
                    if back is not None:
                        inverse_applied(*back[0:2])
                    for l in range(1, LEVELS - 1):
                        for d in range(2):
                            e.wait_ge(th_full, n * 10 + (2 * (l - 1) + d + 1))
                            e.activation(th[:, d, :, :, :], thb[d][:, :, :].rearrange("p (x u) c -> p x u c", x=2),
                                         ACT.Copy).then_inc(th_kept, 1)
                    if back is not None:
                        outputs(*back[0:2])
                    if front is not None:
                        first(front)

                def last(t):
                    inverse_applied(*t[0:2])
                    outputs(*t[0:2])

                e.sem_inc(op_free, 2)
                tiles(e, first, tile, last)

            @block.gpsimd
            def _(e):
                def levels(f, j, before):
                    e.wait_ge(g_kept, f * 2 + 2)
                    ab = g[j][:, OF_B, :, BY_A, :]
                    if before is not None:
                        e.wait_ge(th_full, before * 10 + 2)
                    e.tensor_tensor(h1[:, :, :], ab, bcast(level[:, 0, :], 4), ALU.mult)
                    e.drain()
                    e.tensor_tensor(h1[:, :, :], h1[:, :, :], bcast(S.ident[:, :], 4), ALU.add).then_inc(h1_ready, 1)
                    for l in range(1, LEVELS):
                        if before is not None:
                            e.wait_ge(x_full, before * 10 + 2 * l)
                        e.tensor_tensor(al[:, l, :, :], ab, bcast(level[:, l, :], 4), ALU.mult).then_inc(al_ready, 1)

                tiles(e, lambda t: levels(0, 0, None),
                      lambda now, back, front: levels(front[0], front[1], now[0]) if front is not None else None,
                      lambda t: None)

        summed, centred, squared, eps_ready = sem("s_summed"), sem("s_centred"), sem("s_squared"), sem("s_eps_ready")
        root_ready, yt_full, y_normed, wo_in = sem("s_root"), sem("s_yt_full"), sem("s_y_normed"), sem("s_wo_in")
        bank = [*xb, *thb, *w]
        with nc.Block() as block:
            @block.sync
            def _(e):
                e.dma_start(S.proj[:, WO_T:WO_T + KD, :], A["w_out"]).then_inc(wo_in, 16)
                e.wait_ge(wo_in, 16)

            @block.gpsimd
            def _(e):
                for p in range(PAIRS):
                    y0, y1 = (y[:, d, p * NT:(p + 1) * NT, :] for d in range(2))
                    for t in range(NT):
                        m = e.tensor_tensor(y0[:, t, :], y0[:, t, :], y1[:, NT - 1 - t, :], ALU.add)
                    m.then_inc(summed, 1)

            @block.vector
            def _(e):
                def centre(p):
                    st = stat[:, p % 2, 0, :]
                    yy = y[:, 0, p * NT:(p + 1) * NT, :].rearrange("p t (h c) -> p (t h) c", c=CH)
                    e.wait_ge(summed, p + 1)
                    e.tensor_reduce(st, yy, AX.X, ALU.add)
                    e.drain()
                    e.tensor_scalar(st, st, 1.0 / CH, None, ALU.mult)
                    e.drain()
                    e.tensor_tensor(yy, yy, st.unsqueeze(2).to_broadcast([P, 2 * NT, CH]), ALU.subtract).then_inc(centred, 1)

                def scale(p):
                    st = stat[:, p % 2, 1, :]
                    yy, sq = (y[:, d, p * NT:(p + 1) * NT, :].rearrange("p t (h c) -> p (t h) c", c=CH) for d in range(2))
                    e.wait_ge(squared, p + 1)
                    e.tensor_reduce(st, sq, AX.X, ALU.add)
                    e.drain()
                    e.tensor_scalar(st, st, 1.0 / CH, 64e-5, ALU.mult, ALU.add).then_inc(eps_ready, 1)
                    e.wait_ge(root_ready, p + 1)
                    e.reciprocal(st, st)
                    e.drain()
                    e.tensor_tensor(yy, yy, st.unsqueeze(2).to_broadcast([P, 2 * NT, CH]), ALU.mult).then_inc(y_normed, 1)

                def gate(p):
                    for q in range(2):
                        cut = slice(q * HALF, (q + 1) * HALF)
                        e.wait_ge(yt_full, p * 2 + (q + 1))
                        t = y[:, 1, p * NT + 4 * q:p * NT + 4 * q + 4, :].rearrange("p t c -> p (t c)")
                        e.tensor_tensor(t, bank[2 * p + q][:, :, :].rearrange("p t c -> p (t c)"),
                                        S.proj[:, T_R + p, cut], ALU.mult)
                        e.drain()
                        e.tensor_tensor(S.mix[:, 2 + p, cut], S.mix[:, 2 + p, cut], t, ALU.add)

                centre(0)
                for p in range(PAIRS):
                    if p + 1 < PAIRS:
                        centre(p + 1)
                    scale(p)
                    if p >= 1:
                        gate(p - 1)
                gate(PAIRS - 1)

            @block.scalar
            def _(e):
                for p in range(PAIRS):
                    e.wait_ge(centred, p + 1)
                    e.activation(y[:, 1, p * NT:(p + 1) * NT, :], y[:, 0, p * NT:(p + 1) * NT, :], ACT.Square
                                 ).then_inc(squared, 1)
                    e.wait_ge(eps_ready, p + 1)
                    e.activation(stat[:, p % 2, 1, :], stat[:, p % 2, 1, :], ACT.Sqrt).then_inc(root_ready, 1)

            @block.tensor
            def _(e):
                for p in range(PAIRS):
                    e.wait_ge(y_normed, p + 1)
                    for q in range(2):
                        for t in range(4):
                            m = e.transpose(bank[2 * p + q][:, t, :], y[:, 0, p * NT + 4 * q + t, :], S.ident[:, :])
                        m.then_inc(yt_full, 1)


def clear_beyond(e, S, zero, done):
    e.dma_start(S.ys[EXPERTS:BLOCKS, :, :].rearrange("b p d -> p b d"), bcast(zero, OVER)).then_inc(done, 16)


WO_T = T_G
GROUPS, PER_GROUP = 4, 8
EXPERTS = GROUPS * PER_GROUP
NL = GROUPS + EXPERTS
FF = 512
KF = FF // P
BLK = P
OVER = 2 * L // BLK - 1
BLOCKS = EXPERTS + OVER


def output_and_router(nc, A, S, sem):
    ctx = ExitStack()
    with ctx:
        sb = lambda n, s, t=F32: ctx.enter_context(nc.sbuf_tensor(n, s, t))
        ps = lambda n, s: ctx.enter_context(nc.psum_tensor(n, s, F32))
        wo = S.proj[:, WO_T:WO_T + KD, :]
        wr = sb("o_wr", [P, KD, NL])
        br = sb("o_br", [P, NL])
        gb = sb("o_g", [P, D])
        xin = [S.proj[:, 8 + j, :] for j in range(2)]
        h2 = [S.proj[:, 10 + j, :] for j in range(2)]
        h2t = [S.proj[:, 12 + j, :].rearrange("p (k c) -> p k c", c=P) for j in range(2)]
        junk = S.proj[:, 14, :]
        ss, rs = sb("o_ss", [P, 2]), sb("o_rs", [P, 2])
        acc = [[ps(f"o_acc{j}{h}", [P, HALF]) for h in range(2)] for j in range(2)]
        tp = [ps(f"o_tp{j}", [P, 4, P]) for j in range(2)]
        lg = ps("o_lg", [P, NL])
        par_in = sem("o_par_in")
        x_in = [sem(f"o_x_in{j}") for j in range(2)]
        acc_full = sem("o_acc_full")
        x2_ready, squares, mean_ready, root_ready = sem("o_x2"), sem("o_sq"), sem("o_mean"), sem("o_root")
        h2_ready, h2_stored, turned, kept = sem("o_h2"), [sem("o_h2_stored0", True), sem("o_h2_stored1", True)], sem("o_turned"), sem("o_kept")
        lg_full, lg_kept, h2_turned = sem("o_lg_full"), sem("o_lg_kept"), sem("o_h2_turned")
        with nc.Block() as block:
            @block.sync
            def _(e):
                e.dma_start(wr[:, :, :], A["w_router"]).then_inc(par_in, 16)
                e.dma_start(br[:, :], A["b_router"].to_broadcast([P, NL])).then_inc(par_in, 16)
                e.dma_start(gb[:, :], A["norm2_g"].to_broadcast([P, D])).then_inc(par_in, 16)
                for t in range(NT):
                    if t >= 2:
                        e.wait_ge(x2_ready, t - 1)
                    e.dma_start(xin[t % 2], A["x"][t * P:(t + 1) * P, :]).then_inc(x_in[t % 2], 16)
                for j in range(2):
                    e.wait_ge(h2_stored[j], 16 * NT // 2)

            @block.gpsimd
            def _(e):
                for t in range(NT):
                    e.wait_ge(h2_ready, t + 1)
                    e.dma_start(S.h2d[t * P:(t + 1) * P, :], h2[t % 2]).then_inc(h2_stored[t % 2], 16)

            @block.tensor
            def _(e):
                e.wait_ge(par_in, 48)

                def project_tile(t):
                    b = t % 2
                    if t >= 2:
                        e.wait_ge(x2_ready, t - 1)
                    for h in range(2):
                        for k in range(KD):
                            m = e.matmul(acc[b][h][:, :], S.mix[:, k, t * P:(t + 1) * P], wo[:, k, h * HALF:(h + 1) * HALF],
                                         start=(k == 0), stop=(k == KD - 1))
                    m.then_inc(acc_full, 1)

                project_tile(0)
                for t in range(NT):
                    b = t % 2
                    if t + 1 < NT:
                        project_tile(t + 1)
                    e.wait_ge(h2_ready, t + 1)
                    if t >= 1:
                        e.wait_ge(kept, 2 * t)
                    for k in range(KD):
                        m = e.transpose(tp[k // 4][:, k % 4, :], h2[b][:, k * P:(k + 1) * P], S.ident[:, :])
                    m.then_inc(turned, 1)
                    e.wait_ge(turned, t + 1)
                    e.sem_inc(h2_turned, 1)
                    e.wait_ge(kept, 2 * t + 2)
                    if t >= 1:
                        e.wait_ge(lg_kept, t)
                    for k in range(KD):
                        m = e.matmul(lg[:, :], h2t[b][:, k, :], wr[:, k, :], start=(k == 0), stop=(k == KD - 1))
                    m.then_inc(lg_full, 1)

            @block.vector
            def _(e):
                e.wait_ge(par_in, 48)
                for t in range(NT):
                    b = t % 2
                    e.wait_ge(acc_full, t + 1)
                    e.wait_ge(x_in[b], 16 * (t // 2 + 1))
                    for h in range(2):
                        cut = slice(h * HALF, (h + 1) * HALF)
                        m = e.tensor_tensor(S.x2[:, t, cut], acc[b][h][:, :], xin[b][:, cut], ALU.add)
                    m.then_inc(x2_ready, 1)
                    e.wait_ge(squares, t + 1)
                    e.tensor_scalar(rs[:, b:b + 1], ss[:, b:b + 1], 1.0 / D, EPS, ALU.mult, ALU.add).then_inc(mean_ready, 1)
                    e.wait_ge(root_ready, t + 1)
                    e.reciprocal(rs[:, b:b + 1], rs[:, b:b + 1])
                    e.drain()
                    if t >= 2:
                        e.wait_ge(h2_stored[b], 16 * (t // 2))
                        e.wait_ge(h2_turned, t - 1)
                    e.scalar_tensor_tensor(out=h2[b], in0=S.x2[:, t, :], scalar=rs[:, b:b + 1], in1=gb[:, :],
                                           op0=ALU.mult, op1=ALU.mult).then_inc(h2_ready, 1)
                    e.wait_ge(turned, t + 1)
                    if t >= 2:
                        e.wait_ge(lg_full, t - 1)
                    e.tensor_copy(h2t[b][:, 0:4, :], tp[0][:, :, :]).then_inc(kept, 1)
                    e.wait_ge(lg_full, t + 1)
                    e.tensor_tensor(S.logits[:, t, :], lg[:, :], br[:, :], ALU.add).then_inc(lg_kept, 1)

            @block.scalar
            def _(e):
                for t in range(NT):
                    b = t % 2
                    e.wait_ge(x2_ready, t + 1)
                    e.drain()
                    e.activation(junk, S.x2[:, t, :], ACT.Square, accum_out=ss[:, b:b + 1]).then_inc(squares, 1)
                    e.wait_ge(mean_ready, t + 1)
                    e.activation(rs[:, b:b + 1], rs[:, b:b + 1], ACT.Sqrt).then_inc(root_ready, 1)
                    e.wait_ge(turned, t + 1)
                    if t >= 2:
                        e.wait_ge(lg_full, t - 1)
                    e.activation(h2t[b][:, 4:8, :], tp[1][:, :, :], ACT.Copy).then_inc(kept, 1)


def expert_room(S):
    flat = S.proj[:, 8:CT, :].rearrange("p c t -> p (c t)")
    cut = lambda a, n: flat[:, a * L:(a + n) * L]
    w1 = [cut(4 * j, 4).rearrange("p (k f) -> p k f", f=FF) for j in range(2)]
    w3 = [cut(8 + 4 * j, 4).rearrange("p (k f) -> p k f", f=FF) for j in range(2)]
    w2 = [S.mix[:, 4 * j:4 * j + 4, :].rearrange("p c t -> p (c t)").rearrange("p (k d) -> p k d", d=D) for j in range(2)]
    return w1, w3, w2


def load_expert(e, A, room, j, which, done):
    for n in range(3):
        load_matrix(e, A, room, n, j, which, done[n])


def load_matrix(e, A, room, n, j, which, done):
    of = A[("moe_w1", "moe_w3", "moe_w2")[n]]
    e.dma_start(room[n][j], of[ds(which, 1), :, :, :].rearrange("o p k c -> (o p) k c")).then_inc(done, 16)


def route(nc, A, S, sem, w_in):
    ctx = ExitStack()
    with ctx:
        sb = lambda n, s, t=F32: ctx.enter_context(nc.sbuf_tensor(n, s, t))
        ps = lambda n, s: ctx.enter_context(nc.psum_tensor(n, s, F32))
        G, E, Q = GROUPS, PER_GROUP, EXPERTS
        tri = sb("q_tri", [P, 2, P])
        down = sb("q_down", [P, E])
        far = sb("q_far", [P, Q])
        gm, ge, gsum = sb("q_gm", [P, NT]), sb("q_ge", [P, NT, G]), sb("q_gsum", [P, NT])
        og = sb("q_og", [P, NT, G])
        prod = sb("q_prod", [P, NT, Q])
        es, top, rank8 = sb("q_es", [P, NT, E]), sb("q_top", [P, 2, NT]), sb("q_rank8", [P, NT, E])
        oe = [sb(f"q_oe{k}", [P, NT, E]) for k in range(2)]
        eo = [sb(f"q_eo{k}", [P, NT, Q]) for k in range(2)]
        m = sb("q_m", [P, NT, Q])
        rank = sb("q_rank", [P, NT, Q])
        counts = sb("q_counts", [P, NT + 1, Q])
        extra, ends, starts = sb("q_extra", [P, Q]), sb("q_ends", [P, Q]), sb("q_starts", [P, Q])
        first = sb("q_first", [P, Q])
        slot, slot_o, is_over, eid = sb("q_slot", [P, NT]), sb("q_slot_o", [P, NT]), sb("q_is_over", [P, NT]), sb("q_eid", [P, NT])
        owner = sb("q_owner", [P, OVER])
        ids0 = sb("q_ids0", [P, BLOCKS], U32)
        token = sb("q_token", [P, NT], U32)
        idrow, idrowf = sb("q_idrow", [BLOCKS, P], U32), sb("q_idrowf", [BLOCKS, P])
        pr, pt, pi = ps("q_pr", [P, NT, Q]), ps("q_pt", [P, NT, Q]), ps("q_pi", [P, BLOCKS])
        par_in, zeroed, cleared = sem("q_par_in"), sem("q_zeroed"), sem("q_cleared")
        gexp, esub, eexp, m_ready, ranked = sem("q_gexp"), sem("q_esub"), sem("q_eexp"), sem("q_m"), sem("q_ranked")
        places, scattered, rows_in, rowf, turned = (sem("q_places"), sem("q_scattered", True), sem("q_rows_in"),
                                                    sem("q_rowf"), sem("q_turned"))
        gready, tokens = sem("q_gready"), sem("q_tokens")
        lo = S.logits
        el = lo[:, :, G:NL].rearrange("p t (g e) -> p t g e", g=G)
        with nc.Block() as block:
            @block.sync
            def _(e):
                e.dma_start(tri[:, :, :], A["rt_tri"]).then_inc(par_in, 16)
                e.dma_start(down[:, :], A["rt_down"].to_broadcast([P, E])).then_inc(par_in, 16)
                e.dma_start(far[:, :], A["rt_far"].to_broadcast([P, Q])).then_inc(par_in, 16)
                for j in range(2):
                    load_expert(e, A, expert_room(S), j, j, w_in[j])
                e.wait_ge(zeroed, 1)
                e.dma_start(S.tok.rearrange("(p b) o -> p (b o)", p=P), ids0[:, :]).then_inc(cleared, 16)
                e.wait_ge(scattered, 16 * 2 * NT)
                e.dma_start(idrow[:, :], S.tok.rearrange("(b p) o -> b (p o)", p=P)).then_inc(rows_in, 16)
                e.wait_ge(rows_in, 16)

            @block.gpsimd
            def _(e):
                e.memset(ids0[:, :], 0).then_inc(zeroed, 1)
                e.iota(token[:, :], [[P, NT]], base=0, channel_multiplier=1).then_inc(tokens, 1)
                e.wait_ge(tokens, 1)
                e.wait_ge(cleared, 16)
                e.wait_ge(places, 2)
                for t in range(NT):
                    for k in range(2):
                        e.indirect_dma_start(S.tok, bass.IndirectOffsetOnAxis(ap=S.place[:, t, k:k + 1], axis=0),
                                             token[:, t:t + 1], None).then_inc(scattered, 16)

            @block.tensor
            def _(e):
                e.wait_ge(par_in, 48)
                e.wait_ge(m_ready, 1)
                e.matmul(pr[:, :, :].rearrange("p t q -> p (t q)"), tri[:, 0, :], m[:, :, :].rearrange("p t q -> p (t q)"),
                         start=True, stop=True)
                e.matmul(pt[:, :, :].rearrange("p t q -> p (t q)"), tri[:, 1, :], m[:, :, :].rearrange("p t q -> p (t q)"),
                         start=True, stop=True).then_inc(ranked, 1)
                e.wait_ge(rowf, 1)
                e.transpose(pi[:, :], idrowf[:, :], S.ident[0:BLOCKS, 0:BLOCKS]).then_inc(turned, 1)

            @block.scalar
            def _(e):
                e.wait_ge(gready, 1)
                e.activation(ge[:, :, :], ge[:, :, :], ACT.Exp).then_inc(gexp, 1)
                e.wait_ge(esub, 1)
                e.activation(S.gate[:, :, 1], S.gate[:, :, 1], ACT.Exp).then_inc(eexp, 1)

            @block.vector
            def _(e):
                tt, sc = e.tensor_tensor, e.tensor_scalar
                d = e.drain
                e.wait_ge(par_in, 48)

                def first_max(out, val, best, n, tmp):
                    tt(out, val, best.unsqueeze(2).to_broadcast([P, NT, n]), ALU.is_equal)
                    d()
                    tt(out, out, bcast(down[:, 0:n], NT), ALU.mult)
                    d()
                    e.tensor_reduce(tmp, out, AX.X, ALU.max)
                    d()
                    tt(out, bcast(down[:, 0:n], NT), tmp.unsqueeze(2).to_broadcast([P, NT, n]), ALU.is_equal)
                    d()

                e.tensor_reduce(gm[:, :], lo[:, :, 0:G], AX.X, ALU.max)
                d()
                tt(ge[:, :, :], lo[:, :, 0:G], gm[:, :].unsqueeze(2).to_broadcast([P, NT, G]), ALU.subtract
                   ).then_inc(gready, 1)
                first_max(og[:, :, :], lo[:, :, 0:G], gm[:, :], G, gsum[:, :])
                tt(prod[:, :, :].rearrange("p t (g e) -> p t g e", g=G), el,
                   og[:, :, :].unsqueeze(3).to_broadcast([P, NT, G, E]), ALU.mult)
                d()
                e.tensor_reduce(es[:, :, :], prod[:, :, :].rearrange("p t (g e) -> p t e g", g=G), AX.X, ALU.add)
                d()
                for k in range(2):
                    e.tensor_reduce(top[:, k, :], es[:, :, :], AX.X, ALU.max)
                    d()
                    first_max(oe[k][:, :, :], es[:, :, :], top[:, k, :], E, gm[:, :])
                    if k == 0:
                        e.scalar_tensor_tensor(out=es[:, :, :], in0=oe[0][:, :, :], scalar=-3e38, in1=es[:, :, :],
                                               op0=ALU.mult, op1=ALU.add)
                        d()
                tt(S.gate[:, :, 1], top[:, 1, :], top[:, 0, :], ALU.subtract).then_inc(esub, 1)
                e.wait_ge(gexp, 1)
                e.tensor_reduce(gsum[:, :], ge[:, :, :], AX.X, ALU.add)
                e.wait_ge(eexp, 1)
                sc(gm[:, :], S.gate[:, :, 1], 1.0, None, ALU.add)
                d()
                tt(gsum[:, :], gsum[:, :], gm[:, :], ALU.mult)
                d()
                e.reciprocal(S.gate[:, :, 0], gsum[:, :])
                d()
                tt(S.gate[:, :, 1], S.gate[:, :, 1], S.gate[:, :, 0], ALU.mult)
                for k in range(2):
                    for g in range(G):
                        tt(eo[k][:, :, g * E:(g + 1) * E], oe[k][:, :, :],
                           og[:, :, g:g + 1].to_broadcast([P, NT, E]), ALU.mult)
                d()
                tt(m[:, :, :], eo[0][:, :, :], eo[1][:, :, :], ALU.add).then_inc(m_ready, 1)
                e.wait_ge(ranked, 1)
                e.memset(counts[:, 0, :], 0.0)
                d()
                for t in range(NT):
                    tt(counts[:, t + 1, :], counts[:, t, :], pt[:, t, :], ALU.add)
                    d()
                tt(rank[:, :, :], pr[:, :, :], counts[:, 0:NT, :], ALU.add)
                total = counts[:, NT, :]
                sc(extra[:, :], total, float(BLK), None, ALU.is_gt)
                for k in range(2, L // BLK):
                    sc(first[:, :], total, float(k * BLK), None, ALU.is_gt)
                    d()
                    tt(extra[:, :], extra[:, :], first[:, :], ALU.add)
                    d()
                e.memset(first[:, :], 1.0)
                d()
                e.tensor_tensor_scan(ends[:, :], first[:, :], extra[:, :], 0.0, ALU.mult, ALU.add)
                d()
                tt(starts[:, :], ends[:, :], extra[:, :], ALU.subtract)
                d()
                sc(starts[:, :], starts[:, :], float(BLK), float((EXPERTS - 1) * BLK), ALU.mult, ALU.add)
                sc(first[:, :], far[:, :], float(BLK), None, ALU.mult)
                d()
                for k in range(2):
                    def pick(out, what):
                        tt(prod[:, :, :], eo[k][:, :, :], what, ALU.mult)
                        d()
                        e.tensor_reduce(out, prod[:, :, :], AX.X, ALU.add)
                        d()
                    pick(slot[:, :], rank[:, :, :])
                    pick(eid[:, :], bcast(first[:, :], NT))
                    pick(slot_o[:, :], bcast(starts[:, :], NT))
                    sc(is_over[:, :], slot[:, :], float(BLK), None, ALU.is_ge)
                    tt(slot_o[:, :], slot_o[:, :], eid[:, :], ALU.subtract)
                    tt(slot[:, :], slot[:, :], eid[:, :], ALU.add)
                    d()
                    tt(slot_o[:, :], slot_o[:, :], is_over[:, :], ALU.mult)
                    d()
                    tt(slot[:, :], slot[:, :], slot_o[:, :], ALU.add)
                    d()
                    e.tensor_copy(S.place[:, :, k], slot[:, :]).then_inc(places, 1)
                for b in range(OVER):
                    sc(first[:, :], ends[:, :], float(b), None, ALU.is_le)
                    d()
                    e.tensor_reduce(owner[:, b:b + 1], first[:, :], AX.X, ALU.add)
                    d()
                sc(owner[:, :], owner[:, :], float(EXPERTS - 1), None, ALU.min)
                d()
                e.tensor_copy(S.over[:, 0:OVER], owner[:, :])
                e.tensor_copy(S.over[:, OVER:OVER + 1], ends[:, Q - 1:Q])
                e.wait_ge(rows_in, 16)
                e.tensor_copy(idrowf[:, :], idrow[:, :]).then_inc(rowf, 1)
                e.wait_ge(turned, 1)
                e.tensor_copy(S.ids[:, 0:BLOCKS], pi[:, :])


def experts(nc, A, S, sem, w_in):
    ctx = ExitStack()
    with ctx:
        sb = lambda n, s, t=F32: ctx.enter_context(nc.sbuf_tensor(n, s, t))
        ps = lambda n, s: ctx.enter_context(nc.psum_tensor(n, s, F32))
        w1, w3, w2 = room = expert_room(S)
        spare = lambda t: S.proj[:, t, :]
        xg = [spare(CT - 3), spare(CT - 2)]
        act, at = spare(CT - 1)[:, 0:FF], spare(CT - 1)[:, FF:2 * FF].rearrange("p (k c) -> p k c", c=P)
        idx = [sb(f"e_idx{j}", [P, 1], U32) for j in range(2)]
        xh, xl = (sb(f"e_{n}", [P, KD, P], F32R) for n in ("xh", "xl"))
        RING, PIECES = 4, 8
        USES = PIECES + 1
        rh, rl = ([sb(f"e_{n}{r}", [P, D], F32R) for r in range(RING)] for n in ("rh", "rl"))
        yo = [sb(f"e_yo{j}", [P, D]) for j in range(2)]
        xt = yo[1][:, :].rearrange("p (k c) -> p k c", c=P)
        tp = [ps(f"e_tp{j}", [P, 4, P]) for j in range(2)]
        ph = [ps(f"e_ph{j}", [P, FF]) for j in range(2)]
        pa = ps("e_pa", [P, KF, P])
        py = [ps(f"e_py{j}", [P, HALF]) for j in range(2)]
        idx_ready, x_in, x_used = sem("e_idx_ready"), [sem("e_x_in0", True), sem("e_x_in1", True)], sem("e_x_used")
        turned, x_high, x_low, silu, act_ready = sem("e_turned"), sem("e_x_high"), sem("e_x_low"), sem("e_silu"), sem("e_act_ready")
        a_turned, a_kept, y_kept = sem("e_a_turned"), sem("e_a_kept"), sem("e_y_kept")
        high, low, used = sem("e_high"), sem("e_low"), sem("e_used")
        stored = [sem("e_stored0"), sem("e_stored1")]
        stepped, passed = sem("e_stepped"), sem("e_passed")
        NP = EXPERTS // 2

        def piece(j, s):
            return (w1, w3)[s // 4][j][:, 2 * (s % 4):2 * (s % 4) + 2, :].rearrange("p k f -> p (k f)")

        def experts_in_order(body):
            def pair(i):
                body(0, i * 2, i, i)
                body(1, i * 2 + 1, i, i + 1)
            return pair, lambda: (body(0, EXPERTS - 2, NP - 1, NP - 1), body(1, EXPERTS - 1, NP - 1, None))

        def run_experts(e, body):
            pair, end = experts_in_order(body)
            with e.Fori(0, NP - 1) as i:
                pair(i)
            end()

        with nc.Block() as block:
            @block.sync
            def _(e):
                with e.Fori(1, NP) as i:
                    for j in range(2):
                        n = i * 2 + (j - 2)
                        for k, (done, count) in enumerate(((low, n * PIECES + RING), (low, n * PIECES + PIECES),
                                                           (used, n * USES + USES))):
                            e.wait_ge(done, count)
                            e.sem_inc(passed, 1)
                            load_matrix(e, A, room, k, j, i * 2 + j, w_in[j][k])

            @block.gpsimd
            def _(e):
                e.sem_inc(x_used, 2)

                def gather(j, b, n, half_n):
                    e.wait_ge(x_used, n + 1)
                    e.tensor_copy(idx[j][:, :], S.ids[:, ds(b, 1)]).then_inc(idx_ready, 1)
                    e.wait_ge(idx_ready, n + 1)
                    e.sem_inc(stepped, 1)
                    e.indirect_dma_start(xg[j], None, S.h2d,
                                         bass.IndirectOffsetOnAxis(ap=idx[j][:, :], axis=0)).then_inc(x_in[j], 16)
                with e.Fori(0, NP) as i:
                    for j in range(2):
                        gather(j, i * 2 + j, i * 2 + j, i)
                e.wait_ge(x_in[0], NP * 16)
                e.wait_ge(x_in[1], NP * 16)

            @block.tensor
            def _(e):
                def turn(j, half_n):
                    e.wait_ge(x_in[j], half_n * 16 + 16)
                    for k in range(KD):
                        m = e.transpose(tp[k // 4][:, k % 4, :], xg[j][:, k:D:KD], S.ident[:, :])
                    m.then_inc(turned, 1)

                def expert(j, n, half_n, next_half):
                    e.wait_ge(x_low, n + 1)
                    for s in range(PIECES):
                        e.wait_ge(low, n * PIECES + (s + 1))
                        for q in range(2):
                            k, cut = 2 * (s % 4) + q, slice(q * HALF, (q + 1) * HALF)
                            m = split_matmul(e, ph[s // 4][:, :], (xh[:, k, :], xl[:, k, :]),
                                             (rh[s % RING][:, cut], rl[s % RING][:, cut]), k == 0, k == KD - 1)
                        m.then_inc(used, 1)
                    if next_half is not None:
                        turn(1 - j, next_half)
                    e.wait_ge(act_ready, n + 1)
                    for k in range(KF):
                        m = e.transpose(pa[:, k, :], act[:, k:FF:KF], S.ident[:, :])
                    m.then_inc(a_turned, 1)
                    e.wait_ge(w_in[j][2], half_n * 16 + 16)
                    e.wait_ge(a_kept, n + 1)
                    e.wait_ge(y_kept, n * 2 + 2)
                    for h in range(2):
                        for k in range(KF):
                            m = e.matmul(py[h][:, :], at[:, k, :], w2[j][:, k, h * HALF:(h + 1) * HALF],
                                         start=(k == 0), stop=(k == KF - 1))
                    m.then_inc(used, 1)

                turn(0, 0)
                run_experts(e, expert)

            @block.scalar
            def _(e):
                def split(j, s):
                    e.activation(rh[s % RING][:, :], piece(j, s), ACT.Copy).then_inc(high, 1)

                def rows(n):
                    e.wait_ge(turned, n + 1)
                    e.sem_inc(x_used, 1)
                    for q in range(2):
                        m = e.activation(xh[:, 4 * q:4 * q + 4, :], tp[q][:, :, :], ACT.Copy)
                    m.then_inc(x_high, 1)

                def expert(j, n, half_n, next_half):
                    for s in range(4):
                        if s == 0:
                            e.wait_ge(w_in[j][1], half_n * 16 + 16)
                        e.wait_ge(used, n * USES + (s + 1))
                        split(j, RING + s)
                    e.activation(act, ph[0][:, :], ACT.Silu).then_inc(silu, 1)

                    def ahead(s):
                        if next_half is not None:
                            if s == 0:
                                e.wait_ge(w_in[1 - j][0], next_half * 16 + 16)
                            e.wait_ge(used, n * USES + (s + RING + 1))
                            split(1 - j, s)
                    ahead(0)
                    ahead(1)
                    e.wait_ge(a_turned, n + 1)
                    e.activation(at, pa[:, :, :], ACT.Copy).then_inc(a_kept, 1)
                    if next_half is not None:
                        rows(n + 1)
                    ahead(2)
                    ahead(3)
                    e.wait_ge(used, n * USES + USES)
                    e.wait_ge(stored[j], half_n * 16 + 16)
                    e.activation(yo[j][:, 0:HALF], py[0][:, :], ACT.Copy).then_inc(y_kept, 1)
                    e.wait_ge(y_kept, n * 2 + 4)
                    e.sem_inc(passed, 1)
                    e.dma_start(S.ys[ds(n, 1), :, :].rearrange("o p d -> (o p) d"), yo[j][:, :]).then_inc(stored[j], 16)

                e.sem_inc(stored[0], 16)
                e.sem_inc(stored[1], 16)
                e.sem_inc(y_kept, 2)
                e.wait_ge(w_in[0][0], 16)
                for s in range(RING):
                    split(0, s)
                rows(0)
                run_experts(e, expert)
                for j in range(2):
                    e.wait_ge(stored[j], NP * 16 + 16)

            @block.vector
            def _(e):
                def split(j, s, count):
                    e.wait_ge(high, count)
                    e.tensor_tensor(rl[s % RING][:, :], piece(j, s), rh[s % RING][:, :].bitcast(F32), ALU.subtract
                                    ).then_inc(low, 1)

                def rows(n):
                    e.wait_ge(x_high, n + 1)
                    for q in range(2):
                        cut = (slice(None), slice(4 * q, 4 * q + 4), slice(None))
                        m = e.tensor_tensor(xl[cut], tp[q][:, :, :], xh[cut].bitcast(F32), ALU.subtract)
                    m.then_inc(x_low, 1)

                def expert(j, n, half_n, next_half):
                    ahead = lambda s: split(1 - j, s, n * PIECES + (PIECES + s + 1)) if next_half is not None else None
                    for s in range(4):
                        split(j, RING + s, n * PIECES + (RING + s + 1))
                    ahead(0)
                    ahead(1)
                    e.wait_ge(used, n * USES + PIECES)
                    e.wait_ge(silu, n + 1)
                    e.tensor_tensor(act, act, ph[1][:, :], ALU.mult).then_inc(act_ready, 1)
                    if next_half is not None:
                        rows(n + 1)
                    ahead(2)
                    ahead(3)
                    e.wait_ge(used, n * USES + USES)
                    e.wait_ge(stored[j], half_n * 16 + 16)
                    e.tensor_copy(yo[j][:, HALF:D], py[1][:, :]).then_inc(y_kept, 1)

                for s in range(RING):
                    split(0, s, s + 1)
                rows(0)
                run_experts(e, expert)

        v = [sem(f"f_{n}", n == "x_in") for n in ("idx", "x_in", "w_in", "turned", "kept", "h_full", "silu", "act", "a_turned",
                                     "a_kept", "y_full", "y_kept", "stored")]
        f_idx, f_x, f_w, f_turned, f_kept, f_h, f_silu, f_act, f_at, f_ak, f_y, f_yk, f_st = v
        count_at, owner_at = S.over[0:1, OVER:OVER + 1], S.over

        def beyond(e, body):
            n = e.value_load(count_at, min_val=0, max_val=OVER)
            with e.If(n > 0):
                with e.Fori(0, OVER) as b:
                    body(b)

        with nc.Block() as block:
            @block.sync
            def _(e):
                def body(b):
                    e.wait_ge(f_st, b * 16 + 16)
                    e.sem_inc(passed, 1)
                    owner = e.value_load(owner_at[0:1, ds(b, 1)], min_val=0, max_val=EXPERTS - 1)
                    load_expert(e, A, room, 0, owner, (f_w, f_w, f_w))
                e.sem_inc(f_st, 16)
                beyond(e, body)

            @block.gpsimd
            def _(e):
                def body(b):
                    e.wait_ge(f_st, b * 16 + 16)
                    e.tensor_copy(idx[0][:, :], S.ids[:, ds(b + EXPERTS, 1)]).then_inc(f_idx, 1)
                    e.wait_ge(f_idx, b + 1)
                    e.sem_inc(stepped, 1)
                    e.indirect_dma_start(xg[0], None, S.h2d,
                                         bass.IndirectOffsetOnAxis(ap=idx[0][:, :], axis=0)).then_inc(f_x, 16)
                beyond(e, body)

            @block.tensor
            def _(e):
                def body(b):
                    e.wait_ge(f_x, b * 16 + 16)
                    for k in range(KD):
                        m = e.transpose(tp[k // 4][:, k % 4, :], xg[0][:, k:D:KD], S.ident[:, :])
                    m.then_inc(f_turned, 1)
                    e.wait_ge(f_w, b * 48 + 48)
                    e.wait_ge(f_kept, b + 1)
                    for s, w in ((0, w1[0]), (1, w3[0])):
                        for k in range(KD):
                            m = e.matmul(ph[s][:, :], xt[:, k, :], w[:, k, :], start=(k == 0), stop=(k == KD - 1))
                    m.then_inc(f_h, 1)
                    e.wait_ge(f_act, b + 1)
                    for k in range(KF):
                        m = e.transpose(pa[:, k, :], act[:, k:FF:KF], S.ident[:, :])
                    m.then_inc(f_at, 1)
                    e.wait_ge(f_ak, b + 1)
                    for h in range(2):
                        for k in range(KF):
                            m = e.matmul(py[h][:, :], at[:, k, :], w2[0][:, k, h * HALF:(h + 1) * HALF],
                                         start=(k == 0), stop=(k == KF - 1))
                    m.then_inc(f_y, 1)
                beyond(e, body)

            @block.vector
            def _(e):
                def body(b):
                    e.wait_ge(f_turned, b + 1)
                    e.tensor_copy(xt[:, 0:4, :], tp[0][:, :, :])
                    e.tensor_copy(xt[:, 4:8, :], tp[1][:, :, :]).then_inc(f_kept, 1)
                    e.wait_ge(f_silu, b + 1)
                    e.tensor_tensor(act, act, ph[1][:, :], ALU.mult).then_inc(f_act, 1)
                    e.wait_ge(f_at, b + 1)
                    e.tensor_copy(at, pa[:, :, :]).then_inc(f_ak, 1)
                    e.wait_ge(f_y, b + 1)
                    e.tensor_copy(yo[0][:, 0:HALF], py[0][:, :])
                    e.tensor_copy(yo[0][:, HALF:D], py[1][:, :]).then_inc(f_yk, 1)
                beyond(e, body)

            @block.scalar
            def _(e):
                def body(b):
                    e.wait_ge(f_h, b + 1)
                    e.activation(act, ph[0][:, :], ACT.Silu).then_inc(f_silu, 1)
                    e.wait_ge(f_yk, b + 1)
                    e.sem_inc(passed, 1)
                    e.dma_start(S.ys[ds(b + EXPERTS, 1), :, :].rearrange("o p d -> (o p) d"), yo[0][:, :]).then_inc(f_st, 16)
                    e.wait_ge(f_st, b * 16 + 32)
                beyond(e, body)


def combine(nc, A, S, sem, out):
    ctx = ExitStack()
    with ctx:
        sb = lambda n, s, t=F32: ctx.enter_context(nc.sbuf_tensor(n, s, t))
        gb = S.proj[:, 8, :]
        NB = 3
        ya = [[S.proj[:, 9 + 2 * j + k, :] for k in range(2)] for j in range(NB)]
        junk = S.proj[:, 16, :]
        ss, rs = sb("z_ss", [P, NT]), sb("z_rs", [P, NT])
        par_in, stored = sem("z_par_in"), sem("z_stored")
        y_in = [sem(f"z_y_in{j}", True) for j in range(NB)]
        summed, squares, mean_ready, root_ready, normed = (sem("z_summed"), sem("z_squares"), sem("z_mean"),
                                                           sem("z_root"), sem("z_normed"))
        with nc.Block() as block:
            @block.sync
            def _(e):
                e.dma_start(gb, A["norm_f_g"].to_broadcast([P, D])).then_inc(par_in, 16)
                for t in range(NT):
                    e.wait_ge(normed, t + 1)
                    e.dma_start(out[t * P:(t + 1) * P, :], S.x2[:, t, :]).then_inc(stored, 16)
                e.wait_ge(stored, 16 * NT)

            @block.gpsimd
            def _(e):
                for t in range(NT):
                    if t >= NB:
                        e.wait_ge(summed, 2 * (t - NB) + 2)
                    for k in range(2):
                        e.indirect_dma_start(ya[t % NB][k], None, S.ys.rearrange("b p d -> (b p) d"),
                                             bass.IndirectOffsetOnAxis(ap=S.place[:, t, k:k + 1], axis=0)
                                             ).then_inc(y_in[t % NB], 16)

            @block.vector
            def _(e):
                e.wait_ge(par_in, 16)

                def add(t):
                    e.wait_ge(y_in[t % NB], 32 * (t // NB + 1))
                    for k in range(2):
                        e.scalar_tensor_tensor(out=S.x2[:, t, :], in0=ya[t % NB][k], scalar=S.gate[:, t, k:k + 1],
                                               in1=S.x2[:, t, :], op0=ALU.mult, op1=ALU.add).then_inc(summed, 1)
                        e.wait_ge(summed, 2 * t + k + 1)
                add(0)
                for t in range(NT):
                    if t + 1 < NT:
                        add(t + 1)
                    e.wait_ge(squares, t + 1)
                    e.tensor_scalar(rs[:, t:t + 1], ss[:, t:t + 1], 1.0 / D, EPS, ALU.mult, ALU.add).then_inc(mean_ready, 1)
                    e.wait_ge(root_ready, t + 1)
                    e.reciprocal(rs[:, t:t + 1], rs[:, t:t + 1])
                    e.drain()
                    e.scalar_tensor_tensor(out=S.x2[:, t, :], in0=S.x2[:, t, :], scalar=rs[:, t:t + 1], in1=gb,
                                           op0=ALU.mult, op1=ALU.mult).then_inc(normed, 1)

            @block.scalar
            def _(e):
                for t in range(NT):
                    e.wait_ge(summed, 2 * t + 2)
                    e.drain()
                    e.activation(junk, S.x2[:, t, :], ACT.Square, accum_out=ss[:, t:t + 1]).then_inc(squares, 1)
                    e.wait_ge(mean_ready, t + 1)
                    e.activation(rs[:, t:t + 1], rs[:, t:t + 1], ACT.Sqrt).then_inc(root_ready, 1)


@contextmanager
def semaphores(nc, whole):
    with ExitStack() as ctx:
        used = []

        def sem(name, kept=False):
            s = (whole if kept else ctx).enter_context(nc.semaphore(name))
            if not kept:
                used.append(s)
            return s
        yield sem
        with nc.Block() as block:
            @block.sync
            def _(e):
                for s in used:
                    e.sem_clear(s)


def program(nc, A, out):
    ctx = ExitStack()
    with ctx:
        sb = lambda n, s, t=F32: ctx.enter_context(nc.sbuf_tensor(n, s, t))
        S = Memory()
        S.proj = sb("proj", [P, CT, L])
        S.ident, S.ones = sb("ident", [P, P]), sb("ones", [P, 1])
        S.rpar = sb("rpar", [P, PAIRS, N_PAR])
        S.carry = sb("carry", [P, PAIRS, 2, NCH])
        S.logits, S.gate = sb("logits", [P, NT, NL]), sb("gate", [P, NT, 2])
        S.place = sb("place", [P, NT, 2], U32)
        S.ids = sb("ids", [P, BLOCKS + 1], U32)
        S.over = sb("over", [P, OVER + 1], I32)
        S.x2 = S.proj[:, 0:NT, :]
        dram = lambda n, s, t=F32: nc.dram_tensor(n, s, t, kind="Internal").ap()
        S.ops = dram("scan_operands", (PAIRS, 2, NT, P, N_OP, P))
        S.h2d = dram("h2_rows", (L, D))
        S.tok = dram("token_of_place", (BLOCKS * BLK, 1), U32)
        S.ys = dram("expert_rows", (BLOCKS, BLK, D))
        with semaphores(nc, ctx) as sem:
            project(nc, A, S, sem)
        S.mix = sb("mix", [P, KD, L])
        with semaphores(nc, ctx) as sem:
            hyena(nc, A, S, sem)
        with semaphores(nc, ctx) as sem:
            attention(nc, A, S, sem)
        with semaphores(nc, ctx) as sem:
            rwkv_operands(nc, A, S, sem)
        with semaphores(nc, ctx) as sem:
            rwkv_scan(nc, A, S, sem)
        with semaphores(nc, ctx) as sem:
            output_and_router(nc, A, S, sem)
        with semaphores(nc, ctx) as sem:
            w_in = [[sem(f"w{m}_in_{j}") for m in (1, 3, 2)] for j in range(2)]
            route(nc, A, S, sem, w_in)
            experts(nc, A, S, sem, w_in)
        with semaphores(nc, ctx) as sem:
            combine(nc, A, S, sem, out)


def hyena_consts(I):
    L=1024; D=256
    o={}
    f4=np.float32
    t=np.linspace(0.0,1.0,L,dtype=f4)[:,None]
    w=(f4(2.0*math.pi/L)*np.arange(L,dtype=f4))[:,None]
    f=np.linspace(1e-4,15,16,dtype=f4)[None,:]
    z=np.concatenate([t,np.cos(f*w),-np.sin(f*w)],-1).astype(f4)
    o['hy_pos']=np.ascontiguousarray(z.T)
    for k in ('w1','w2','w3','wout'): o['hy_'+k]=I['hy_'+k][0]
    o['hy_fb']=np.stack([I['hy_b1'][0],I['hy_b2'][0],I['hy_b3'][0],I['hy_freq'][0]],1)
    dl=np.abs(np.linspace(math.log(1e-2)/1.5,math.log(1e-2)/0.3,D,dtype=f4))
    o['hy_decay']=np.exp(-t*dl).astype(f4)
    cw=I['hy_conv_w'][0]; 
    cv=np.concatenate([cw,I['hy_conv_b']],0)
    o['hy_conv']=np.ascontiguousarray(cv.reshape(4,6,128).transpose(2,1,0))
    o['hy_skip']=np.ascontiguousarray(I['hy_skip'][0].reshape(2,128).T)
    n=np.arange(L,dtype=np.float64)
    a=np.pi*np.outer(n,2*n+1)/2048
    b=np.pi*np.outer(2*n+1,2*n+1)/4096
    def cols(m):
        return m.reshape(2,8,128,8,128).transpose(3,2,0,1,4)
    o['hy_cu']=np.ascontiguousarray(cols(np.stack([np.cos(a),np.sin(a)]))).astype(f4)
    o['hy_cs']=np.ascontiguousarray(cols(np.stack([np.cos(b),np.sin(b)]))).astype(f4)
    o['hy_rows']=np.ascontiguousarray(np.stack([np.cos(b),np.sin(b)]).reshape(2,8,128,L).transpose(1,2,0,3)).astype(f4)
    return o
def na_consts(I):
    o={}
    rpb=I['na_rpb'][0]
    pad=np.zeros((4,15,127),np.float32); pad[:,:,48:79]=rpb
    b=np.stack([pad[:,:,63-q:127-q] for q in range(64)],1)
    o['na_bias']=np.ascontiguousarray(b.reshape(2,128,15,64).transpose(1,0,2,3))
    q=np.arange(64); st=np.clip(q-8,0,48); c=np.arange(64)
    band=np.where((c[None]>=st[:,None])&(c[None]<st[:,None]+16),0,-1e30).astype(np.float32)
    o['na_band']=np.concatenate([band,band],0)
    return o
def rw_consts(I):
    o={}
    L=1024
    mu=I['rw_mu'][0]
    rows=[mu[0,0],mu[0,1],mu[1,0],mu[1,1],mu[2,0],mu[2,1],I['rw_w0'][0,0],I['rw_w0'][0,1],I['rw_a0'][0,0],I['rw_a0'][0,1],
          I['rw_kk'][0],I['rw_ka'][0],I['rw_rk'][0].reshape(-1),I['rw_ln_w'][0],I['rw_ln_b'][0]]
    o['rw_par']=np.ascontiguousarray(np.stack(rows).reshape(15,4,128).transpose(2,1,0))
    lo=np.stack([I['rw_w2'][0].reshape(128,4,128),I['rw_a2'][0].reshape(128,4,128),I['rw_g2'][0].reshape(128,4,128)])
    o['rw_lora']=np.ascontiguousarray(lo.transpose(2,1,0,3))
    r=np.ones((128,L),np.float32); r[:,::64]=0
    o['rw_reset']=r
    o['rw_heads']=np.kron(np.eye(2),np.ones((64,64))).astype(np.float32)
    s=np.arange(128)[:,None]; t=np.arange(128)[None]
    same=(s//64==t//64)
    m=np.stack([np.stack([same&(s<t),same&(s<=t),same&(s<t),same&(s<=t)]),np.stack([same&(s>t),same&(s>=t),same&(s>t),same&(s>=t)])])
    o['rw_mask']=np.ascontiguousarray(m.transpose(2,0,1,3)).astype(np.float32)
    lv=np.stack([(s//(2*b)==t//(2*b))&(s//b!=t//b) for b in (1,2,4,8,16,32)])
    o['rw_level']=np.ascontiguousarray(lv.transpose(1,0,2)).astype(np.float32)
    return o
def moe_consts(I):
    o={}
    o['w_out']=np.ascontiguousarray(I['w_out'][0].reshape(8,128,1024).transpose(1,0,2))
    wr=np.concatenate([I['moe_wg'][0],I['moe_we'][0]],1)
    o['w_router']=np.ascontiguousarray(wr.reshape(8,128,36).transpose(1,0,2))
    o['b_router']=np.concatenate([I['moe_bg'],I['moe_be']],1)
    o['norm2_g']=I['norm2_g']; o['norm_f_g']=I['norm_f_g'][None]
    s=np.arange(128)[:,None]; t=np.arange(128)[None]
    o['rt_tri']=np.ascontiguousarray(np.stack([s<t,s<1e9+0*t],1)).astype(np.float32)
    o['rt_down']=np.arange(8,0,-1).astype(np.float32)[None]
    o['rt_far']=np.arange(32).astype(np.float32)[None]
    o['moe_w1']=I['moe_w1'][0].reshape(32,128,8,512); o['moe_w3']=I['moe_w3'][0].reshape(32,128,8,512)
    o['moe_w2']=I['moe_w2'][0].reshape(32,128,4,1024)
    return o


def kernel(**inputs):
    import concourse.bacc as bacc
    from concourse.bass_utils import run_bass_kernel_spmd

    I = {name: np.asarray(a) for name, a in inputs.items()}
    arrays = {"x": I["x"][0], "norm1_g": I["norm1_g"], "ident": np.eye(P, dtype=np.float32),
              "w_in": np.ascontiguousarray(I["w_in"][0].reshape(KD, P, CT, P).transpose(2, 1, 0, 3))}
    for part in (hyena_consts(I), na_consts(I), rw_consts(I), moe_consts(I)):
        arrays.update(part)
    arrays = {f"in_{name}": np.ascontiguousarray(a) for name, a in arrays.items()}
    nc = bacc.Bacc("TRN2", target_bir_lowering=False, num_devices=1)
    A = {name[3:]: nc.dram_tensor(name, a.shape, mybir.dt.from_np(a.dtype), kind="ExternalInput").ap()
         for name, a in arrays.items()}
    out = nc.dram_tensor("out_rows", (L, D), F32, kind="ExternalOutput").ap()
    program(nc, A, out)
    r = run_bass_kernel_spmd(nc, [arrays], core_ids=[0])
    return r.results[0]["out_rows"].reshape(1, L, D)
```
